# Optimizing a Trainium2 kernel written in Bass

```python
import math
import jax, jax.numpy as jnp
from jax import lax
import numpy as np

D_MODEL = 1024
BATCH = 1
SEQ = 256
DEPTH = 1

SSD_INNER = D_MODEL
SSD_HEAD_DIM = 64
SSD_HEADS = SSD_INNER // SSD_HEAD_DIM
SSD_GROUPS = 4
SSD_STATE = 128
SSD_CHUNK = 128
SSD_CONV = 4
SSD_BC = SSD_GROUPS * SSD_STATE
SSD_CONV_CH = SSD_INNER + 2 * SSD_BC
DT_MIN = 0.001
DT_MAX = 0.1
ATT_HEAD_DIM = 64
ATT_HEADS = D_MODEL // 128
ATT_INNER = ATT_HEADS * ATT_HEAD_DIM
Q_BLOCK = 128
N_GROUPS = 4
EXPERTS_PER_GROUP = 4
N_EXPERTS = N_GROUPS * EXPERTS_PER_GROUP
TOP_K = 2
EXPERT_FF = D_MODEL // 2
IN_SIZES = (SSD_INNER, SSD_CONV_CH, SSD_HEADS, ATT_INNER, ATT_INNER, ATT_INNER, ATT_HEADS, D_MODEL, D_MODEL)
N_IN = sum(IN_SIZES)
N_MOD = 6
DEEPNORM_ALPHA = (2 * DEPTH) ** 0.25
DEEPNORM_BETA = (8 * DEPTH) ** -0.25
LN_EPS = 1e-5


def layer_norm(x, gain=None, bias=None):
    xf = x.astype(jnp.float32)
    mu = jnp.mean(xf, axis=-1, keepdims=True)
    var = jnp.mean(jnp.square(xf - mu), axis=-1, keepdims=True)
    y = ((xf - mu) * lax.rsqrt(var + LN_EPS)).astype(x.dtype)
    if gain is None:
        return y
    return y * gain + bias

def gated_rms_norm(y, z, w):
    g = (y * jax.nn.silu(z)).astype(jnp.float32)
    g = g * lax.rsqrt(jnp.mean(jnp.square(g), axis=-1, keepdims=True) + LN_EPS)
    return g.astype(y.dtype) * w

def causal_depthwise_conv(u, w, bias):
    k_width, ch = w.shape
    out = lax.conv_general_dilated(
        u, w[:, None, :].astype(u.dtype), window_strides=(1,),
        padding=((k_width - 1, 0),), dimension_numbers=('NWC', 'WIO', 'NWC'),
        feature_group_count=ch)
    return out + bias

def ssd_chunked(xh, dt, a_log, bmat, cmat):
    b, s, h, p = xh.shape
    g, n = bmat.shape[-2:]
    r = h // g
    L = SSD_CHUNK
    nc = s // L
    f32 = jnp.float32
    A = -jnp.exp(a_log.astype(f32))
    a = (dt * A).reshape(b, nc, L, g, r)
    xdt = (xh.astype(f32) * dt[..., None]).reshape(b, nc, L, g, r, p)
    bc = bmat.astype(f32).reshape(b, nc, L, g, n)
    cc = cmat.astype(f32).reshape(b, nc, L, g, n)
    a_cs = jnp.cumsum(a, axis=2)
    causal = jnp.tril(jnp.ones((L, L), dtype=bool))[None, None, :, :, None, None]
    seg = a_cs[:, :, :, None] - a_cs[:, :, None, :]
    decay = jnp.exp(jnp.where(causal, seg, -jnp.inf))
    cb = jnp.einsum('bclgn,bcsgn->bclsg', cc, bc)
    y_diag = jnp.einsum('bclsgr,bcsgrp->bclgrp', cb[..., None] * decay, xdt)
    to_end = jnp.exp(a_cs[:, :, -1:] - a_cs)
    states = jnp.einsum('bclgn,bclgrp->bcgrpn', bc, xdt * to_end[..., None])
    chunk_decay = jnp.exp(a_cs[:, :, -1])

    def carry_state(state, inp):
        st, dec = inp
        return state * dec[..., None, None] + st, state

    _, prev = lax.scan(carry_state, jnp.zeros_like(states[:, 0]),
                       (jnp.moveaxis(states, 1, 0), jnp.moveaxis(chunk_decay, 1, 0)))
    prev = jnp.moveaxis(prev, 0, 1)
    y_off = jnp.einsum('bclgn,bcgrpn->bclgrp', cc, prev) * jnp.exp(a_cs)[..., None]
    return (y_diag + y_off).reshape(b, s, h, p)

def forgetting_attention(q, k, v, log_f):
    b, s, h, d = q.shape
    fcum = jnp.cumsum(log_f.astype(jnp.float32), axis=1).transpose(0, 2, 1)
    scale = d ** -0.5
    q_pos = jnp.arange(Q_BLOCK)
    outs = []
    for i in range(s // Q_BLOCK):
        lo, hi = i * Q_BLOCK, (i + 1) * Q_BLOCK
        logits = jnp.einsum('bqhd,bkhd->bhqk', q[:, lo:hi], k[:, :hi]).astype(jnp.float32) * scale
        logits = logits + fcum[:, :, lo:hi, None] - fcum[:, :, None, :hi]
        causal = jnp.arange(hi)[None, :] <= (lo + q_pos)[:, None]
        logits = jnp.where(causal, logits, -jnp.inf)
        probs = jax.nn.softmax(logits, axis=-1).astype(v.dtype)
        outs.append(jnp.einsum('bhqk,bkhd->bqhd', probs, v[:, :hi]))
    return jnp.concatenate(outs, axis=1)

def hybrid_mixer(h, w_in, conv_w, conv_b, dt_bias, a_log, d_skip, ssd_norm_w, forget_b,
                 w_ssd_o, w_att_o, w_o):
    b, s, _ = h.shape
    split_points = np.cumsum(IN_SIZES)[:-1].tolist()
    proj = h @ w_in
    z, xbc, dt_raw, q, k, v, f_raw, g_ssd, g_att = jnp.split(proj, split_points, axis=-1)
    xbc = jax.nn.silu(causal_depthwise_conv(xbc, conv_w, conv_b))
    xs, bm, cm = jnp.split(xbc, [SSD_INNER, SSD_INNER + SSD_BC], axis=-1)
    dt = jax.nn.softplus((dt_raw + dt_bias).astype(jnp.float32))
    xh = xs.reshape(b, s, SSD_HEADS, SSD_HEAD_DIM)
    y = ssd_chunked(xh, dt, a_log,
                    bm.reshape(b, s, SSD_GROUPS, SSD_STATE),
                    cm.reshape(b, s, SSD_GROUPS, SSD_STATE))
    y = (y + d_skip[:, None] * xh).astype(h.dtype).reshape(b, s, SSD_INNER)
    y_ssd = gated_rms_norm(y, z, ssd_norm_w) @ w_ssd_o
    log_f = jax.nn.log_sigmoid((f_raw + forget_b).astype(jnp.float32))
    o = forgetting_attention(q.reshape(b, s, ATT_HEADS, ATT_HEAD_DIM),
                             k.reshape(b, s, ATT_HEADS, ATT_HEAD_DIM),
                             v.reshape(b, s, ATT_HEADS, ATT_HEAD_DIM), log_f)
    y_att = o.reshape(b, s, ATT_INNER) @ w_att_o
    merged = jax.nn.sigmoid(g_ssd) * y_ssd + jax.nn.sigmoid(g_att) * y_att
    return merged @ w_o

def hierarchical_moe(h, w_rg, b_rg, w_re, b_re, w_gate, w_up, w_down):
    b, s, d = h.shape
    t = h.reshape(-1, d)
    f32 = jnp.float32
    g_prob = jax.nn.softmax((t @ w_rg + b_rg).astype(f32), axis=-1)
    g_p, g_idx = lax.top_k(g_prob, 1)
    onehot_g = jax.nn.one_hot(g_idx[:, 0], N_GROUPS, dtype=f32)
    e_logits = (t @ w_re + b_re).astype(f32).reshape(-1, N_GROUPS, EXPERTS_PER_GROUP)
    e_in = jnp.einsum('tg,tge->te', onehot_g, e_logits)
    top_l, top_i = lax.top_k(e_in, TOP_K)
    w_k = jax.nn.softmax(top_l, axis=-1) * g_p
    w_group = jnp.einsum('tk,tke->te', w_k, jax.nn.one_hot(top_i, EXPERTS_PER_GROUP, dtype=f32))
    gates = (onehot_g[:, :, None] * w_group[:, None, :]).reshape(-1, N_EXPERTS).astype(t.dtype)
    out = jnp.zeros_like(t)
    for e in range(N_EXPERTS):
        hid = jax.nn.silu(t @ w_gate[e]) * (t @ w_up[e])
        out = out + gates[:, e:e + 1] * (hid @ w_down[e])
    return out.reshape(b, s, d)

def first_inputs(seed: int = 0) -> dict:
    key = jax.random.key(seed)
    ks = iter(jax.random.split(key, 32))
    f32 = jnp.float32

    def nrm(shape, scale):
        return jax.random.normal(next(ks), shape, f32) * scale

    offs = np.concatenate([[0], np.cumsum(IN_SIZES)])
    col_scale = np.ones((N_IN,), np.float32)
    col_scale[offs[1]:offs[1] + SSD_INNER] = DEEPNORM_BETA
    col_scale[offs[5]:offs[6]] = DEEPNORM_BETA
    dt0 = jnp.exp(jax.random.uniform(next(ks), (DEPTH, SSD_HEADS), f32)
                  * (math.log(DT_MAX) - math.log(DT_MIN)) + math.log(DT_MIN))
    return {
        'x': nrm((BATCH, SEQ, D_MODEL), 1.0),
        'c': nrm((BATCH, D_MODEL), 1.0),
        'w_mod': nrm((DEPTH, D_MODEL, N_MOD * D_MODEL), 0.5 * D_MODEL ** -0.5),
        'b_mod': nrm((DEPTH, N_MOD * D_MODEL), 0.02),
        'w_in': nrm((DEPTH, D_MODEL, N_IN), D_MODEL ** -0.5) * jnp.asarray(col_scale),
        'conv_w': nrm((DEPTH, SSD_CONV, SSD_CONV_CH), SSD_CONV ** -0.5),
        'conv_b': nrm((DEPTH, SSD_CONV_CH), 0.02),
        'dt_bias': dt0 + jnp.log(-jnp.expm1(-dt0)),
        'a_log': jnp.log(jax.random.uniform(next(ks), (DEPTH, SSD_HEADS), f32, minval=1.0, maxval=16.0)),
        'd_skip': 1.0 + nrm((DEPTH, SSD_HEADS), 0.1),
        'ssd_norm_w': 1.0 + nrm((DEPTH, SSD_INNER), 0.05),
        'forget_b': jax.random.uniform(next(ks), (DEPTH, ATT_HEADS), f32, minval=1.0, maxval=4.0),
        'w_ssd_o': nrm((DEPTH, SSD_INNER, D_MODEL), DEEPNORM_BETA * SSD_INNER ** -0.5),
        'w_att_o': nrm((DEPTH, ATT_INNER, D_MODEL), DEEPNORM_BETA * ATT_INNER ** -0.5),
        'w_o': nrm((DEPTH, D_MODEL, D_MODEL), DEEPNORM_BETA * D_MODEL ** -0.5),
        'ln1_g': 1.0 + nrm((DEPTH, D_MODEL), 0.05),
        'ln1_b': nrm((DEPTH, D_MODEL), 0.02),
        'w_router_group': nrm((DEPTH, D_MODEL, N_GROUPS), D_MODEL ** -0.5),
        'b_router_group': nrm((DEPTH, N_GROUPS), 0.01),
        'w_router_expert': nrm((DEPTH, D_MODEL, N_EXPERTS), D_MODEL ** -0.5),
        'b_router_expert': nrm((DEPTH, N_EXPERTS), 0.01),
        'w_gate': nrm((DEPTH, N_EXPERTS, D_MODEL, EXPERT_FF), D_MODEL ** -0.5),
        'w_up': nrm((DEPTH, N_EXPERTS, D_MODEL, EXPERT_FF), DEEPNORM_BETA * D_MODEL ** -0.5),
        'w_down': nrm((DEPTH, N_EXPERTS, EXPERT_FF, D_MODEL), DEEPNORM_BETA * EXPERT_FF ** -0.5),
        'ln2_g': 1.0 + nrm((DEPTH, D_MODEL), 0.05),
        'ln2_b': nrm((DEPTH, D_MODEL), 0.02),
    }

def first_block(x, c, w_mod, b_mod, w_in, conv_w, conv_b, dt_bias, a_log, d_skip, ssd_norm_w,
              forget_b, w_ssd_o, w_att_o, w_o, ln1_g, ln1_b, w_router_group, b_router_group,
              w_router_expert, b_router_expert, w_gate, w_up, w_down, ln2_g, ln2_b):
    c_act = jax.nn.silu(c)
    for l in range(DEPTH):
        mod = (c_act @ w_mod[l] + b_mod[l])[:, None, :]
        sh1, sc1, gt1, sh2, sc2, gt2 = jnp.split(mod, N_MOD, axis=-1)
        h = layer_norm(x) * (1.0 + sc1) + sh1
        y = hybrid_mixer(h, w_in[l], conv_w[l], conv_b[l], dt_bias[l], a_log[l], d_skip[l],
                         ssd_norm_w[l], forget_b[l], w_ssd_o[l], w_att_o[l], w_o[l])
        x = layer_norm(DEEPNORM_ALPHA * x + (1.0 + gt1) * y, ln1_g[l], ln1_b[l])
        h = layer_norm(x) * (1.0 + sc2) + sh2
        y = hierarchical_moe(h, w_router_group[l], b_router_group[l], w_router_expert[l],
                             b_router_expert[l], w_gate[l], w_up[l], w_down[l])
        x = layer_norm(DEEPNORM_ALPHA * x + (1.0 + gt2) * y, ln2_g[l], ln2_b[l])
    return x


MLA_HEADS = 8
MLA_Q_RANK = 384
MLA_KV_RANK = 256
MLA_NOPE_DIM = 128
MLA_ROPE_DIM = 64
MLA_V_DIM = D_MODEL // MLA_HEADS
ROPE_THETA = 10000.0
DIL_GROUPS = ((128, 1), (512, 4), (2048, 16))
DIL_HEADS = 8
DIL_HEAD_DIM = D_MODEL // DIL_HEADS
N_DIL_HEADS = len(DIL_GROUPS) * DIL_HEADS
REL_BUCKETS = 32
REL_MAX_DIST = 1024
N_EXPERTS_2 = 16
EC_CAPACITY_FACTOR = 2
D_FF_EXPERT = 2 * D_MODEL
N_BRANCHES = 2
NORM_EPS = 1e-6
NEG_INF = -1e30
COLS_DIL = len(DIL_GROUPS) * 3 * DIL_HEADS * DIL_HEAD_DIM
SPLIT_SIZES = (MLA_Q_RANK, MLA_KV_RANK, MLA_ROPE_DIM, COLS_DIL, N_BRANCHES * D_MODEL)
D_IN = sum(SPLIT_SIZES)


def rmsnorm(t, g):
    tf = t.astype(jnp.float32)
    y = tf * lax.rsqrt(jnp.mean(tf * tf, axis=-1, keepdims=True) + NORM_EPS)
    return (y * g.astype(jnp.float32)).astype(t.dtype)

def rope(t, cos, sin):
    t1, t2 = jnp.split(t, 2, axis=-1)
    return jnp.concatenate([t1 * cos - t2 * sin, t1 * sin + t2 * cos], axis=-1).astype(t.dtype)

def t5_bucket(rel):
    nb = REL_BUCKETS // 2
    ret = jnp.where(rel > 0, nb, 0)
    n = jnp.abs(rel)
    max_exact = nb // 2
    nf = jnp.maximum(n, 1).astype(jnp.float32)
    large = max_exact + (jnp.log(nf / max_exact) / math.log(REL_MAX_DIST / max_exact)
                         * (nb - max_exact)).astype(jnp.int32)
    large = jnp.minimum(large, nb - 1)
    return ret + jnp.where(n < max_exact, n, large)

def mla_attention(c_q, c_kv, k_pe, g_q_lat, g_kv_lat, w_uq, w_ukv, cos, sin):
    B, S, _ = c_q.shape
    q = (rmsnorm(c_q, g_q_lat) @ w_uq).reshape(B, S, MLA_HEADS, MLA_NOPE_DIM + MLA_ROPE_DIM)
    q_nope = q[..., :MLA_NOPE_DIM]
    q_pe = rope(q[..., MLA_NOPE_DIM:], cos[:, :, None], sin[:, :, None])
    kv = (rmsnorm(c_kv, g_kv_lat) @ w_ukv).reshape(B, S, MLA_HEADS, MLA_NOPE_DIM + MLA_V_DIM)
    k_nope, v = kv[..., :MLA_NOPE_DIM], kv[..., MLA_NOPE_DIM:]
    k_pe = rope(k_pe, cos, sin)
    scale = (MLA_NOPE_DIM + MLA_ROPE_DIM) ** -0.5
    nqb = S // Q_BLOCK

    def to_blocks(t):
        return jnp.moveaxis(t.reshape((B, nqb, Q_BLOCK) + t.shape[2:]), 1, 0)

    def attend(blk):
        qn, qp = blk
        s = (jnp.einsum('bqhc,bkhc->bhqk', qn, k_nope)
             + jnp.einsum('bqhr,bkr->bhqk', qp, k_pe))
        p = jax.nn.softmax(s.astype(jnp.float32) * scale, axis=-1).astype(v.dtype)
        return jnp.einsum('bhqk,bkhc->bqhc', p, v)

    o = lax.map(attend, (to_blocks(q_nope), to_blocks(q_pe)))
    return jnp.moveaxis(o, 0, 1).reshape(B, S, MLA_HEADS * MLA_V_DIM)

def dilated_band_attention(q, k, v, pos, bias_table, window, dilation):
    B, S, H, Dh = q.shape
    d = dilation
    r = window // (2 * d)
    L = S // d
    nb = -(-L // r)
    Lp = nb * r

    def to_classes(t):
        t = jnp.moveaxis(t.reshape((B, L, d) + t.shape[2:]), 2, 1)
        return jnp.pad(t, [(0, 0), (0, 0), (0, Lp - L)] + [(0, 0)] * (t.ndim - 3))

    def band(t):
        t = jnp.pad(t, [(0, 0), (0, 0), (r, r)] + [(0, 0)] * (t.ndim - 3))
        t = t.reshape((B, d, nb + 2, r) + t.shape[3:])
        return jnp.concatenate([t[:, :, :-2], t[:, :, 1:-1], t[:, :, 2:]], axis=3)

    qc, kc, vc, pc = to_classes(q), to_classes(k), to_classes(v), to_classes(pos)
    kb, vb, pkb = band(kc), band(vc), band(pc)
    qb = qc.reshape(B, d, nb, r, H, Dh)
    pqb = pc.reshape(B, d, nb, r)
    s = jnp.einsum('bgnqhc,bgnkhc->bgnhqk', qb, kb).astype(jnp.float32) * (Dh ** -0.5)
    rel = pkb[:, :, :, None, :] - pqb[..., None]
    bias = bias_table[t5_bucket(rel)]
    s = s + jnp.moveaxis(bias, -1, 3).astype(jnp.float32)
    qi = jnp.arange(nb)[:, None, None] * r + jnp.arange(r)[None, :, None]
    kj = (jnp.arange(nb)[:, None, None] - 1) * r + jnp.arange(3 * r)[None, None, :]
    valid = (jnp.abs(kj - qi) <= r) & (kj >= 0) & (kj < L)
    s = jnp.where(valid[:, None], s, NEG_INF)
    m = jnp.max(s, axis=-1, keepdims=True)
    p = jnp.exp(s - m)
    den = jnp.sum(p, axis=-1, keepdims=True)
    o = jnp.einsum('bgnhqk,bgnkhc->bgnqhc', (p / den).astype(v.dtype), vb)
    lse = (m + jnp.log(den))[..., 0]
    o = o.reshape(B, d, Lp, H, Dh)[:, :, :L]
    o = jnp.moveaxis(o, 1, 2).reshape(B, S, H, Dh)
    lse = jnp.moveaxis(lse, 3, 4).reshape(B, d, Lp, H)[:, :, :L]
    lse = jnp.moveaxis(lse, 1, 2).reshape(B, S, H)
    return o, lse

def expert_choice_ffn(h, w_router, w_gate, w_up, w_down):
    B, S, D = h.shape
    cap = EC_CAPACITY_FACTOR * S // N_EXPERTS_2
    aff = jax.nn.softmax((h @ w_router).astype(jnp.float32), axis=-1)
    gate, idx = lax.top_k(jnp.swapaxes(aff, 1, 2), cap)
    bidx = jnp.arange(B)[:, None, None]
    xe = h[bidx, idx]
    hid = (jax.nn.silu(jnp.einsum('becd,edf->becf', xe, w_gate))
           * jnp.einsum('becd,edf->becf', xe, w_up))
    ye = jnp.einsum('becf,efd->becd', hid, w_down) * gate[..., None].astype(h.dtype)
    return jnp.zeros_like(h).at[bidx, idx].add(ye)

def second_inputs(seed: int = 0) -> dict:
    key = jax.random.key(seed)
    ks = jax.random.split(key, 20)
    f32 = jnp.float32

    def nrm(k, shape, s):
        return jax.random.normal(k, shape, f32) * s

    def gain(k, shape):
        return 1.0 + 0.02 * jax.random.normal(k, shape, f32)

    x = nrm(ks[0], (BATCH, SEQ, D_MODEL), 1.0)
    c = nrm(ks[1], (BATCH, D_MODEL), 1.0)
    offs = jax.random.randint(ks[2], (BATCH, 1), 0, 4096, dtype=jnp.int32)
    positions = offs + jnp.arange(SEQ, dtype=jnp.int32)[None, :]
    w_ada = nrm(ks[3], (DEPTH, D_MODEL, 6 * D_MODEL), 0.02)
    b_ada = nrm(ks[4], (DEPTH, 6 * D_MODEL), 0.02)
    g_norm_mix = gain(ks[5], (DEPTH, D_MODEL))
    w_in = nrm(ks[6], (DEPTH, D_MODEL, D_IN), D_MODEL ** -0.5)
    g_q_lat = gain(ks[7], (DEPTH, MLA_Q_RANK))
    g_kv_lat = gain(ks[8], (DEPTH, MLA_KV_RANK))
    w_uq = nrm(ks[9], (DEPTH, MLA_Q_RANK, MLA_HEADS * (MLA_NOPE_DIM + MLA_ROPE_DIM)), MLA_Q_RANK ** -0.5)
    w_ukv = nrm(ks[10], (DEPTH, MLA_KV_RANK, MLA_HEADS * (MLA_NOPE_DIM + MLA_V_DIM)), MLA_KV_RANK ** -0.5)
    rel_bias = nrm(ks[11], (REL_BUCKETS, N_DIL_HEADS), 0.5)
    w_out = nrm(ks[12], (DEPTH, D_MODEL, D_MODEL), D_MODEL ** -0.5)
    g_norm_ffn = gain(ks[13], (DEPTH, D_MODEL))
    w_router = nrm(ks[14], (DEPTH, D_MODEL, N_EXPERTS_2), D_MODEL ** -0.5)
    w_gate = nrm(ks[15], (DEPTH, N_EXPERTS_2, D_MODEL, D_FF_EXPERT), D_MODEL ** -0.5)
    w_up = nrm(ks[16], (DEPTH, N_EXPERTS_2, D_MODEL, D_FF_EXPERT), D_MODEL ** -0.5)
    w_down = nrm(ks[17], (DEPTH, N_EXPERTS_2, D_FF_EXPERT, D_MODEL), D_FF_EXPERT ** -0.5)
    g_final = gain(ks[18], (D_MODEL,))
    return {'x': x, 'c': c, 'positions': positions, 'w_ada': w_ada, 'b_ada': b_ada,
            'g_norm_mix': g_norm_mix, 'w_in': w_in, 'g_q_lat': g_q_lat, 'g_kv_lat': g_kv_lat,
            'w_uq': w_uq, 'w_ukv': w_ukv, 'rel_bias': rel_bias, 'w_out': w_out,
            'g_norm_ffn': g_norm_ffn, 'w_router': w_router, 'w_gate': w_gate, 'w_up': w_up,
            'w_down': w_down, 'g_final': g_final}

def second_block(x, c, positions, w_ada, b_ada, g_norm_mix, w_in, g_q_lat, g_kv_lat, w_uq, w_ukv,
              rel_bias, w_out, g_norm_ffn, w_router, w_gate, w_up, w_down, g_final):
    B, S, D = x.shape
    inv_freq = ROPE_THETA ** (-jnp.arange(0, MLA_ROPE_DIM, 2, dtype=jnp.float32) / MLA_ROPE_DIM)
    ang = positions.astype(jnp.float32)[..., None] * inv_freq
    cos, sin = jnp.cos(ang), jnp.sin(ang)
    cond = jax.nn.silu(c)
    split_at = [int(v) for v in np.cumsum(SPLIT_SIZES)[:-1]]
    for l in range(DEPTH):
        mod = (cond @ w_ada[l] + b_ada[l])[:, None, :]
        sh1, sc1, gt1, sh2, sc2, gt2 = jnp.split(mod, 6, axis=-1)
        h = rmsnorm(x, g_norm_mix[l]) * (1.0 + sc1) + sh1
        c_q, c_kv, k_pe, dil, gates = jnp.split(h @ w_in[l], split_at, axis=-1)
        o_a = mla_attention(c_q, c_kv, k_pe, g_q_lat[l], g_kv_lat[l], w_uq[l], w_ukv[l], cos, sin)
        dil = dil.reshape(B, S, len(DIL_GROUPS), 3, DIL_HEADS, DIL_HEAD_DIM)
        outs, lses = [], []
        for gi, (win, dd) in enumerate(DIL_GROUPS):
            o_g, lse_g = dilated_band_attention(
                dil[:, :, gi, 0], dil[:, :, gi, 1], dil[:, :, gi, 2], positions,
                rel_bias[:, gi * DIL_HEADS:(gi + 1) * DIL_HEADS], win, dd)
            outs.append(o_g)
            lses.append(lse_g)
        wts = jax.nn.softmax(jnp.stack(lses), axis=0)
        o_b = jnp.einsum('gbsh,gbshc->bshc', wts.astype(x.dtype), jnp.stack(outs)).reshape(B, S, D)
        g_a, g_b = jnp.split(jax.nn.sigmoid(gates), 2, axis=-1)
        x = x + gt1 * ((g_a * o_a + g_b * o_b) @ w_out[l])
        h2 = rmsnorm(x, g_norm_ffn[l]) * (1.0 + sc2) + sh2
        x = x + gt2 * expert_choice_ffn(h2, w_router[l], w_gate[l], w_up[l], w_down[l])
    return rmsnorm(x, g_final)


def setup_inputs(seed=0):
    out = dict(first_inputs(seed))
    for name, value in second_inputs(seed + 1).items():
        if name != "x":
            out[name + "_2"] = value
    return out


def reference(
    x, c, w_mod, b_mod, w_in, conv_w, conv_b, dt_bias, a_log, d_skip, ssd_norm_w, forget_b,
    w_ssd_o, w_att_o, w_o, ln1_g, ln1_b, w_router_group, b_router_group, w_router_expert,
    b_router_expert, w_gate, w_up, w_down, ln2_g, ln2_b, c_2, positions_2, w_ada_2, b_ada_2,
    g_norm_mix_2, w_in_2, g_q_lat_2, g_kv_lat_2, w_uq_2, w_ukv_2, rel_bias_2, w_out_2,
    g_norm_ffn_2, w_router_2, w_gate_2, w_up_2, w_down_2, g_final_2,
):
    x = first_block(
        x, c, w_mod, b_mod, w_in, conv_w, conv_b, dt_bias, a_log, d_skip, ssd_norm_w, forget_b,
        w_ssd_o, w_att_o, w_o, ln1_g, ln1_b, w_router_group, b_router_group, w_router_expert,
        b_router_expert, w_gate, w_up, w_down, ln2_g, ln2_b,
    )
    return second_block(
        x, c_2, positions_2, w_ada_2, b_ada_2, g_norm_mix_2, w_in_2, g_q_lat_2, g_kv_lat_2,
        w_uq_2, w_ukv_2, rel_bias_2, w_out_2, g_norm_ffn_2, w_router_2, w_gate_2, w_up_2,
        w_down_2, g_final_2,
    )


_drawn_inputs = setup_inputs


def setup_inputs(seed=0):
    import zlib

    import numpy as np

    out = dict(_drawn_inputs(seed))
    spreads = {}
    factors = {'b_mod': 4.32,
     'conv_b': 6.065,
     'd_skip': 4.253,
     'ssd_norm_w': 5.117,
     'b_router_group': 6.068,
     'b_router_expert': 8.0,
     'b_ada_2': 4.324,
     'g_norm_mix_2': 8.0,
     'g_q_lat_2': 8.0,
     'g_kv_lat_2': 8.0,
     'rel_bias_2': 2.836,
     'g_norm_ffn_2': 7.043,
     'g_final_2': 2.773}
    for name, (base, spread) in spreads.items():
        noise = np.random.default_rng([zlib.crc32(name.encode()), seed]).standard_normal(out[name].shape)
        drawn = base * np.exp(spread * noise) if base else spread * noise
        out[name] = __import__('jax').numpy.asarray(drawn.astype(out[name].dtype))
    for name, factor in factors.items():
        out[name] = (out[name] * factor).astype(out[name].dtype)
    return out
```

```python
def build_program(nc, A, out):
    from contextlib import ExitStack

    from concourse import bass, mybir

    F32 = mybir.dt.float32
    I32 = mybir.dt.int32
    ALU = mybir.AluOpType
    ACT = mybir.ActivationFunctionType
    AX = mybir.AxisListType.X

    P = 128
    S, D = A["x"].shape[1:]
    TT = S // P
    KC = D // P
    BANKS = 8
    BANK = 512
    SLOTS = 8
    SLOT = 2048
    HEADS, HD, GROUPS, STATE = 16, 64, 4, 128
    PER_GROUP = HEADS // GROUPS
    FOX_HEADS, FOX_D = 8, 64
    DIL_GROUPS, DIL_HEADS, DIL_D = 3, 8, 128
    MLA_HEADS, NOPE, ROPE = 8, 128, 64
    Q_RANK, KV_RANK = 384, 256
    E = 16
    QUADS = E // 4
    BUCKETS = 32
    ALPHA = 2 ** 0.25
    NEG = -1e30
    PI = 3.1415925
    TWO_PI = 6.283185307179586
    TWO_PI_HI = 6.28125
    MAGIC = 12582912.0

    ctx = ExitStack()
    with ctx:
        def sb(name, shape, dt=F32):
            return ctx.enter_context(nc.sbuf_tensor(name, shape, dt))

        def sem(name):
            return ctx.enter_context(nc.semaphore(name))

        ring = sb("ring", [P, SLOTS, SLOT])
        psum = ctx.enter_context(nc.psum_tensor("psum", [P, BANKS, BANK], F32))
        x = sb("x_tok", [P, TT, D])
        h = sb("h_tok", [P, TT, D])
        hT = sb("hT", [P, KC, S])
        mod = sb("mod", [P, 3, D])
        params = sb("params", [P, 2, D])
        consts = sb("consts", [P, A["consts"].shape[1]])
        vecT = sb("vecT", [P, P])
        ssd_w = sb("ssd_w", [P, KC])
        cact = sb("cact", [P, 2, KC])
        cond = sb("cond", [P, KC, P])
        b_row = sb("b_row", [1, 2, BANK])
        small_w = sb("small_w", [P, KC, 24])
        small_b = sb("small_b", [1, 24])
        head_v = sb("head_v", [P, 2, HEADS])
        stats = sb("stats", [P, TT, 2, 6])
        mv = sb("mv", [P, TT, 2])
        rstd = sb("rstd", [P, TT, 2])
        junk = sb("junk", [P, D])
        rows = junk[:, D - P:D]
        row_max = sb("row_max", [P, 80])
        row_sum = sb("row_sum", [P, 80])
        row_inv = sb("row_inv", [P, 80])
        prob = sb("prob", [P, 4, S])
        probT = sb("probT", [P, 4, S])
        pos_i = sb("pos_i", [P, TT], I32)
        turn = sb("turn", [P, 4, TT, ROPE // 2])
        table = sb("table", [P, DIL_GROUPS * DIL_HEADS])
        affT, topped, rank_T = (probT[0:E, i, :] for i in range(3))
        best8 = sb("best8", [E, 8])
        WORK = 17968
        work = sb("work", [P, WORK])

        def view(at, *dims):
            n = 1
            for d in dims:
                n *= d
            assert at + n <= WORK, (at, dims)
            v = work[:, at:at + n]
            if len(dims) == 2:
                v = v.rearrange("p (a b) -> p a b", a=dims[0])
            elif len(dims) == 3:
                v = v.rearrange("p (a b c) -> p a b c", a=dims[0], b=dims[1])
            return v

        at = [0]

        def const(n):
            at[0] += n
            return consts[:, at[0] - n:at[0]]

        ident, tri, causal, seg_mask, ones = const(P), const(P), const(2 * P), const(P), const(P)
        iota1, desc, inv_freq, bucket_range, eps = const(64), const(E), const(ROPE // 2), const(2), const(2)
        ones_row = ones[0:1, :]
        eps5, eps6 = eps[:, 0:1], eps[:, 1:2]

        pe_done = sem("pe_done")
        evacuated = [sem(f"evacuated{b}") for b in range(BANKS)]
        weights_in = [sem(f"weights_in{s}") for s in range(SLOTS)]
        act_step, dve_step = sem("act_step"), sem("dve_step")

        named = {}

        def signal(name):
            if name not in named:
                named[name] = sem(name)
            return named[name]

        first_job, n_jobs = {}, [0]

        def jobs(name, n):
            first_job[name] = n_jobs[0]
            n_jobs[0] += n

        def job(name, i=0):
            return first_job[name] + i

        def bank(k):
            return psum[:, k % BANKS, :]

        def done(k):
            return pe_done, k + 1

        def emptied(k):
            return evacuated[k % BANKS], k // BANKS + 1

        class Turn:

            def __init__(self, eng, own):
                self.eng, self.own, self.n, self.last = eng, own, 0, None
                self.it, self.per = None, 0

            def value(self):
                return self.n if self.it is None else self.n + self.it * self.per

            def __call__(self, op, *args, signals=None, **kw):
                if self.last is not None:
                    self.eng.wait_ge(*self.last)
                ins = op(*args, **kw)
                if signals is None:
                    self.n += 1
                    ins.then_inc(self.own, 1)
                    self.last = self.own, self.value()
                else:
                    ins.then_inc(signals[0], 1)
                    self.last = signals
                return ins

            def begin_loop(self, it, per):
                self.it, self.per, self.start = it, per, self.n
                self.last = self.own, self.value()

            def end_loop(self, rounds):
                assert self.n - self.start == self.per, (self.n - self.start, self.per)
                self.n, self.it = self.start + rounds * self.per, None
                self.last = self.own, self.n

        class Rounds:

            def __init__(self, it, job0, per_jobs, load0=0, per_loads=0):
                assert per_jobs % BANKS == 0 and per_loads % SLOTS == 0
                self.it, self.job0, self.per_jobs, self.load0, self.per_loads = it, job0, per_jobs, load0, per_loads

            def bank(self, j):
                return bank(self.job0 + j)

            def done(self, j):
                return pe_done, self.it * self.per_jobs + (self.job0 + j + 1)

            def emptied(self, j):
                k = self.job0 + j
                return evacuated[k % BANKS], self.it * (self.per_jobs // BANKS) + (k // BANKS + 1)

            def slot(self, i, dims):
                return slot(self.load0 + i, dims)

            def arrived(self, i):
                n = self.load0 + i
                return weights_in[n % SLOTS], self.it * (16 * self.per_loads // SLOTS) + 16 * (n // SLOTS + 1)

        loads = []

        def load(src, dims, reader):
            loads.append((src, dims, reader))
            return len(loads) - 1

        def slot(n, dims):
            a, b = dims
            return ring[:, n % SLOTS, 0:a * b].rearrange("p (a b) -> p a b", a=a)

        def arrived(n):
            return weights_in[n % SLOTS], 16 * (n // SLOTS + 1)

        chunk_loads = {}

        def load_chunk(name, w, cols, reader, kc=KC):
            width = cols.stop - cols.start
            src = w.rearrange("(p c) n -> p c n", c=kc)
            pieces = []
            for c0 in range(0, kc, 4):
                c1 = min(c0 + 4, kc)
                pieces.append((load(src[:, c0:c1, cols], (c1 - c0, width), reader), c0, c1, width))
            chunk_loads[name] = pieces

        def wide(a, b):
            return slice(a, a + b)

        Z0, XBC0 = 0, D
        DT0 = XBC0 + D + 2 * GROUPS * STATE
        Q0 = DT0 + HEADS
        K0, V0 = Q0 + FOX_HEADS * FOX_D, Q0 + 2 * FOX_HEADS * FOX_D
        F0 = V0 + FOX_HEADS * FOX_D
        GS0 = F0 + FOX_HEADS
        GA0 = GS0 + D
        w_in = A["w_in"][0]
        w_mod, w_ada = A["w_mod"][0], A["w_ada_2"][0]

        def plan_mod(name, w, units):
            for u in units:
                jobs(f"{name}{u}", 2)
                for n in range(2):
                    load_chunk(f"{name}{u}_{n}", w, wide(u * D + n * BANK, BANK), job(f"{name}{u}", n))

        def plan_chunks(name, w, col0, n, per_chunk):
            jobs(name, n * per_chunk)
            for i in range(n):
                load_chunk(f"{name}_{i}", w, wide(col0 + i * BANK, BANK), job(name, (i + 1) * per_chunk - 1))

        LAG_T, LAG_PV = 2, 3

        def plan_attention(name, n):
            for i in range(n + LAG_PV):
                if i < n:
                    jobs(f"{name}_qk{i}", 1)
                if 0 <= i - LAG_T < n:
                    jobs(f"{name}_t{i - LAG_T}", 1)
                if 0 <= i - LAG_PV < n:
                    jobs(f"{name}_pv{i - LAG_PV}", 1)

        BIAS_ROUNDS, BIAS_KEYS = 4, 8
        jobs("bias", BIAS_ROUNDS * BANKS)
        jobs("vecT", 1)
        plan_mod("mod", w_mod, (0, 1))
        jobs("hT", 4)
        plan_chunks("xbc", w_in, XBC0, 4, 2)
        jobs("dtf", 1)
        plan_chunks("q", w_in, Q0, 1, 2)
        plan_chunks("k", w_in, K0, 1, 2)
        plan_chunks("v", w_in, V0, 1, 2)
        plan_chunks("z", w_in, Z0, 2, 2)
        plan_chunks("gs", w_in, GS0, 2, 2)
        plan_chunks("ga", w_in, GA0, 2, 2)
        jobs("cumsum", 1)
        plan_mod("mod", w_mod, (2, 3, 4))
        jobs("xs_tok", 4)
        jobs("b_tok", 1)
        jobs("cb", TT)
        for k in range(3):
            jobs(f"a_row{k}", 1)
        jobs("state", 2)
        jobs("y_off", 2)
        for m in range(2 * TT):
            jobs(f"y_diag{m}", 1)
            for k in range(3 + 2 * m, min(5 + 2 * m, TT * GROUPS)):
                jobs(f"a_row{k}", 1)
        FOX_UNITS = FOX_HEADS * TT
        plan_attention("fox", FOX_UNITS)
        jobs("yT", 4)
        jobs("oT", 2)
        jobs("merge", 8)
        for n in range(2):
            load_chunk(f"ssd_o_{n}", A["w_ssd_o"][0], wide(n * BANK, BANK), job("merge", 4 * n + 2))
            load_chunk(f"att_o_{n}", A["w_att_o"][0], wide(n * BANK, BANK), job("merge", 4 * n + 3), kc=4)
        jobs("mT", 4)
        plan_chunks("w_o", A["w_o"][0], 0, 2, 2)
        plan_mod("mod", w_mod, (5,))
        jobs("h2T", 4)
        jobs("router", 1)
        plan_mod("ada", w_ada, (0, 1))
        jobs("rank", 1)

        CAP, PASSES, FF = 64, S // 64, A["w_gate"].shape[-1]
        MOE_ROUNDS, MOE_JOBS, MOE_LOADS = PASSES * QUADS, 24, 24
        MOE_XE, MOE_GW, MOE_GATE, MOE_UP, MOE_T, MOE_DOWN, MOE_SUM = 0, 4, (6, 8), (7, 9), (10, 13), (11, 14), (16, 20)
        jobs("moe", MOE_ROUNDS * MOE_JOBS)
        moe_load0 = len(loads)
        w_gate, w_up, w_down = A["w_gate"][0], A["w_up"][0], A["w_down"][0]
        moe_loads = []
        for p in range(2):
            for w, reader in ((w_gate, MOE_GATE[p]), (w_up, MOE_UP[p])):
                for c0 in (0, 4):
                    for i in range(2):
                        moe_loads.append((w.rearrange("e (p c) f -> e p c f", c=KC)[:, :, c0:c0 + 4, :], 2 * p + i, (4, FF), reader))
        for p in range(2):
            for c0 in (0, 2):
                for i in range(2):
                    moe_loads.append((w_down.rearrange("e (c p) n -> e p c n", p=P)[:, :, c0:c0 + 2, :], 2 * p + i, (2, D), MOE_DOWN[p] + 1))
        assert len(moe_loads) == MOE_LOADS
        loads.extend([None] * (MOE_ROUNDS * MOE_LOADS))

        w_in2 = A["w_in_2"][0]
        LAT = Q_RANK + KV_RANK + ROPE
        DIL0 = LAT
        GATE0 = DIL0 + DIL_GROUPS * 3 * DIL_HEADS * DIL_D
        jobs("h3T", 4)
        jobs("lat", 4)
        load_chunk("lat_0", w_in2, wide(0, BANK), job("lat", 1))
        load_chunk("lat_1", w_in2, wide(BANK, LAT - BANK), job("lat", 3))
        jobs("latT", 4)
        jobs("q_nope", 4)
        jobs("q_pe", 2)
        q_loads = [load(A["w_uq_2"][0].rearrange("(c p) n -> p c n", p=P)[:, :, wide(i * 384, 384)], (3, 384), job("q_pe", 1)) for i in range(4)]
        jobs("k_nope", 4)
        jobs("v_mla", 4)
        kv_loads = [load(A["w_ukv_2"][0].rearrange("(c p) n -> p c n", p=P)[:, :, wide(i * 1024, 1024)], (2, 1024), job("v_mla", 2 * i + 1)) for i in range(2)]
        jobs("q_peT", 2)
        MLA_UNITS = MLA_HEADS * TT
        plan_attention("mla", MLA_UNITS)
        DIL_UNITS = DIL_HEADS * TT
        for g in range(DIL_GROUPS):
            for i, nm in enumerate("qkv"):
                plan_chunks(f"dil_{nm}{g}", w_in2, DIL0 + (3 * g + i) * DIL_HEADS * DIL_D, 2, 2)
            plan_attention(f"dil{g}_", DIL_UNITS)
        plan_chunks("gates2", w_in2, GATE0, 4, 2)
        plan_mod("ada", w_ada, (2, 3, 4))
        jobs("mixT", 4)
        plan_chunks("w_out", A["w_out_2"][0], 0, 2, 2)
        plan_mod("ada", w_ada, (5,))
        jobs("h4T", 4)
        jobs("router2", 1)
        jobs("affT", 1)
        jobs("rank2", 1)

        CAP2, FF2 = 2 * S // E, A["w_gate_2"].shape[-1]
        assert CAP2 * 4 == P
        EC_ROUNDS, EC_JOBS, EC_LOADS = QUADS, 24, 96
        EC_XE, EC_GW, EC_GATE, EC_UP, EC_T, EC_DOWN, EC_SUM = 0, 4, (6, 12), (8, 14), (10, 16), 18, 20
        jobs("ec", EC_ROUNDS * EC_JOBS)
        ec_load0 = len(loads)
        w_gate2, w_up2, w_down2 = A["w_gate_2"][0], A["w_up_2"][0], A["w_down_2"][0]
        ec_loads, EC_PIECES = [], 0

        def plan_pieces(n, src_of, dims, last_job):
            nonlocal EC_PIECES
            for i in range(n):
                reader = last_job if i == n - 1 else ("piece", EC_PIECES)
                EC_PIECES += i < n - 1
                ec_loads.extend((src_of(i), e, dims, reader) for e in range(4))

        for fp in range(2):
            for w, last_job in ((w_gate2, EC_GATE[fp] + 1), (w_up2, EC_UP[fp] + 1)):
                rows_first = w.rearrange("e (p c) f -> e p c f", c=KC)[:, :, :, wide(fp * 1024, 1024)]
                plan_pieces(KC // 2, lambda i: rows_first[:, :, 2 * i:2 * i + 2, :], (2, 1024), last_job)
        chunks_first = w_down2.rearrange("e (c p) n -> e p c n", p=P)
        plan_pieces(FF2 // P // 2, lambda i: chunks_first[:, :, 2 * i:2 * i + 2, :], (2, D), EC_DOWN + 1)
        assert len(ec_loads) == EC_LOADS
        loads.extend([None] * (EC_ROUNDS * EC_LOADS))

        pieces_used = sem("pieces_used")

        block = ctx.enter_context(nc.Block())

        @block.sync
        def _(sp):
            def fetch_rounds(rounds, todo, job0, per_jobs, load0):
                per = len(todo)

                def place(i):
                    return (load0 + i) % SLOTS

                def fetch_expert(i, quad, used):
                    which, used = used
                    src, e, dims, _ = todo[i % per]
                    if not isinstance(quad, int):
                        used = sp.lower_val(sp.snap(used))
                    sp.dma_start(slot(place(i), dims), src[quad * 4 + e]).wait_op(which, used, "sem-ge").then_inc(weights_in[place(i)], 16)

                def used(i, it):
                    reader = todo[i - SLOTS][3]
                    if isinstance(reader, tuple):
                        return pieces_used, it * EC_PIECES + (reader[1] + 1)
                    return pe_done, it * per_jobs + (job0 + reader + 1)

                for i in range(SLOTS):
                    fetch_expert(i, 0, done(prior_reader(load0 + i - SLOTS)))
                with sp.Fori(0, rounds - 1) as it:
                    for i in range(SLOTS, per):
                        fetch_expert(i, quad_of(it), used(i, it))
                    for i in range(per, per + SLOTS):
                        fetch_expert(i, quad_of(it + 1), used(i, it))
                for i in range(SLOTS, per):
                    fetch_expert(i, (rounds - 1) % QUADS, used(i, rounds - 1))

            def quad_of(it):
                return it & (QUADS - 1)

            def prior_reader(n):
                if n < moe_load0:
                    return loads[n][2]
                if n < moe_load0 + MOE_ROUNDS * MOE_LOADS:
                    r, i = divmod(n - moe_load0, MOE_LOADS)
                    return job("moe") + r * MOE_JOBS + moe_loads[i][3]
                return loads[n][2]

            def fetch_run(first, end):
                for n in range(first, end):
                    src, dims, _ = loads[n]
                    if n >= SLOTS:
                        sp.wait_ge(*done(prior_reader(n - SLOTS)))
                    sp.dma_start(slot(n, dims), src).then_inc(weights_in[n % SLOTS], 16)

            fetch_run(0, moe_load0)
            fetch_rounds(MOE_ROUNDS, moe_loads, job("moe"), MOE_JOBS, moe_load0)
            fetch_run(moe_load0 + MOE_ROUNDS * MOE_LOADS, ec_load0)
            fetch_rounds(EC_ROUNDS, ec_loads, job("ec"), EC_JOBS, ec_load0)
            for t in range(TT):
                sp.wait_ge(signal("out_ready"), t + 1)
                sp.dma_start(out[0, wide(t * P, P), :], h[:, t, :]).then_inc(signal("out_stored"), 16)
            sp.wait_ge(signal("out_stored"), 16 * TT)

        bias = view(0, DIL_GROUPS * DIL_HEADS, TT * S)
        bands = view(12288, DIL_GROUPS, TT * S)
        rel, one_hot = view(13824, BIAS_KEYS, S), view(15872, BIAS_KEYS, S)
        pos_rows = junk[:, 512:512 + S + S // 4].bitcast(I32)
        pos_all, pos_quarter = junk[:, 0:S], junk[:, S:S + S // 4]
        bias_dram = nc.dram_tensor("bias_dram", [DIL_GROUPS * DIL_HEADS, P, TT * S], F32, kind="Internal").ap()
        bias_in = [sem(f"bias_in{i}") for i in range(4)]
        mla_unit0, dil_unit0 = FOX_UNITS, FOX_UNITS + MLA_UNITS

        lat = view(0, TT, LAT)
        c_qT, c_kvT = view(1408, 3, S), view(2176, 2, S)
        q_nopeT, k_nopeT = view(2688, MLA_HEADS, S), view(4736, MLA_HEADS, S)
        v_mla = view(6784, TT, MLA_HEADS * NOPE)
        q_pe = view(8832, TT, MLA_HEADS * ROPE)
        k_pe = view(9856, TT, 2 * ROPE)
        q_peT, k_peT = view(10112, MLA_HEADS // 2, S), view(11136, S)
        rope_tmp = view(11392, 2, MLA_HEADS * ROPE // 2)
        o_mla = h
        q_dilT, k_dilT = view(0, DIL_HEADS, S), view(2048, DIL_HEADS, S)
        v_dil = view(4096, TT, DIL_HEADS * DIL_D)
        o_dil = [view(6144 + 2048 * g, TT, D) for g in range(DIL_GROUPS)]
        bias_tile = view(12288, 4, TT * S)
        dil_w = view(14336, 3, TT * DIL_HEADS)
        sig_a, sig_b = view(0, TT, D), view(2048, TT, D)

        pick, pick_gate = view(0, TT, 4 * 64), view(512, TT, 4 * 64)
        gate_T = view(1024, 2, S)
        x_e = view(1536, KC, 4 * 64)
        silu_g, hid = view(3584, 2, BANK), view(4608, 2, BANK)
        hidT = view(5632, 16, P)
        y_e = view(7680, 2, D)
        y_sum = view(9728, TT, D)

        @block.gpsimd
        def _(pool):
            const_in = signal("const_in")
            pool.dma_start(cact[:, 0, :], A["c"][0].rearrange("(p c) -> p c", c=KC)).then_inc(signal("c_in"), 16)
            pool.dma_start(cact[:, 1, :], A["c_2"][0].rearrange("(p c) -> p c", c=KC)).then_inc(signal("c_in"), 16)
            pool.dma_start(pos_rows[:, 0:S], A["positions_2"].to_broadcast([P, S])).then_inc(signal("pos_in"), 16)
            for q in range(4):
                part = wide(q * BUCKETS, BUCKETS)
                pool.dma_start(pos_rows[part, S:S + S // 4], A["positions_2"][:, wide(q * S // 4, S // 4)].to_broadcast([BUCKETS, S // 4])).then_inc(signal("pos_in"), 16)
                pool.dma_start(table[part, :], A["rel_bias_2"]).then_inc(signal("table_in"), 16)
            with nc.allow_non_contiguous_dma(reason="256 numbers"):
                pool.dma_start(pos_i[:], A["positions_2"][0].rearrange("(t p) -> p t", p=P)).then_inc(signal("pos_in"), 16)
            pool.dma_start(bands[:], A["bands"].rearrange("p g t s -> p g (t s)")).then_inc(signal("bands_in"), 16)
            pool.dma_start(x[:], A["x"][0].rearrange("(t p) d -> p t d", p=P)).then_inc(signal("x_in"), 16)
            pool.dma_start(consts[:], A["consts"]).then_inc(const_in, 16)
            pool.dma_start(rows[0:64, :], A["conv_w"][0].rearrange("j (t p) -> (j t) p", p=P)).then_inc(signal("rows_in"), 16)
            pool.dma_start(rows[64:80, :], A["conv_b"][0].rearrange("(t p) -> t p", p=P)).then_inc(signal("rows_in"), 16)
            pool.dma_start(rows[80:83, :], A["g_q_lat_2"][0].rearrange("(t p) -> t p", p=P)).then_inc(signal("rows_in"), 16)
            pool.dma_start(rows[83:85, :], A["g_kv_lat_2"][0].rearrange("(t p) -> t p", p=P)).then_inc(signal("rows_in"), 16)
            with nc.allow_non_contiguous_dma(reason="24 columns"):
                pool.dma_start(small_w[:, :, 0:HEADS], w_in.rearrange("(p c) n -> p c n", c=KC)[:, :, wide(DT0, HEADS)]).then_inc(signal("dtf_in"), 16)
                pool.dma_start(small_w[:, :, HEADS:24], w_in.rearrange("(p c) n -> p c n", c=KC)[:, :, wide(F0, FOX_HEADS)]).then_inc(signal("dtf_in"), 16)
            pool.dma_start(small_b[:, 0:HEADS], A["dt_bias"]).then_inc(signal("dtf_in"), 16)
            pool.dma_start(small_b[:, HEADS:24], A["forget_b"]).then_inc(signal("dtf_in"), 16)
            pool.dma_start(head_v[:, 0, :], A["a_log"].to_broadcast([P, HEADS])).then_inc(signal("head_in"), 16)
            pool.dma_start(head_v[:, 1, :], A["d_skip"].to_broadcast([P, HEADS])).then_inc(signal("head_in"), 16)
            pool.dma_start(ssd_w[:], A["ssd_norm_w"][0].rearrange("(p c) -> p c", c=KC)).then_inc(signal("ssd_w_in"), 16)

            for g in range(DIL_GROUPS):
                heads = wide(g * DIL_HEADS, DIL_HEADS)
                pool.wait_ge(signal("bias_ready"), g + 1)
                pool.dma_start(bias_dram[heads].rearrange("h p s -> p h s"), bias[:, heads, :]).then_inc(signal("bias_stored"), 16)

            def bias_rows(b, unit, after, n):
                if after is not None:
                    pool.wait_ge(*done(after))
                pool.dma_start(b_row[:], b[:, wide(unit * D, D)].rearrange("o (n k) -> o n k", n=2)).then_inc(signal("b_row_in"), 16)

            bias_rows(A["b_mod"], 0, None, 0)
            bias_rows(A["b_mod"], 1, job("mod0", 1), 1)
            bias_rows(A["b_mod"], 2, job("mod1", 1), 2)
            bias_rows(A["b_mod"], 3, job("mod2", 1), 3)
            bias_rows(A["b_mod"], 4, job("mod3", 1), 4)
            pool.wait_ge(signal("y_ssd_ready"), 2)
            pool.dma_start(params[:, 0, :], A["ln1_g"].to_broadcast([P, D])).then_inc(signal("params_in"), 16)
            pool.dma_start(params[:, 1, :], A["ln1_b"].to_broadcast([P, D])).then_inc(signal("params_in"), 16)
            bias_rows(A["b_mod"], 5, job("mod4", 1), 5)
            with nc.allow_non_contiguous_dma(reason="20 columns"):
                pool.dma_start(small_w[:, :, 0:4], A["w_router_group"][0].rearrange("(p c) n -> p c n", c=KC)).then_inc(signal("router_in"), 16)
                pool.dma_start(small_w[:, :, 4:20], A["w_router_expert"][0].rearrange("(p c) n -> p c n", c=KC)).then_inc(signal("router_in"), 16)
            pool.dma_start(small_b[:, 0:4], A["b_router_group"]).then_inc(signal("router_in"), 16)
            pool.dma_start(small_b[:, 4:20], A["b_router_expert"]).then_inc(signal("router_in"), 16)

            def two_rows(ready, value, first, second):
                pool.wait_ge(signal(ready), value)
                for i, name in enumerate((first, second)):
                    row = A[name] if len(A[name].shape) == 2 else A[name].unsqueeze(0)
                    pool.dma_start(params[:, i, :], row.to_broadcast([P, D])).then_inc(signal("params_in"), 16)

            two_rows("x_mid_ready", 1, "ln2_g", "ln2_b")
            bias_rows(A["b_ada_2"], 0, job("mod5", 1), 6)
            bias_rows(A["b_ada_2"], 1, job("ada0", 1), 7)
            two_rows("x_b1_ready", 1, "g_norm_mix_2", "g_norm_ffn_2")
            bias_rows(A["b_ada_2"], 2, job("ada1", 1), 8)

            def bias_tiles(g):
                for hd in range(DIL_HEADS):
                    n = g * DIL_HEADS + hd
                    if n >= 4:
                        pool.wait_ge(signal("max_ready"), dil_unit0 + (n - 4) * TT + TT)
                    else:
                        pool.wait_ge(*emptied(job(f"mla_pv{MLA_UNITS - 1}")))
                    pool.dma_start(bias_tile[:, n % 4, :], bias_dram[n]).then_inc(bias_in[n % 4], 16)

            for g in range(DIL_GROUPS):
                bias_tiles(g)
            with nc.allow_non_contiguous_dma(reason="16 columns"):
                pool.dma_start(small_w[:, :, 0:E], A["w_router_2"][0].rearrange("(p c) n -> p c n", c=KC)).then_inc(signal("router2_in"), 16)
            bias_rows(A["b_ada_2"], 3, job("ada2", 1), 9)
            bias_rows(A["b_ada_2"], 4, job("ada3", 1), 10)
            bias_rows(A["b_ada_2"], 5, job("ada4", 1), 11)
            two_rows("h4_ready", TT, "g_final_2", "g_final_2")

        silu_z, sig_gs, sig_ga = view(0, TT, D), view(2048, TT, D), view(4096, TT, D)
        u_pad = view(6144, 16, S + 3)
        xcT = view(10288, 16, S)
        qT, kT, v_tok = view(14384, 4, S), view(15408, 4, S), view(16432, TT, 512)
        b_tok = view(17456, GROUPS, STATE)
        xs_tok, xdt = view(6144, TT, D), view(8192, TT, D)
        x_end, prev = view(10288, D), view(11312, D)
        o_fox = view(10288, TT, 512)
        cb = junk[:].rearrange("p (t g l) -> p t g l", t=TT, g=GROUPS)
        decay = [prob[:, 0:2, :].rearrange("p a b -> p (a b)"), prob[:, 2:4, :].rearrange("p a b -> p (a b)"),
                 probT[:, 0:2, :].rearrange("p a b -> p (a b)")]
        y_tok = h
        dtf = sb("dtf", [P, TT, 24])
        dtf_e = sb("dtf_e", [P, TT, 24])
        cum_in = sb("cum_in", [P, TT, 24])
        a_cs = sb("a_cs", [P, TT, HEADS])
        neg_F = sb("neg_F", [P, TT, FOX_HEADS])
        a_exp = sb("a_exp", [P, 2, HEADS])

        ATT_BUF = 4
        oT = view(14384, 4, S)
        silu_junk = junk
        mv2 = sb("mv2", [P, TT, 2])
        posf = sb("posf", [P, TT])
        dil_top = sb("dil_top", [P, DIL_UNITS])
        pass_shift = sb("pass_shift", [P, QUADS])
        chosen = sb("chosen", [P, TT, E])
        gates = sb("gates", [P, TT, E])
        rank = sb("rank", [P, TT, E])
        logits, in_group = sb("logits", [P, TT, 20]), sb("in_group", [P, TT, E])
        hot_g, hot1, hot2, e_in = sb("hot_g", [P, TT, 4]), sb("hot1", [P, TT, 4]), sb("hot2", [P, TT, 4]), sb("e_in", [P, TT, 4])
        route_g, route_2, route_top = sb("route_g", [P, TT, 4]), sb("route_2", [P, TT]), sb("route_top", [P, TT])
        top1, top2 = sb("top1", [P, TT]), sb("top2", [P, TT])

        @block.tensor
        def _(pe):
            next_job = [0]

            def begin(k):
                assert k == next_job[0], (k, next_job[0], [n for n, v in first_job.items() if v <= k][-1])
                next_job[0] += 1
                if k >= BANKS:
                    pe.wait_ge(*emptied(k - BANKS))
                return bank(k)

            def end(mm):
                mm.then_inc(pe_done, 1)

            def pieces(name):
                for n, c0, c1, width in chunk_loads[name]:
                    pe.wait_ge(*arrived(n))
                    for c in range(c0, c1):
                        yield c, slot(n, (c1 - c0, width))[:, c - c0, :]

            def chunks(name):
                return [(c, slot(n, (c1 - c0, width))[:, c - c0, :]) for n, c0, c1, width in chunk_loads[name] for c in range(c0, c1)]

            def modulation(name, unit, n_bias):
                pe.wait_ge(signal("b_row_in"), 16 * (n_bias + 1))
                for n in range(2):
                    o = begin(job(f"{name}{unit}", n))
                    pe.matmul(o, ones_row, b_row[0:1, n, :], start=True, stop=False)
                    for c, w in pieces(f"{name}{unit}_{n}"):
                        mm = pe.matmul(o, cond[:, c, :], w, start=False, stop=(c == KC - 1))
                    end(mm)

            def transpose_tokens(name, src):
                for t in range(TT):
                    for c0 in range(0, KC, 4):
                        o = begin(job(name, t * 2 + c0 // 4))
                        for c in range(c0, c0 + 4):
                            mm = pe.transpose(o[:, wide((c - c0) * P, P)], src[:, t, c::KC], ident)
                        end(mm)

            def channel_major(name, n, actT, kc=KC):
                for i in range(n):
                    for half in range(2):
                        o = begin(job(name, 2 * i + half))
                        for j in range(2):
                            ch = wide((2 * half + j) * P, P)
                            src = pieces(f"{name}_{i}") if half == j == 0 else chunks(f"{name}_{i}")
                            for c, w in src:
                                mm = pe.matmul(o[:, wide(j * S, S)], w[:, ch], actT[:, c, :], start=(c == 0), stop=(c == kc - 1))
                        end(mm)

            def token_major(name, n, actT, kc=KC):
                for i in range(n):
                    for t in range(TT):
                        o = begin(job(name, 2 * i + t))
                        for c, w in pieces(f"{name}_{i}") if t == 0 else chunks(f"{name}_{i}"):
                            mm = pe.matmul(o, actT[:, c, wide(t * P, P)], w, start=(c == 0), stop=(c == kc - 1))
                        end(mm)

            def attention(name, n, unit0, scores, values, keys):
                for i in range(n + LAG_PV):
                    if i < n:
                        o = begin(job(f"{name}_qk{i}"))
                        end(scores(o, i))
                    if 0 <= (j := i - LAG_T) < n:
                        o = begin(job(f"{name}_t{j}"))
                        pe.wait_ge(signal("probs_ready"), unit0 + j + 1)
                        for t in range(keys(j)):
                            mm = pe.transpose(o[:, wide(t * P, P)], prob[:, (unit0 + j) % ATT_BUF, wide(t * P, P)], ident)
                        end(mm)
                    if 0 <= (j := i - LAG_PV) < n:
                        o = begin(job(f"{name}_pv{j}"))
                        pe.wait_ge(*emptied(job(f"{name}_t{j}")))
                        end(values(o, j))

            pe.wait_ge(signal("table_in"), 64)
            with pe.Fori(0, BIAS_ROUNDS) as it:
                R = Rounds(it, job("bias"), BANKS)
                for j in range(BANKS):
                    if j % 4 == 0:
                        pe.wait_ge(signal("one_hot_ready"), it * 2 + (j // 4 + 1))
                    pe.wait_ge(evacuated[j], it)
                    part = wide(j % 4 * BUCKETS, BUCKETS)
                    for t in range(TT):
                        for s in range(BIAS_KEYS):
                            mm = pe.matmul(R.bank(j)[:, wide((t * BIAS_KEYS + s) * 24, 24)], one_hot[part, s, wide(t * P, P)], table[part, :], start=True, stop=True)
                    end(mm)
            next_job[0] += BIAS_ROUNDS * BANKS
            pe.wait_ge(signal("const_in"), 16)
            pe.wait_ge(signal("rows_in"), 64)
            o = begin(job("vecT"))
            end(pe.transpose(o[:, 0:85], rows[0:85, :], ident[0:85, 0:85]))

            pe.wait_ge(signal("cond_ready"), 1)
            modulation("mod", 0, 0)
            modulation("mod", 1, 1)

            pe.wait_ge(signal("h_ready"), TT)
            transpose_tokens("hT", h)

            for k in range(4):
                pe.wait_ge(*emptied(job("hT", k)))
            channel_major("xbc", 4, hT)
            pe.wait_ge(signal("dtf_in"), 64)
            o = begin(job("dtf"))
            for t in range(TT):
                pe.matmul(o[:, wide(t * 24, 24)], ones_row, small_b[0:1, :], start=True, stop=False)
                for c in range(KC):
                    mm = pe.matmul(o[:, wide(t * 24, 24)], hT[:, c, wide(t * P, P)], small_w[:, c, :], start=False, stop=(c == KC - 1))
            end(mm)
            channel_major("q", 1, hT)
            channel_major("k", 1, hT)
            token_major("v", 1, hT)
            token_major("z", 2, hT)
            token_major("gs", 2, hT)
            token_major("ga", 2, hT)

            pe.wait_ge(signal("cum_in_ready"), 1)
            o = begin(job("cumsum"))
            pe.matmul(o[:, 0:24], tri, cum_in[:, 0, :], start=True, stop=True)
            pe.matmul(o[:, 32:48], tri, cum_in[:, 1, 0:HEADS], start=True, stop=True)
            pe.matmul(o[:, 64:72], tri, cum_in[:, 1, HEADS:24], start=True, stop=False)
            pe.matmul(o[:, 64:72], ones, cum_in[:, 0, HEADS:24], start=False, stop=True)
            end(pe.matmul(o[:, 96:112], ones, cum_in[:, 0, 0:HEADS], start=True, stop=True))
            pe.wait_ge(signal("h_ready"), TT)
            modulation("mod", 2, 2)
            modulation("mod", 3, 3)
            modulation("mod", 4, 4)

            pe.wait_ge(signal("conv_ready"), 16)
            for t in range(TT):
                for c0 in range(0, KC, 4):
                    o = begin(job("xs_tok", 2 * t + c0 // 4))
                    for c in range(c0, c0 + 4):
                        mm = pe.transpose(o[:, wide((c - c0) * P, P)], xcT[:, c, wide(t * P, P)], ident)
                    end(mm)
            o = begin(job("b_tok"))
            for g in range(GROUPS):
                mm = pe.transpose(o[:, wide(g * P, P)], xcT[:, KC + g, 0:P], ident)
            end(mm)
            for t in range(TT):
                o = begin(job("cb", t))
                for g in range(GROUPS):
                    mm = pe.matmul(o[:, wide(g * P, P)], xcT[:, KC + g, wide(t * P, P)], xcT[:, KC + GROUPS + g, wide(t * P, P)], start=True, stop=True)
                end(mm)
            def a_row(k):
                t, g = divmod(k, GROUPS)
                o = begin(job(f"a_row{k}"))
                for r in range(PER_GROUP):
                    hd = g * PER_GROUP + r
                    mm = pe.matmul(o[:, wide(r * P, P)], cum_in[:, t, hd:hd + 1].to_broadcast([P, P]), tri, start=True, stop=True)
                end(mm)

            for k in range(3):
                a_row(k)
            pe.wait_ge(signal("x_end_ready"), 1)
            pe.wait_ge(*emptied(job("b_tok")))
            for half in range(2):
                o = begin(job("state", half))
                for g in (2 * half, 2 * half + 1):
                    mm = pe.matmul(o[:, wide((g % 2) * S, S)], b_tok[:, g, :], x_end[:, wide(g * S, S)], start=True, stop=True)
                end(mm)
            for half in range(2):
                o = begin(job("y_off", half))
                pe.wait_ge(*emptied(job("state", half)))
                for g in (2 * half, 2 * half + 1):
                    mm = pe.matmul(o[:, wide((g % 2) * S, S)], xcT[:, KC + GROUPS + g, P:S], prev[:, wide(g * S, S)], start=True, stop=True)
                end(mm)
            for m in range(2 * TT):
                t, half = divmod(m, 2)
                o = begin(job(f"y_diag{m}"))
                for k in (2 * m, 2 * m + 1):
                    pe.wait_ge(signal("decay_ready"), k + 1)
                    for r in range(PER_GROUP):
                        hd = (k % GROUPS) * PER_GROUP + r
                        mm = pe.matmul(o[:, wide((hd % 8) * HD, HD)], decay[k % 3][:, wide(r * P, P)], xdt[:, t, wide(hd * HD, HD)], start=True, stop=True)
                end(mm)
                for k in range(3 + 2 * m, min(5 + 2 * m, TT * GROUPS)):
                    a_row(k)

            def fox_scores(o, i):
                hd, t = divmod(i, TT)
                part, n = wide((hd % 2) * HD, HD), (t + 1) * P
                if i == 0:
                    for nm in ("q", "k"):
                        for j in range(2):
                            pe.wait_ge(*emptied(job(nm, j)))
                pe.matmul(o[:, 0:n], qT[part, hd // 2, wide(t * P, P)], kT[part, hd // 2, 0:n], start=True, stop=False)
                for s in range(t + 1):
                    lhs = cum_in[:, s, HEADS + hd:HEADS + hd + 1].to_broadcast([P, P])
                    mm = pe.matmul(o[:, s * P:(s + 1) * P], lhs, tri, start=False, stop=(s == t))
                    if s < t:
                        mm = pe.matmul(o[:, P:2 * P], lhs, ones, start=False, stop=False)
                return mm

            def fox_values(o, i):
                hd, t = divmod(i, TT)
                if i == 0:
                    for j in range(2):
                        pe.wait_ge(*emptied(job("v", j)))
                for s in range(t + 1):
                    mm = pe.matmul(o[:, 0:FOX_D], probT[:, i % ATT_BUF, wide(s * P, P)], v_tok[:, s, wide(hd * FOX_D, FOX_D)], start=(s == 0), stop=(s == t))
                return mm

            attention("fox", FOX_UNITS, 0, fox_scores, fox_values, lambda i: i % TT + 1)

            pe.wait_ge(signal("y_ssd_ready"), 2)
            transpose_tokens("yT", y_tok)
            for t in range(TT):
                o = begin(job("oT", t))
                for i in range(t, FOX_UNITS, TT):
                    pe.wait_ge(*emptied(job(f"fox_pv{i}")))
                for c in range(4):
                    mm = pe.transpose(o[:, wide(c * P, P)], o_fox[:, t, c::4], ident)
                end(mm)
            for k in range(4):
                pe.wait_ge(*emptied(job("yT", k)))
            for k in range(2):
                pe.wait_ge(*emptied(job("oT", k)))
            for n in range(2):
                for t in range(TT):
                    o = begin(job("merge", 4 * n + 2 * t))
                    for c, w in pieces(f"ssd_o_{n}"):
                        mm = pe.matmul(o, hT[:, c, wide(t * P, P)], w, start=(c == 0), stop=(c == KC - 1))
                    end(mm)
                    o = begin(job("merge", 4 * n + 2 * t + 1))
                    for c, w in pieces(f"att_o_{n}"):
                        mm = pe.matmul(o, oT[:, c, wide(t * P, P)], w, start=(c == 0), stop=(c == 3))
                    end(mm)
            pe.wait_ge(signal("merged_ready"), 4)
            transpose_tokens("mT", h)
            for k in range(4):
                pe.wait_ge(*emptied(job("mT", k)))
            token_major("w_o", 2, hT)
            pe.wait_ge(signal("x_mid_ready"), 1)
            modulation("mod", 5, 5)
            pe.wait_ge(signal("h2_ready"), TT)
            transpose_tokens("h2T", h)
            for k in range(4):
                pe.wait_ge(*emptied(job("h2T", k)))
            pe.wait_ge(signal("router_in"), 64)
            o = begin(job("router"))
            for t in range(TT):
                pe.matmul(o[:, wide(t * 20, 20)], ones_row, small_b[0:1, 0:20], start=True, stop=False)
                for c in range(KC):
                    mm = pe.matmul(o[:, wide(t * 20, 20)], hT[:, c, wide(t * P, P)], small_w[:, c, 0:20], start=False, stop=(c == KC - 1))
            end(mm)
            pe.wait_ge(signal("cond_ready"), 2)
            modulation("ada", 0, 6)
            modulation("ada", 1, 7)
            pe.wait_ge(signal("chosen_ready"), 1)
            o = begin(job("rank"))
            pe.matmul(o[:, 0:E], tri, chosen[:, 0, :], start=True, stop=True)
            pe.matmul(o[:, E:2 * E], tri, chosen[:, 1, :], start=True, stop=False)
            end(pe.matmul(o[:, E:2 * E], ones, chosen[:, 0, :], start=False, stop=True))

            def ffn_products(o, lhs, w, parts, width, start, stop):
                for (i, ws) in enumerate(w):
                    mm = pe.matmul(o[wide(parts[i] * width, width), :], lhs(i), ws, start=start, stop=stop)
                return mm

            def loop_begin(R, j):
                k = R.job0 + j
                pe.wait_ge(evacuated[k % BANKS], R.it * (R.per_jobs // BANKS) + k // BANKS)
                return R.bank(j)

            assert next_job[0] == job("moe")
            with pe.Fori(0, MOE_ROUNDS) as it:
                R = Rounds(it, job("moe"), MOE_JOBS, moe_load0, MOE_LOADS)
                pe.wait_ge(signal("pick_ready"), it + 1)
                for j in range(4):
                    o = loop_begin(R, MOE_XE + j)
                    for c in (2 * j, 2 * j + 1):
                        for t in range(TT):
                            mm = pe.matmul(o[:, wide((c % 2) * S, S)], h[:, t, c::KC], pick[:, t, :], start=(t == 0), stop=(t == TT - 1))
                    end(mm)
                for p in range(2):
                    o = loop_begin(R, MOE_GW + p)
                    for t in range(TT):
                        mm = pe.transpose(o[:, wide(t * P, P)], pick_gate[:, t, wide(p * P, P)], ident)
                    end(mm)
                for j in range(4):
                    pe.wait_ge(*R.emptied(MOE_XE + j))
                for p in range(2):
                    for what, j in ((0, MOE_GATE[p]), (1, MOE_UP[p])):
                        o = loop_begin(R, j)
                        for half in range(2):
                            n = 8 * p + 4 * what + 2 * half
                            for i in range(2):
                                pe.wait_ge(*R.arrived(n + i))
                            for c in range(4):
                                for i in range(2):
                                    mm = pe.matmul(o[wide(i * CAP, CAP), :], x_e[:, 4 * half + c, wide((2 * p + i) * CAP, CAP)],
                                                   R.slot(n + i, (4, FF))[:, c, :], start=(half == c == 0), stop=(half == 1 and c == 3))
                        end(mm)
                for p in range(2):
                    o = loop_begin(R, MOE_T[p])
                    pe.wait_ge(*R.emptied(MOE_UP[p]))
                    for c in range(4):
                        mm = pe.transpose(o[:, wide(c * P, P)], hid[:, p, wide(c * P, P)], ident)
                    end(mm)
                    out2 = [loop_begin(R, MOE_DOWN[p] + n) for n in range(2)]
                    pe.wait_ge(*R.emptied(MOE_T[p]))
                    for half in range(2):
                        l = 16 + 4 * p + 2 * half
                        for i in range(2):
                            pe.wait_ge(*R.arrived(l + i))
                        for c in range(2):
                            for n in range(2):
                                for i in range(2):
                                    mm = pe.matmul(out2[n][wide(i * CAP, CAP), :], hidT[:, 4 * p + 2 * half + c, wide(i * CAP, CAP)],
                                                   R.slot(l + i, (2, D))[:, c, wide(n * BANK, BANK)], start=(half == c == 0), stop=(half == c == 1))
                                if half == c == 1:
                                    end(mm)
                for p in range(2):
                    for n in range(2):
                        pe.wait_ge(*R.emptied(MOE_DOWN[p] + n))
                    for n in range(2):
                        for t in range(TT):
                            o = loop_begin(R, MOE_SUM[p] + 2 * n + t)
                            end(pe.matmul(o, gate_T[:, p, wide(t * P, P)], y_e[:, p, wide(n * BANK, BANK)], start=True, stop=True))
            next_job[0] += MOE_ROUNDS * MOE_JOBS

            pe.wait_ge(signal("h3_ready"), TT)
            transpose_tokens("h3T", h)
            for k in range(4):
                pe.wait_ge(*emptied(job("h3T", k)))
            for i in range(2):
                for t in range(TT):
                    o = begin(job("lat", 2 * i + t))
                    for c, w in pieces(f"lat_{i}") if t == 0 else chunks(f"lat_{i}"):
                        mm = pe.matmul(o[:, 0:w.shape[-1]], hT[:, c, wide(t * P, P)], w, start=(c == 0), stop=(c == KC - 1))
                    end(mm)
            pe.wait_ge(signal("lat_ready"), 1)
            for t in range(TT):
                o = begin(job("latT", 2 * t))
                for c in range(3):
                    mm = pe.transpose(o[:, wide(c * P, P)], lat[:, t, wide(c * P, P)], ident)
                end(mm)
                o = begin(job("latT", 2 * t + 1))
                for c in range(2):
                    mm = pe.transpose(o[:, wide(c * P, P)], lat[:, t, wide(Q_RANK + c * P, P)], ident)
                end(pe.transpose(o[:, 2 * P:3 * P], k_pe[:, t, :], ident))
            for k in range(4):
                pe.wait_ge(*emptied(job("latT", k)))
            for i, n in enumerate(q_loads):
                pe.wait_ge(*arrived(n))
                o = begin(job("q_nope", i))
                for j in range(2):
                    for c in range(3):
                        mm = pe.matmul(o[:, wide(j * S, S)], slot(n, (3, 384))[:, c, wide(j * (NOPE + ROPE), NOPE)], c_qT[:, c, :], start=(c == 0), stop=(c == 2))
                end(mm)
            for t in range(TT):
                o = begin(job("q_pe", t))
                for i, n in enumerate(q_loads):
                    for c in range(3):
                        w = slot(n, (3, 384))[:, c, :].rearrange("p (h d) -> p h d", h=2)[:, :, NOPE:NOPE + ROPE]
                        mm = pe.matmul(o[:, wide(i * P, P)], c_qT[:, c, wide(t * P, P)], w, start=(c == 0), stop=(c == 2))
                end(mm)
            for i, n in enumerate(kv_loads):
                pe.wait_ge(*arrived(n))
                for half in range(2):
                    o = begin(job("k_nope", 2 * i + half))
                    for j in range(2):
                        for c in range(2):
                            mm = pe.matmul(o[:, wide(j * S, S)], slot(n, (2, 1024))[:, c, wide((2 * half + j) * 2 * NOPE, NOPE)], c_kvT[:, c, :], start=(c == 0), stop=(c == 1))
                    end(mm)
            for i, n in enumerate(kv_loads):
                for t in range(TT):
                    o = begin(job("v_mla", 2 * i + t))
                    for c in range(2):
                        w = slot(n, (2, 1024))[:, c, :].rearrange("p (h d) -> p h d", h=4)[:, :, NOPE:2 * NOPE]
                        mm = pe.matmul(o, c_kvT[:, c, wide(t * P, P)], w, start=(c == 0), stop=(c == 1))
                    end(mm)
            for t in range(TT):
                pe.wait_ge(signal("q_pe_ready"), t + 1)
                o = begin(job("q_peT", t))
                for c in range(MLA_HEADS // 2):
                    mm = pe.transpose(o[:, wide(c * P, P)], q_pe[:, t, wide(c * P, P)], ident)
                end(mm)

            def mla_scores(o, i):
                hd, t = divmod(i, TT)
                if i == 0:
                    for nm, n in (("q_nope", 4), ("k_nope", 4), ("v_mla", 4), ("q_peT", 2)):
                        for j in range(n):
                            pe.wait_ge(*emptied(job(nm, j)))
                part = wide((hd % 2) * ROPE, ROPE)
                pe.matmul(o[:, 0:S], q_nopeT[:, hd, wide(t * P, P)], k_nopeT[:, hd, :], start=True, stop=False)
                return pe.matmul(o[:, 0:S], q_peT[part, hd // 2, wide(t * P, P)], k_peT[part, :], start=False, stop=True)

            def wide_values(v, unit0):
                def values(o, i):
                    for s in range(TT):
                        mm = pe.matmul(o[:, 0:P], probT[:, (unit0 + i) % ATT_BUF, wide(s * P, P)], v[:, s, wide(i // TT * P, P)], start=(s == 0), stop=(s == 1))
                    return mm
                return values

            attention("mla", MLA_UNITS, mla_unit0, mla_scores, wide_values(v_mla, mla_unit0), lambda i: TT)

            for g in range(DIL_GROUPS):
                channel_major(f"dil_q{g}", 2, hT)
                channel_major(f"dil_k{g}", 2, hT)
                token_major(f"dil_v{g}", 2, hT)

                def dil_scores(o, i):
                    hd, t = divmod(i, TT)
                    if i == 0:
                        for nm in "qkv":
                            for j in range(4):
                                pe.wait_ge(*emptied(job(f"dil_{nm}{g}", j)))
                    return pe.matmul(o[:, 0:S], q_dilT[:, hd, wide(t * P, P)], k_dilT[:, hd, :], start=True, stop=True)

                unit0 = dil_unit0 + g * DIL_UNITS
                attention(f"dil{g}_", DIL_UNITS, unit0, dil_scores, wide_values(v_dil, unit0), lambda i: TT)
            token_major("gates2", 4, hT)
            modulation("ada", 2, 8)
            modulation("ada", 3, 9)
            modulation("ada", 4, 10)
            pe.wait_ge(signal("mix_ready"), TT)
            transpose_tokens("mixT", h)
            for k in range(4):
                pe.wait_ge(*emptied(job("mixT", k)))
            token_major("w_out", 2, hT)
            modulation("ada", 5, 11)
            pe.wait_ge(signal("h4_ready"), TT)
            transpose_tokens("h4T", h)
            for k in range(4):
                pe.wait_ge(*emptied(job("h4T", k)))
            pe.wait_ge(signal("router2_in"), 16)
            o = begin(job("router2"))
            for t in range(TT):
                for c in range(KC):
                    mm = pe.matmul(o[:, wide(t * E, E)], hT[:, c, wide(t * P, P)], small_w[:, c, 0:E], start=(c == 0), stop=(c == KC - 1))
            end(mm)
            pe.wait_ge(signal("aff_ready"), 1)
            o = begin(job("affT"))
            for t in range(TT):
                mm = pe.transpose(o[0:E, wide(t * P, P)], gates[:, t, :], ident)
            end(mm)
            pe.wait_ge(signal("rank_T_ready"), 1)
            o = begin(job("rank2"))
            for t in range(TT):
                mm = pe.transpose(o[:, wide(t * E, E)], rank_T[:, wide(t * P, P)], ident[0:E, 0:E])
            end(mm)

            assert next_job[0] == job("ec")
            with pe.Fori(0, EC_ROUNDS) as it:
                R = Rounds(it, job("ec"), EC_JOBS, ec_load0, EC_LOADS)
                pe.wait_ge(signal("pick_ready"), it + (MOE_ROUNDS + 1))
                for j in range(4):
                    o = loop_begin(R, EC_XE + j)
                    for c in (2 * j, 2 * j + 1):
                        for t in range(TT):
                            mm = pe.matmul(o[:, wide((c % 2) * P, P)], h[:, t, c::KC], pick[:, t, 0:P], start=(t == 0), stop=(t == TT - 1))
                    end(mm)
                for t in range(TT):
                    o = loop_begin(R, EC_GW + t)
                    end(pe.transpose(o[:, 0:P], pick_gate[:, t, 0:P], ident))
                for j in range(4):
                    pe.wait_ge(*R.emptied(EC_XE + j))

                def ec_products(outs, lhs, l0, n_loads, width):
                    for n in range(n_loads):
                        for i in range(4):
                            pe.wait_ge(*R.arrived(l0 + 4 * n + i))
                        for c in range(2):
                            for b in range(2):
                                for i in range(4):
                                    mm = pe.matmul(outs[b][wide(i * CAP2, CAP2), :], lhs(2 * n + c, i), R.slot(l0 + 4 * n + i, (2, width))[:, c, wide(b * BANK, BANK)],
                                                   start=(n == c == 0), stop=(n == n_loads - 1 and c == 1))
                                if n == n_loads - 1 and c == 1:
                                    end(mm)
                        if n < n_loads - 1:
                            mm.then_inc(pieces_used, 1)

                for fp in range(2):
                    for l0, j in ((32 * fp, EC_GATE[fp]), (32 * fp + 16, EC_UP[fp])):
                        ec_products([loop_begin(R, j + b) for b in range(2)], lambda c, i: x_e[:, c, wide(i * CAP2, CAP2)], l0, 4, 1024)
                    for b in range(2):
                        o = loop_begin(R, EC_T[fp] + b)
                        pe.wait_ge(*R.emptied(EC_UP[fp] + b))
                        for c in range(4):
                            mm = pe.transpose(o[:, wide(c * P, P)], hid[:, b, wide(c * P, P)], ident)
                        end(mm)
                for fp in range(2):
                    for b in range(2):
                        pe.wait_ge(*R.emptied(EC_T[fp] + b))
                ec_products([loop_begin(R, EC_DOWN + b) for b in range(2)], lambda c, i: hidT[:, c, wide(i * CAP2, CAP2)], 64, 8, D)
                for n in range(2):
                    pe.wait_ge(*R.emptied(EC_DOWN + n))
                for n in range(2):
                    for t in range(TT):
                        o = loop_begin(R, EC_SUM + 2 * n + t)
                        end(pe.matmul(o, gate_T[:, 0, wide(t * P, P)], y_e[:, 0, wide(n * BANK, BANK)], start=True, stop=True))

        @block.scalar
        def _(act):
            step = Turn(act, act_step)
            a = nc.scalar

            def take(k, out, func=ACT.Copy, src=None, **kw):
                act.wait_ge(*done(k))
                step(a.activation, out, bank(k) if src is None else src(bank(k)), func, signals=emptied(k), **kw)

            def rstd_of(n, eps_col, squares=None):
                act.wait_ge(signal("var_ready"), n + 1)
                step(a.activation, rstd[:, :, 0], mv[:, :, 1], ACT.Ln, bias=eps_col)
                step(a.activation, rstd[:, :, 1], rstd[:, :, 0], ACT.Exp, scale=-0.5, signals=(signal("rstd_ready"), n + 1))

            def attention(name, n, unit0, keys):
                for i in range(n + LAG_PV):
                    if i < n:
                        u = unit0 + i
                        act.wait_ge(signal("max_ready"), u + 1)
                        step(a.activation, prob[:, u % ATT_BUF, 0:keys(i) * P], prob[:, u % ATT_BUF, 0:keys(i) * P], ACT.Exp,
                             bias=row_max[:, u:u + 1], accum_out=row_sum[:, u:u + 1], signals=(signal("probs_ready"), u + 1))
                    if 0 <= (j := i - LAG_T) < n:
                        if j >= ATT_BUF:
                            act.wait_ge(*done(job(f"{name}_pv{j - ATT_BUF}")))
                        w = keys(j) * P
                        take(job(f"{name}_t{j}"), probT[:, (unit0 + j) % ATT_BUF, 0:w], src=lambda o: o[:, 0:w])

            bias_keys = bias.rearrange("p h (t s) -> p t h s", t=TT)
            with act.Fori(0, BIAS_ROUNDS) as it:
                R = Rounds(it, job("bias"), BANKS)
                step.begin_loop(it, 0)
                for j in range(BANKS):
                    act.wait_ge(*R.done(j))
                    for t in range(TT):
                        keys = bass.ds(it * (2 * BIAS_KEYS) + (j % 4 * (S // 4) + j // 4 * BIAS_KEYS), BIAS_KEYS)
                        ins = a.activation(bias_keys[:, t, :, keys], R.bank(j)[:, wide(t * BIAS_KEYS * 24, BIAS_KEYS * 24)].rearrange("p (s h) -> p h s", h=24), ACT.Copy)
                    ins.then_inc(R.emptied(j)[0], 1)
                step.end_loop(BIAS_ROUNDS)
                step.last = None
            act.wait_ge(signal("c_in"), 32)
            step(a.activation, cact[:], cact[:], ACT.Silu, signals=(signal("cact_ready"), 1))
            act.wait_ge(signal("const_in"), 16)
            rstd_of(0, eps5)
            for n in range(2):
                take(job("mod0", n), mod[:, 0, wide(n * BANK, BANK)])
            for n in range(2):
                take(job("mod1", n), mod[:, 1, wide(n * BANK, BANK)], ACT.Identity, bias=1.0)
            act.wait_ge(signal("pad_ready"), 1)

            def conv_silu(j):
                for ct in (2 * j, 2 * j + 1):
                    act.wait_ge(signal("conv_sum_ready"), ct + 1)
                    step(a.activation, xcT[:, ct, :], prob[:, ct % ATT_BUF, :], ACT.Silu, signals=(signal("conv_ready"), ct + 1))

            for j in range(8):
                take(job("xbc", j), u_pad[:, 2 * j:2 * j + 2, 3:3 + S], src=lambda o: o.rearrange("p (c t) -> p c t", c=2))
                if j:
                    conv_silu(j - 1)
            for j in range(2):
                take(job("q", j), qT[:, 2 * j:2 * j + 2, :], src=lambda o: o.rearrange("p (c t) -> p c t", c=2), scale=FOX_D ** -0.5)
            conv_silu(7)
            for j in range(2):
                take(job("k", j), kT[:, 2 * j:2 * j + 2, :], src=lambda o: o.rearrange("p (c t) -> p c t", c=2))
            for j in range(4):
                take(job("z", j), silu_z[:, j % 2, wide(j // 2 * BANK, BANK)], ACT.Silu)
            for j in range(4):
                take(job("gs", j), sig_gs[:, j % 2, wide(j // 2 * BANK, BANK)], ACT.Sigmoid)
            for j in range(4):
                take(job("ga", j), sig_ga[:, j % 2, wide(j // 2 * BANK, BANK)], ACT.Sigmoid)
            act.wait_ge(signal("neg_abs_ready"), 1)
            step(a.activation, dtf_e[:], dtf_e[:], ACT.Exp)
            step(a.activation, dtf_e[:], dtf_e[:], ACT.Ln, bias=1.0)
            act.wait_ge(signal("head_in"), 32)
            step(a.activation, head_v[:, 0, :], head_v[:, 0, :], ACT.Exp, signals=(signal("softplus_ready"), 1))
            act.wait_ge(*emptied(job("cumsum")))
            step(a.activation, a_exp[:], a_exp[:], ACT.Exp, signals=(signal("a_exp_ready"), 1))
            for j in range(4):
                t, half = divmod(j, 2)
                take(job("xs_tok", j), xs_tok[:, t, wide(half * BANK, BANK)])
            take(job("b_tok"), b_tok[:].rearrange("p g n -> p (g n)"))
            for t in range(TT):
                take(job("cb", t), cb[:, t].rearrange("p g l -> p (g l)"))

            def decay_exp(k):
                act.wait_ge(*emptied(job(f"a_row{k}")))
                step(a.activation, decay[k % 3], decay[k % 3], ACT.Exp, signals=(signal("decay_exp_ready"), k + 1))

            for k in range(3):
                decay_exp(k)
            act.wait_ge(signal("x_end_ready"), 1)
            for half in range(2):
                take(job("state", half), prev[:, wide(half * BANK, BANK)])
            for k in range(3, TT * GROUPS):
                decay_exp(k)
            for t in range(TT):
                act.wait_ge(signal("gated_ready"), t + 1)
                step(a.activation, silu_z[:, t, :], y_tok[:, t, :], ACT.Square, scale=D ** -0.5, accum_out=mv[:, t, 1:2])
            act.wait_ge(act_step, step.n)
            step(a.activation, rstd[:, :, 0], mv[:, :, 1], ACT.Ln, bias=eps5)
            step(a.activation, rstd[:, :, 1], rstd[:, :, 0], ACT.Exp, scale=-0.5, signals=(signal("rms_ready"), 1))
            attention("fox", FOX_UNITS, 0, lambda i: i % TT + 1)
            for t in range(TT):
                take(job("oT", t), oT[:, :, wide(t * P, P)], src=lambda o: o.rearrange("p (c t) -> p c t", c=4))
            for j in range(4):
                t, half = divmod(j, 2)
                take(job("mT", j), hT[:, 4 * half:4 * half + 4, wide(t * P, P)], src=lambda o: o.rearrange("p (c t) -> p c t", c=4))
            rstd_of(1, eps5)
            for n in range(2):
                take(job("mod5", n), mod[:, 2, wide(n * BANK, BANK)], ACT.Identity, bias=1.0)
            rstd_of(2, eps5)
            for j in range(4):
                t, half = divmod(j, 2)
                take(job("h2T", j), hT[:, 4 * half:4 * half + 4, wide(t * P, P)], src=lambda o: o.rearrange("p (c t) -> p c t", c=4))
            act.wait_ge(signal("route_logits_ready"), 1)
            step(a.activation, route_g[:], route_g[:], ACT.Exp)
            step(a.activation, route_2[:], route_2[:], ACT.Exp, signals=(signal("route_exp_ready"), 1))

            for n in range(2):
                take(job("ada0", n), mod[:, 0, wide(n * BANK, BANK)])
            for n in range(2):
                take(job("ada1", n), mod[:, 1, wide(n * BANK, BANK)], ACT.Identity, bias=1.0)

            with act.Fori(0, MOE_ROUNDS) as it:
                R = Rounds(it, job("moe"), MOE_JOBS)
                step.begin_loop(it, 0)
                step.last = None

                def take_round(j, out, func=ACT.Copy, width=BANK):
                    act.wait_ge(*R.done(j))
                    step(a.activation, out, R.bank(j)[:, 0:width], func, signals=R.emptied(j))

                for p in range(2):
                    take_round(MOE_GW + p, gate_T[:, p, :], width=S)
                for p in range(2):
                    take_round(MOE_GATE[p], silu_g[:, p, :], ACT.Silu)
                for p in range(2):
                    take_round(MOE_T[p], hidT[:, 4 * p:4 * p + 4, :].rearrange("p c t -> p (c t)"))
                    for n in range(2):
                        take_round(MOE_DOWN[p] + n, y_e[:, p, wide(n * BANK, BANK)])
                step.end_loop(MOE_ROUNDS)
                step.last = None

            rstd_of(3, eps5)

            def square_means(n, srcs):
                for t in range(TT):
                    for src, to, width in srcs:
                        step(a.activation, silu_junk[:, 0:width], src(t), ACT.Square, scale=width ** -0.5, accum_out=to[:, t, 1:2])
                act.wait_ge(act_step, step.n)
                for _, to, _ in srcs:
                    step(a.activation, rstd[:, :, 0], to[:, :, 1], ACT.Ln, bias=eps6)
                    step(a.activation, to[:, :, 0], rstd[:, :, 0], ACT.Exp, scale=-0.5)
                act.wait_ge(act_step, step.n)
                step(a.activation, rstd[:, :, 0], to[:, :, 1], ACT.Copy, signals=(signal("rms2_ready"), n + 1))

            act.wait_ge(signal("x_b1_ready"), 1)
            step(a.activation, turn[:, 2:4].rearrange("p a t f -> p (a t f)"), turn[:, 0:2].rearrange("p a t f -> p (a t f)"), ACT.Sin, signals=(signal("sin_ready"), 1))
            square_means(0, [(lambda t: x[:, t, :], mv, D)])
            for j in range(4):
                t, half = divmod(j, 2)
                take(job("h3T", j), hT[:, 4 * half:4 * half + 4, wide(t * P, P)], src=lambda o: o.rearrange("p (c t) -> p c t", c=4))
            for j in range(4):
                i, t = divmod(j, 2)
                w = min(BANK, LAT - i * BANK)
                take(job("lat", j), lat[:, t, wide(i * BANK, w)], src=lambda o: o[:, 0:w])
            square_means(1, [(lambda t: lat[:, t, 0:Q_RANK], mv, Q_RANK), (lambda t: lat[:, t, wide(Q_RANK, KV_RANK)], mv2, KV_RANK)])

            def two_tiles(o):
                return o.rearrange("p (c t) -> p c t", c=2)

            for j in range(4):
                take(job("q_nope", j), q_nopeT[:, 2 * j:2 * j + 2, :], src=two_tiles)
            for j in range(4):
                take(job("k_nope", j), k_nopeT[:, 2 * j:2 * j + 2, :], src=two_tiles)
            for j in range(4):
                half, t = divmod(j, 2)
                take(job("v_mla", j), v_mla[:, t, wide(half * BANK, BANK)])
            for t in range(TT):
                take(job("q_peT", t), q_peT[:, :, wide(t * P, P)], src=lambda o: o.rearrange("p (c t) -> p c t", c=4))
            attention("mla", MLA_UNITS, mla_unit0, lambda i: TT)
            for g in range(DIL_GROUPS):
                for j in range(4):
                    take(job(f"dil_q{g}", j), q_dilT[:, 2 * j:2 * j + 2, :], src=two_tiles)
                for j in range(4):
                    take(job(f"dil_k{g}", j), k_dilT[:, 2 * j:2 * j + 2, :], src=two_tiles)
                for j in range(4):
                    take(job(f"dil_v{g}", j), v_dil[:, j % 2, wide(j // 2 * BANK, BANK)])
                attention(f"dil{g}_", DIL_UNITS, dil_unit0 + g * DIL_UNITS, lambda i: TT)
            for j in range(8):
                n, t = divmod(j, 2)
                take(job("gates2", j), (sig_a, sig_b)[n // 2][:, t, wide(n % 2 * BANK, BANK)], ACT.Sigmoid)
            act.wait_ge(signal("dil_shift_ready"), 1)
            step(a.activation, dil_w.rearrange("p g u -> p (g u)"), dil_w.rearrange("p g u -> p (g u)"), ACT.Exp, signals=(signal("dil_exp_ready"), 1))
            for unit in (2, 3, 4):
                for n in range(2):
                    take(job(f"ada{unit}", n), mod[:, (2, 0, 1)[unit - 2], wide(n * BANK, BANK)], ACT.Identity, bias=1.0 if unit == 4 else 0.0)
            for j in range(4):
                t, half = divmod(j, 2)
                take(job("mixT", j), hT[:, 4 * half:4 * half + 4, wide(t * P, P)], src=lambda o: o.rearrange("p (c t) -> p c t", c=4))
            act.wait_ge(signal("x2_ready"), 1)
            square_means(2, [(lambda t: x[:, t, :], mv, D)])
            for n in range(2):
                take(job("ada5", n), mod[:, 2, wide(n * BANK, BANK)])
            for j in range(4):
                t, half = divmod(j, 2)
                take(job("h4T", j), hT[:, 4 * half:4 * half + 4, wide(t * P, P)], src=lambda o: o.rearrange("p (c t) -> p c t", c=4))
            act.wait_ge(signal("aff_logits_ready"), 1)
            step(a.activation, gates[:], gates[:], ACT.Exp, signals=(signal("aff_exp_ready"), 1))

            with act.Fori(0, EC_ROUNDS) as it:
                R = Rounds(it, job("ec"), EC_JOBS)
                step.begin_loop(it, 0)
                step.last = None

                def take_ec(j, out, func=ACT.Copy, width=BANK):
                    act.wait_ge(*R.done(j))
                    step(a.activation, out, R.bank(j)[:, 0:width], func, signals=R.emptied(j))

                for t in range(TT):
                    take_ec(EC_GW + t, gate_T[:, 0, wide(t * P, P)], width=P)
                for fp in range(2):
                    for b in range(2):
                        take_ec(EC_GATE[fp] + b, silu_g[:, b, :], ACT.Silu)
                    for b in range(2):
                        take_ec(EC_T[fp] + b, hidT[:, 8 * fp + 4 * b:8 * fp + 4 * b + 4, :].rearrange("p c t -> p (c t)"))
                for n in range(2):
                    take_ec(EC_DOWN + n, y_e[:, 0, wide(n * BANK, BANK)])
                step.end_loop(EC_ROUNDS)
                step.last = None
            act.wait_ge(signal("x3_ready"), 1)
            square_means(3, [(lambda t: x[:, t, :], mv, D)])

        @block.vector
        def _(dve):
            step = Turn(dve, dve_step)
            v = nc.vector

            def take(k, op, *args, **kw):
                dve.wait_ge(*done(k))
                step(op, *args, signals=emptied(k), **kw)

            def norm_stats(src, n):
                for t in range(TT):
                    for half in range(2):
                        step(v.bn_stats, stats[:, t, half, :], src[:, t, wide(half * 512, 512)])
                    step(v.bn_aggr, mv[:, t, :], stats[:, t].rearrange("p a b -> p (a b)"), signals=(signal("var_ready"), n + 1) if t == TT - 1 else None)

            def normalize(dst, src, n, t):
                if t == 0:
                    dve.wait_ge(signal("rstd_ready"), n + 1)
                step(v.tensor_scalar, dst[:, t, :], src[:, t, :], mv[:, t, 0:1], rstd[:, t, 1:2], ALU.subtract, ALU.mult)

            def attention(name, n, unit0, masked, keys, out):
                for i in range(n + LAG_PV):
                    if i < n:
                        u, k, w = unit0 + i, job(f"{name}_qk{i}"), keys(i) * P
                        if i >= ATT_BUF:
                            dve.wait_ge(*done(job(f"{name}_t{i - ATT_BUF}")))
                        dve.wait_ge(*done(k))
                        masked(i, prob[:, u % ATT_BUF, 0:w], bank(k)[:, 0:w], emptied(k))
                        step(v.tensor_reduce, row_max[:, u:u + 1], prob[:, u % ATT_BUF, 0:w], AX, ALU.max, negate=True, signals=(signal("max_ready"), u + 1))
                    if 0 <= (j := i - LAG_PV) < n:
                        u, k = unit0 + j, job(f"{name}_pv{j}")
                        step(v.reciprocal, row_inv[:, u:u + 1], row_sum[:, u:u + 1])
                        take(k, v.tensor_scalar, out(j), bank(k)[:, 0:out(j).shape[-1]], row_inv[:, u:u + 1], None, ALU.mult)

            dve.wait_ge(signal("pos_in"), 96)
            dve.wait_ge(signal("const_in"), 16)
            step(v.tensor_copy, pos_all, pos_rows[:, 0:S])
            step(v.tensor_copy, pos_quarter, pos_rows[:, S:S + S // 4])
            with dve.Fori(0, BIAS_ROUNDS) as it:
                R = Rounds(it, job("bias"), BANKS)
                step.begin_loop(it, 4)
                for half in range(2):
                    dve.wait_ge(signal("one_hot_ready"), it * 2 + half)
                    keys = pos_quarter[:, bass.ds(it * (2 * BIAS_KEYS) + half * BIAS_KEYS, BIAS_KEYS)]
                    step(v.tensor_tensor, rel, keys.unsqueeze(2).to_broadcast([P, BIAS_KEYS, S]), pos_all.unsqueeze(1).to_broadcast([P, BIAS_KEYS, S]), ALU.subtract)
                    dve.wait_ge(pe_done, it * BANKS + 4 * half)
                    step(v.tensor_scalar, one_hot, rel, bucket_range[:, 0:1], None, ALU.is_ge)
                    step(v.scalar_tensor_tensor, one_hot, rel, bucket_range[:, 1:2], one_hot, ALU.is_le, ALU.mult,
                         signals=(signal("one_hot_ready"), it * 2 + (half + 1)))
                step.end_loop(BIAS_ROUNDS)
            dve.wait_ge(signal("bands_in"), 16)
            for b in range(BANKS):
                dve.wait_ge(evacuated[b], BIAS_ROUNDS)
            for g in range(DIL_GROUPS):
                heads = bias[:, wide(g * DIL_HEADS, DIL_HEADS), :]
                step(v.tensor_tensor, heads, heads, bands[:, g:g + 1, :].to_broadcast([P, DIL_HEADS, TT * S]), ALU.add, signals=(signal("bias_ready"), g + 1))
            step(v.tensor_copy, posf[:], pos_i[:])
            for t in range(TT):
                step(v.tensor_scalar, turn[:, 0, t, :], inv_freq, posf[:, t:t + 1], None, ALU.mult)
            step(v.tensor_scalar, turn[:, 2], turn[:, 0], 1.0 / TWO_PI, MAGIC, ALU.mult, ALU.add)
            step(v.tensor_scalar, turn[:, 2], turn[:, 2], MAGIC, None, ALU.subtract)
            step(v.scalar_tensor_tensor, turn[:, 0], turn[:, 2], -TWO_PI_HI, turn[:, 0], ALU.mult, ALU.add)
            step(v.scalar_tensor_tensor, turn[:, 0], turn[:, 2], -(TWO_PI - TWO_PI_HI), turn[:, 0], ALU.mult, ALU.add)
            step(v.tensor_scalar, turn[:, 1], turn[:, 0], TWO_PI / 4, None, ALU.add)
            step(v.tensor_scalar, turn[:, 2], turn[:, 1], PI, -TWO_PI, ALU.is_gt, ALU.mult)
            step(v.tensor_tensor, turn[:, 1], turn[:, 1], turn[:, 2], ALU.add)
            step(v.tensor_scalar, turn[:, 0:2], turn[:, 0:2], PI, -PI, ALU.min, ALU.max)
            dve.wait_ge(signal("bias_stored"), 16 * DIL_GROUPS)
            step(v.memset, u_pad[:, :, 0:3], 0.0, signals=(signal("pad_ready"), 1))
            dve.wait_ge(signal("x_in"), 16)
            norm_stats(x, 0)
            dve.wait_ge(signal("const_in"), 16)
            dve.wait_ge(signal("cact_ready"), 1)

            def repeat_cond(b):
                for c in range(KC):
                    step(v.tensor_scalar, cond[:, c, :], ones, cact[:, b, c:c + 1], None, ALU.mult, signals=(signal("cond_ready"), b + 1) if c == KC - 1 else None)

            repeat_cond(0)
            take(job("vecT"), v.tensor_copy, vecT[:, 0:85], bank(job("vecT"))[:, 0:85])
            for t in range(TT):
                normalize(h, x, 0, t)

            for unit in ("mod0", "mod1"):
                for n in range(2):
                    dve.wait_ge(*emptied(job(unit, n)))
            for t in range(TT):
                step(v.tensor_tensor, h[:, t, :], h[:, t, :], mod[:, 1, :], ALU.mult)
                step(v.tensor_tensor, h[:, t, :], h[:, t, :], mod[:, 0, :], ALU.add, signals=(signal("h_ready"), t + 1))
            for j in range(4):
                t, half = divmod(j, 2)
                take(job("hT", j), v.tensor_copy, hT[:, 4 * half:4 * half + 4, wide(t * P, P)], bank(job("hT", j)).rearrange("p (c t) -> p c t", c=4))

            for ct in range(16):
                dve.wait_ge(*emptied(job("xbc", ct // 2)))
                if ct >= ATT_BUF:
                    dve.wait_ge(signal("conv_ready"), ct - ATT_BUF + 1)
                acc = prob[:, ct % ATT_BUF, :]
                step(v.tensor_scalar, acc, u_pad[:, ct, 0:S], vecT[:, ct:ct + 1], vecT[:, 64 + ct:65 + ct], ALU.mult, ALU.add)
                for j in range(1, 4):
                    step(v.scalar_tensor_tensor, acc, u_pad[:, ct, j:j + S], vecT[:, 16 * j + ct:16 * j + ct + 1], acc, ALU.mult, ALU.add,
                         signals=(signal("conv_sum_ready"), ct + 1) if j == 3 else None)
            k = job("dtf")
            dve.wait_ge(*done(k))
            both = bank(k)[:, 0:TT * 24].rearrange("p (t c) -> p t c", t=TT)
            step(v.tensor_copy, dtf[:, :, 0:HEADS], both[:, :, 0:HEADS])
            step(v.tensor_scalar, dtf[:, :, HEADS:24], both[:, :, HEADS:24], -1.0, None, ALU.mult, signals=emptied(k))
            step(v.scalar_tensor_tensor, dtf_e[:], dtf[:], -1.0, dtf[:], ALU.mult, ALU.min, signals=(signal("neg_abs_ready"), 1))
            for j in range(2):
                take(job("v", j), v.tensor_copy, v_tok[:, j, :], bank(job("v", j)))
            dve.wait_ge(signal("softplus_ready"), 1)
            step(v.scalar_tensor_tensor, dtf[:], dtf[:], 0.0, dtf_e[:], ALU.max, ALU.add)
            step(v.tensor_copy, cum_in[:, :, HEADS:24], dtf[:, :, HEADS:24])
            step(v.scalar_tensor_tensor, cum_in[:, :, 0:HEADS], dtf[:, :, 0:HEADS], -1.0, head_v[:, 0:1, :].to_broadcast([P, TT, HEADS]), ALU.mult, ALU.mult,
                 signals=(signal("cum_in_ready"), 1))
            k = job("cumsum")
            dve.wait_ge(*done(k))
            step(v.tensor_copy, a_cs[:], bank(k)[:, 0:64].rearrange("p (t c) -> p t c", t=TT)[:, :, 0:HEADS])
            step(v.tensor_copy, neg_F[:, 0, :], bank(k)[:, 16:24])
            step(v.tensor_copy, neg_F[:, 1, :], bank(k)[:, 64:72])
            step(v.tensor_copy, a_exp[:, 0, :], a_cs[:, 1, :])
            step(v.tensor_tensor, a_exp[:, 1, :], bank(k)[:, 96:112], a_cs[:, 0, :], ALU.subtract, signals=emptied(k))
            for unit in (2, 3, 4):
                for n in range(2):
                    k = job(f"mod{unit}", n)
                    take(k, v.tensor_scalar, mod[:, (2, 0, 1)[unit - 2], wide(n * BANK, BANK)], bank(k), 0.0 if unit == 3 else 1.0, None, ALU.add)
            for j in range(4):
                t, half = divmod(j, 2)
                dve.wait_ge(*emptied(job("xs_tok", j)))
                step(v.tensor_tensor, xdt[:, t, wide(half * BANK, BANK)].rearrange("p (g d) -> p g d", d=HD), xs_tok[:, t, wide(half * BANK, BANK)].rearrange("p (g d) -> p g d", d=HD),
                     dtf[:, t, wide(half * 8, 8)].unsqueeze(2).to_broadcast([P, 8, HD]), ALU.mult)
            dve.wait_ge(signal("a_exp_ready"), 1)
            step(v.tensor_tensor, x_end.rearrange("p (g d) -> p g d", d=HD), xdt[:, 0, :].rearrange("p (g d) -> p g d", d=HD),
                 a_exp[:, 1, :].unsqueeze(2).to_broadcast([P, HEADS, HD]), ALU.mult, signals=(signal("x_end_ready"), 1))

            def segments(k):
                t, g = divmod(k, GROUPS)
                dve.wait_ge(*done(job(f"a_row{k}")))
                if k >= 3:
                    dve.wait_ge(*done(job(f"y_diag{(k - 3) // 2}")))
                for r in range(PER_GROUP):
                    hd = g * PER_GROUP + r
                    last = r == PER_GROUP - 1
                    step(v.scalar_tensor_tensor, decay[k % 3][:, wide(r * P, P)], bank(job(f"a_row{k}"))[:, wide(r * P, P)], a_cs[:, t, hd:hd + 1], seg_mask,
                         ALU.subtract, ALU.add, signals=emptied(job(f"a_row{k}")) if last else None)

            def masked_cb(k):
                t, g = divmod(k, GROUPS)
                dve.wait_ge(signal("decay_exp_ready"), k + 1)
                if k == 0:
                    for j in range(TT):
                        dve.wait_ge(*emptied(job("cb", j)))
                step(v.tensor_tensor, decay[k % 3].rearrange("p (r l) -> p r l", r=PER_GROUP), decay[k % 3].rearrange("p (r l) -> p r l", r=PER_GROUP),
                     cb[:, t, g:g + 1, :].to_broadcast([P, PER_GROUP, P]), ALU.mult, signals=(signal("decay_ready"), k + 1))

            y_off = params[:, 0, :]

            def heads_of(ap):
                return ap.rearrange("p (g d) -> p g d", d=HD)

            def assemble(m):
                t, half = divmod(m, 2)
                cols, k = wide(half * BANK, BANK), job(f"y_diag{m}")
                step(v.tensor_tensor, heads_of(y_tok[:, t, cols]), heads_of(xs_tok[:, t, cols]), head_v[:, 1, wide(half * 8, 8)].unsqueeze(2).to_broadcast([P, 8, HD]), ALU.mult)
                take(k, v.tensor_tensor, y_tok[:, t, cols], bank(k), y_tok[:, t, cols], ALU.add)
                if t:
                    step(v.tensor_tensor, y_tok[:, t, cols], y_tok[:, t, cols], y_off[:, cols], ALU.add)
                if m == 0:
                    for j in range(4):
                        dve.wait_ge(*emptied(job("z", j)))
                step(v.tensor_tensor, y_tok[:, t, cols], y_tok[:, t, cols], silu_z[:, t, cols], ALU.mult, signals=(signal("gated_ready"), t + 1) if half else None)

            segments(0)
            segments(1)
            masked_cb(0)
            segments(2)
            masked_cb(1)
            for half in range(2):
                k = job("y_off", half)
                take(k, v.tensor_tensor, heads_of(y_off[:, wide(half * BANK, BANK)]), heads_of(bank(k)), a_exp[:, 0, wide(half * 8, 8)].unsqueeze(2).to_broadcast([P, 8, HD]), ALU.mult)
            for m in range(2 * TT):
                assemble(m)
                for k in range(3 + 2 * m, min(5 + 2 * m, TT * GROUPS)):
                    segments(k)
                    masked_cb(k - 1)
                if m == 2:
                    masked_cb(TT * GROUPS - 1)
            dve.wait_ge(signal("rms_ready"), 1)
            for t in range(TT):
                step(v.tensor_scalar, y_tok[:, t, :], y_tok[:, t, :], rstd[:, t, 1:2], None, ALU.mult, signals=(signal("y_ssd_ready"), t + 1))

            def fox_mask(i, dst, src, taken):
                hd, t = divmod(i, TT)
                step(v.scalar_tensor_tensor, dst, src, neg_F[:, t, hd:hd + 1], causal[:, (1 - t) * P:2 * P], ALU.subtract, ALU.add, signals=taken)

            attention("fox", FOX_UNITS, 0, fox_mask, lambda i: i % TT + 1, lambda i: o_fox[:, i % TT, wide(i // TT * FOX_D, FOX_D)])
            dve.wait_ge(signal("ssd_w_in"), 16)
            for j in range(4):
                t, half = divmod(j, 2)
                k = job("yT", j)
                take(k, v.tensor_tensor, hT[:, 4 * half:4 * half + 4, wide(t * P, P)], bank(k).rearrange("p (c t) -> p c t", c=4),
                     ssd_w[:, 4 * half:4 * half + 4].unsqueeze(2).to_broadcast([P, 4, P]), ALU.mult)
            for j in range(4):
                n, t = divmod(j, 2)
                cols = wide(n * BANK, BANK)
                if j == 0:
                    for i in range(4):
                        dve.wait_ge(*emptied(job("ga", i)))
                k = job("merge", 2 * j)
                take(k, v.tensor_tensor, h[:, t, cols], bank(k), sig_gs[:, t, cols], ALU.mult)
                k = job("merge", 2 * j + 1)
                take(k, v.tensor_tensor, junk[:, 0:BANK], bank(k), sig_ga[:, t, cols], ALU.mult)
                step(v.tensor_tensor, h[:, t, cols], h[:, t, cols], junk[:, 0:BANK], ALU.add, signals=(signal("merged_ready"), j + 1))

            def residual(name):
                for j in range(4):
                    n, t = divmod(j, 2)
                    cols, k = wide(n * BANK, BANK), job(name, j)
                    take(k, v.tensor_tensor, junk[:, 0:BANK], bank(k), mod[:, 2, cols], ALU.mult)
                    step(v.scalar_tensor_tensor, x[:, t, cols], x[:, t, cols], ALPHA, junk[:, 0:BANK], ALU.mult, ALU.add)

            residual("w_o")
            norm_stats(x, 1)
            for t in range(TT):
                normalize(x, x, 1, t)
                if t == 0:
                    dve.wait_ge(signal("params_in"), 32)
                step(v.tensor_tensor, x[:, t, :], x[:, t, :], params[:, 0, :], ALU.mult)
                step(v.tensor_tensor, x[:, t, :], x[:, t, :], params[:, 1, :], ALU.add, signals=(signal("x_mid_ready"), 1) if t else None)
            norm_stats(x, 2)
            for t in range(TT):
                normalize(h, x, 2, t)
                step(v.tensor_tensor, h[:, t, :], h[:, t, :], mod[:, 1, :], ALU.mult)
                step(v.tensor_tensor, h[:, t, :], h[:, t, :], mod[:, 0, :], ALU.add, signals=(signal("h2_ready"), t + 1))

            for n in range(2):
                dve.wait_ge(*done(job("mod5", n)))
            repeat_cond(1)

            def first_of(dst, vals, top, n):
                step(v.tensor_reduce, top, vals, AX, ALU.max)
                step(v.tensor_tensor, dst, vals, top.unsqueeze(2).to_broadcast([P, TT, n]), ALU.is_equal)
                step(v.tensor_tensor, dst, dst, desc[:, E - n:E].unsqueeze(1).to_broadcast([P, TT, n]), ALU.mult)
                step(v.tensor_reduce, route_top[:], dst, AX, ALU.max)
                step(v.tensor_tensor, dst, dst, route_top[:].unsqueeze(2).to_broadcast([P, TT, n]), ALU.is_equal)

            k = job("router")
            dve.wait_ge(*done(k))
            step(v.tensor_copy, logits[:], bank(k)[:, 0:TT * 20].rearrange("p (t c) -> p t c", t=TT), signals=emptied(k))
            first_of(hot_g[:], logits[:, :, 0:4], top1[:], 4)
            step(v.tensor_tensor, route_g[:], logits[:, :, 0:4], top1[:].unsqueeze(2).to_broadcast([P, TT, 4]), ALU.subtract)
            for t in range(TT):
                step(v.tensor_tensor, in_group[:, t].rearrange("p (g e) -> p g e", g=4), logits[:, t, 4:20].rearrange("p (g e) -> p g e", g=4), hot_g[:, t, :].unsqueeze(2).to_broadcast([P, 4, 4]), ALU.mult)
                step(v.tensor_reduce, e_in[:, t, :], in_group[:, t].rearrange("p (g e) -> p e g", g=4), AX, ALU.add)
            first_of(hot1[:], e_in[:], top1[:], 4)
            step(v.scalar_tensor_tensor, e_in[:], hot1[:], NEG, e_in[:], ALU.mult, ALU.add)
            first_of(hot2[:], e_in[:], top2[:], 4)
            step(v.tensor_tensor, route_2[:], top2[:], top1[:], ALU.subtract, signals=(signal("route_logits_ready"), 1))
            step(v.tensor_tensor, e_in[:], hot1[:], hot2[:], ALU.add)
            for t in range(TT):
                step(v.tensor_tensor, chosen[:, t].rearrange("p (g e) -> p g e", g=4), hot_g[:, t, :].unsqueeze(2).to_broadcast([P, 4, 4]),
                     e_in[:, t, :].unsqueeze(1).to_broadcast([P, 4, 4]), ALU.mult, signals=(signal("chosen_ready"), 1) if t else None)
            dve.wait_ge(signal("route_exp_ready"), 1)
            step(v.tensor_reduce, top1[:], route_g[:], AX, ALU.add)
            step(v.scalar_tensor_tensor, top1[:], route_2[:], 1.0, top1[:], ALU.add, ALU.mult)
            step(v.reciprocal, top1[:], top1[:])
            step(v.tensor_tensor, top2[:], route_2[:], top1[:], ALU.mult)
            step(v.tensor_tensor, hot1[:], hot1[:], top1[:].unsqueeze(2).to_broadcast([P, TT, 4]), ALU.mult)
            step(v.tensor_tensor, hot2[:], hot2[:], top2[:].unsqueeze(2).to_broadcast([P, TT, 4]), ALU.mult)
            step(v.tensor_tensor, hot1[:], hot1[:], hot2[:], ALU.add)
            for t in range(TT):
                step(v.tensor_tensor, gates[:, t].rearrange("p (g e) -> p g e", g=4), hot_g[:, t, :].unsqueeze(2).to_broadcast([P, 4, 4]),
                     hot1[:, t, :].unsqueeze(1).to_broadcast([P, 4, 4]), ALU.mult)
            k = job("rank")
            take(k, v.tensor_tensor, rank[:], bank(k)[:, 0:TT * E].rearrange("p (t e) -> p t e", t=TT), chosen[:], ALU.mult)

            step(v.memset, y_sum, 0.0)
            step(v.memset, pass_shift[:], 0.0)
            step(v.memset, pass_shift[:, QUADS - 1:QUADS], float(CAP))

            def one_hots(quad, width, n, signalled):
                for t in range(TT):
                    step(v.tensor_tensor, pick[:, t, 0:4 * width].rearrange("p (e j) -> p e j", e=4), iota1[:, 0:width].unsqueeze(1).to_broadcast([P, 4, width]),
                         rank[:, t, bass.ds(quad * 4, 4)].unsqueeze(2).to_broadcast([P, 4, width]), ALU.is_equal)
                for t in range(TT):
                    step(v.tensor_tensor, pick_gate[:, t, 0:4 * width].rearrange("p (e j) -> p e j", e=4), pick[:, t, 0:4 * width].rearrange("p (e j) -> p e j", e=4),
                         gates[:, t, bass.ds(quad * 4, 4)].unsqueeze(2).to_broadcast([P, 4, width]), ALU.mult, signals=(signal("pick_ready"), signalled) if t else None)

            with dve.Fori(0, MOE_ROUNDS) as it:
                R = Rounds(it, job("moe"), MOE_JOBS)
                step.begin_loop(it, 4)
                quad = it & (QUADS - 1)
                one_hots(quad, CAP, 4, it + 1)
                for j in range(4):
                    dve.wait_ge(*R.done(MOE_XE + j))
                    step(v.tensor_copy, x_e[:, 2 * j:2 * j + 2, :].rearrange("p c t -> p (c t)"), R.bank(MOE_XE + j), signals=R.emptied(MOE_XE + j))
                for p in range(2):
                    dve.wait_ge(*R.emptied(MOE_GATE[p]))
                    dve.wait_ge(*R.done(MOE_UP[p]))
                    step(v.tensor_tensor, hid[:, p, :], R.bank(MOE_UP[p]), silu_g[:, p, :], ALU.mult, signals=R.emptied(MOE_UP[p]))
                for p in range(2):
                    for n in range(2):
                        for t in range(TT):
                            j, cols = MOE_SUM[p] + 2 * n + t, wide(n * BANK, BANK)
                            dve.wait_ge(*R.done(j))
                            step(v.tensor_tensor, y_sum[:, t, cols], R.bank(j), y_sum[:, t, cols], ALU.add, signals=R.emptied(j))
                step(v.tensor_tensor, rank[:], rank[:], pass_shift[:, bass.ds(quad, 1)].unsqueeze(2).to_broadcast([P, TT, E]), ALU.subtract)
                step.end_loop(MOE_ROUNDS)

            def residual_sum(alpha):
                for t in range(TT):
                    step(v.tensor_tensor, y_sum[:, t, :], y_sum[:, t, :], mod[:, 2, :], ALU.mult)
                    step(v.scalar_tensor_tensor, x[:, t, :], x[:, t, :], alpha, y_sum[:, t, :], ALU.mult, ALU.add)

            residual_sum(ALPHA)
            norm_stats(x, 3)
            for t in range(TT):
                normalize(x, x, 3, t)
                if t == 0:
                    dve.wait_ge(signal("params_in"), 64)
                step(v.tensor_tensor, x[:, t, :], x[:, t, :], params[:, 0, :], ALU.mult)
                step(v.tensor_tensor, x[:, t, :], x[:, t, :], params[:, 1, :], ALU.add, signals=(signal("x_b1_ready"), 1) if t else None)

            def rms_modulated(n, gain, ready, value):
                dve.wait_ge(signal("rms2_ready"), n + 1)
                for t in range(TT):
                    step(v.scalar_tensor_tensor, h[:, t, :], x[:, t, :], mv[:, t, 0:1], gain, ALU.mult, ALU.mult)
                    step(v.tensor_tensor, h[:, t, :], h[:, t, :], mod[:, 1, :], ALU.mult)
                    step(v.tensor_tensor, h[:, t, :], h[:, t, :], mod[:, 0, :], ALU.add, signals=(signal(ready), t + 1))

            dve.wait_ge(signal("params_in"), 96)
            for unit in ("ada0", "ada1"):
                for n in range(2):
                    dve.wait_ge(*emptied(job(unit, n)))
            rms_modulated(0, params[:, 0, :], "h3_ready", 1)

            def rotate(dst, src, t, heads, taken=None):
                half = ROPE // 2
                n = heads * half
                sin, cos = (turn[:, i, t, :].unsqueeze(1).to_broadcast([P, heads, half]) for i in (2, 3))
                one, two = (rope_tmp[:, i, 0:n].rearrange("p (h d) -> p h d", h=heads) for i in (0, 1))
                s1, s2, d1, d2 = src[:, :, 0:half], src[:, :, half:ROPE], dst[:, :, 0:half], dst[:, :, half:ROPE]
                step(v.tensor_tensor, one, s1, cos, ALU.mult)
                step(v.tensor_tensor, two, s2, sin, ALU.mult)
                step(v.tensor_tensor, d1, one, two, ALU.subtract)
                step(v.tensor_tensor, one, s1, sin, ALU.mult)
                step(v.tensor_tensor, two, s2, cos, ALU.mult, signals=taken)
                return d2, one, two

            for i in range(4):
                dve.wait_ge(*emptied(job("lat", i)))
            dve.wait_ge(signal("rms2_ready"), 2)
            dve.wait_ge(signal("sin_ready"), 1)
            for t in range(TT):
                d2, one, two = rotate(k_pe[:, t, 0:ROPE].unsqueeze(1), lat[:, t, LAT - ROPE:LAT].unsqueeze(1), t, 1)
                step(v.tensor_tensor, d2, one, two, ALU.add)
                step(v.tensor_copy, k_pe[:, t, ROPE:2 * ROPE], k_pe[:, t, 0:ROPE])
                step(v.tensor_scalar, lat[:, t, 0:Q_RANK], lat[:, t, 0:Q_RANK], mv[:, t, 0:1], None, ALU.mult)
                step(v.tensor_scalar, lat[:, t, wide(Q_RANK, KV_RANK)], lat[:, t, wide(Q_RANK, KV_RANK)], mv2[:, t, 0:1], None, ALU.mult,
                     signals=(signal("lat_ready"), 1) if t else None)
            for t in range(TT):
                k = job("latT", 2 * t)
                take(k, v.tensor_tensor, c_qT[:, :, wide(t * P, P)], bank(k)[:, 0:3 * P].rearrange("p (c t) -> p c t", c=3),
                     vecT[:, 80:83].unsqueeze(2).to_broadcast([P, 3, P]), ALU.mult)
                k = job("latT", 2 * t + 1)
                dve.wait_ge(*done(k))
                step(v.tensor_copy, k_peT[:, wide(t * P, P)], bank(k)[:, 2 * P:3 * P])
                step(v.tensor_tensor, c_kvT[:, :, wide(t * P, P)], bank(k)[:, 0:2 * P].rearrange("p (c t) -> p c t", c=2),
                     vecT[:, 83:85].unsqueeze(2).to_broadcast([P, 2, P]), ALU.mult, signals=emptied(k))
            for t in range(TT):
                k = job("q_pe", t)
                dve.wait_ge(*done(k))
                by_head = q_pe[:, t, :].rearrange("p (h d) -> p h d", h=MLA_HEADS)
                d2, one, two = rotate(by_head, bank(k).rearrange("p (h d) -> p h d", h=MLA_HEADS), t, MLA_HEADS, emptied(k))
                dve.wait_ge(dve_step, step.n)
                step(v.tensor_tensor, d2, one, two, ALU.add, signals=(signal("q_pe_ready"), t + 1))

            def mla_scaled(i, dst, src, taken):
                step(v.tensor_scalar, dst, src, (NOPE + ROPE) ** -0.5, None, ALU.mult, signals=taken)

            attention("mla", MLA_UNITS, mla_unit0, mla_scaled, lambda i: TT, lambda i: o_mla[:, i % TT, wide(i // TT * P, P)])

            for g in range(DIL_GROUPS):
                unit0 = dil_unit0 + g * DIL_UNITS

                def dil_biased(i, dst, src, taken):
                    hd, t = divmod(i, TT)
                    n = g * DIL_HEADS + hd
                    if t == 0:
                        dve.wait_ge(bias_in[n % 4], 16 * (n // 4 + 1))
                    step(v.scalar_tensor_tensor, dst, src, DIL_D ** -0.5, bias_tile[:, n % 4, wide(t * S, S)], ALU.mult, ALU.add, signals=taken)

                attention(f"dil{g}_", DIL_UNITS, unit0, dil_biased, lambda i: TT, lambda i: o_dil[g][:, i % TT, wide(i // TT * P, P)])
            top = dil_top[:]
            stat = [wide(dil_unit0 + g * DIL_UNITS, DIL_UNITS) for g in range(DIL_GROUPS)]
            step(v.tensor_tensor, top, row_max[:, stat[0]], row_max[:, stat[1]], ALU.min)
            step(v.tensor_tensor, top, top, row_max[:, stat[2]], ALU.min)
            for g in range(DIL_GROUPS):
                step(v.tensor_tensor, dil_w[:, g, :], top, row_max[:, stat[g]], ALU.subtract, signals=(signal("dil_shift_ready"), 1) if g == 2 else None)
            dve.wait_ge(signal("dil_exp_ready"), 1)
            for g in range(DIL_GROUPS):
                step(v.tensor_tensor, dil_w[:, g, :], dil_w[:, g, :], row_sum[:, stat[g]], ALU.mult)
            step(v.tensor_tensor, top, dil_w[:, 0, :], dil_w[:, 1, :], ALU.add)
            step(v.tensor_tensor, top, top, dil_w[:, 2, :], ALU.add)
            step(v.reciprocal, top, top)
            for g in range(DIL_GROUPS):
                step(v.tensor_tensor, dil_w[:, g, :], dil_w[:, g, :], top, ALU.mult)

            def by_head(ap):
                return ap.rearrange("p (h d) -> p h d", h=DIL_HEADS)

            for j in range(8):
                dve.wait_ge(*emptied(job("gates2", j)))
            for t in range(TT):
                for g in range(DIL_GROUPS):
                    w = dil_w[:, g, t:DIL_UNITS:TT].unsqueeze(2).to_broadcast([P, DIL_HEADS, DIL_D])
                    step(v.tensor_tensor, by_head(o_dil[g][:, t, :]), by_head(o_dil[g][:, t, :]), w, ALU.mult)
                for g in (1, 2):
                    step(v.tensor_tensor, o_dil[0][:, t, :], o_dil[0][:, t, :], o_dil[g][:, t, :], ALU.add)
                step(v.tensor_tensor, o_dil[0][:, t, :], o_dil[0][:, t, :], sig_b[:, t, :], ALU.mult)
                step(v.tensor_tensor, o_mla[:, t, :], o_mla[:, t, :], sig_a[:, t, :], ALU.mult)
                step(v.tensor_tensor, h[:, t, :], o_mla[:, t, :], o_dil[0][:, t, :], ALU.add, signals=(signal("mix_ready"), t + 1))
            for n in range(2):
                dve.wait_ge(*emptied(job("ada2", n)))
            for j in range(4):
                n, t = divmod(j, 2)
                cols, k = wide(n * BANK, BANK), job("w_out", j)
                take(k, v.tensor_tensor, junk[:, 0:BANK], bank(k), mod[:, 2, cols], ALU.mult)
                step(v.tensor_tensor, x[:, t, cols], x[:, t, cols], junk[:, 0:BANK], ALU.add, signals=(signal("x2_ready"), 1) if j == 3 else None)
            for unit in ("ada3", "ada4"):
                for n in range(2):
                    dve.wait_ge(*emptied(job(unit, n)))
            rms_modulated(2, params[:, 1, :], "h4_ready", 1)

            k = job("router2")
            dve.wait_ge(*done(k))
            step(v.tensor_copy, gates[:], bank(k)[:, 0:TT * E].rearrange("p (t e) -> p t e", t=TT), signals=emptied(k))
            step(v.tensor_reduce, top1[:], gates[:], AX, ALU.max)
            step(v.tensor_tensor, gates[:], gates[:], top1[:].unsqueeze(2).to_broadcast([P, TT, E]), ALU.subtract, signals=(signal("aff_logits_ready"), 1))
            dve.wait_ge(signal("aff_exp_ready"), 1)
            step(v.tensor_reduce, top1[:], gates[:], AX, ALU.add)
            step(v.reciprocal, top1[:], top1[:])
            step(v.tensor_tensor, gates[:], gates[:], top1[:].unsqueeze(2).to_broadcast([P, TT, E]), ALU.mult, signals=(signal("aff_ready"), 1))
            k = job("affT")
            take(k, v.tensor_copy, affT[:], bank(k)[0:E, 0:S])
            for i in range(CAP2 // 8):
                src, dst = (affT, topped) if i % 2 == 0 else (topped, affT)
                step(v.max, best8[:], src[:])
                step(v.match_replace, dst[:], best8[:], src[:], -1.0)
            step(v.tensor_scalar, affT[:], affT[:], 0.0, None, ALU.is_lt)
            step(v.memset, topped[:], 1.0)
            step(v.tensor_tensor_scan, rank_T[:], topped[:], affT[:], 0.0, ALU.mult, ALU.add)
            step(v.tensor_tensor, rank_T[:], rank_T[:], affT[:], ALU.mult, signals=(signal("rank_T_ready"), 1))
            k = job("rank2")
            take(k, v.tensor_copy, rank[:], bank(k)[:, 0:TT * E].rearrange("p (t e) -> p t e", t=TT))

            step(v.memset, y_sum, 0.0)
            with dve.Fori(0, EC_ROUNDS) as it:
                R = Rounds(it, job("ec"), EC_JOBS)
                step.begin_loop(it, 3)
                one_hots(it, CAP2, 4, it + (MOE_ROUNDS + 1))
                for j in range(4):
                    dve.wait_ge(*R.done(EC_XE + j))
                    step(v.tensor_copy, x_e[:, 2 * j:2 * j + 2, 0:P], R.bank(EC_XE + j)[:, 0:2 * P].rearrange("p (c t) -> p c t", c=2), signals=R.emptied(EC_XE + j))
                for fp in range(2):
                    for b in range(2):
                        dve.wait_ge(*R.emptied(EC_GATE[fp] + b))
                        dve.wait_ge(*R.done(EC_UP[fp] + b))
                        if fp:
                            dve.wait_ge(*R.done(EC_T[0] + b))
                        step(v.tensor_tensor, hid[:, b, :], R.bank(EC_UP[fp] + b), silu_g[:, b, :], ALU.mult, signals=R.emptied(EC_UP[fp] + b))
                for n in range(2):
                    for t in range(TT):
                        j, cols = EC_SUM + 2 * n + t, wide(n * BANK, BANK)
                        dve.wait_ge(*R.done(j))
                        step(v.tensor_tensor, y_sum[:, t, cols], R.bank(j), y_sum[:, t, cols], ALU.add, signals=R.emptied(j))
                step.end_loop(EC_ROUNDS)
                step.last = None
            for j in range(4):
                dve.wait_ge(evacuated[(job("ec") + EC_SUM + j) % BANKS], (job("ec") + (EC_ROUNDS - 1) * EC_JOBS + EC_SUM + j) // BANKS + 1)
            for n in range(2):
                dve.wait_ge(*emptied(job("ada5", n)))
            for t in range(TT):
                step(v.tensor_tensor, y_sum[:, t, :], y_sum[:, t, :], mod[:, 2, :], ALU.mult)
                step(v.tensor_tensor, x[:, t, :], x[:, t, :], y_sum[:, t, :], ALU.add, signals=(signal("x3_ready"), 1) if t else None)
            dve.wait_ge(signal("rms2_ready"), 4)
            dve.wait_ge(signal("params_in"), 128)
            for t in range(TT):
                step(v.scalar_tensor_tensor, h[:, t, :], x[:, t, :], mv[:, t, 0:1], params[:, 0, :], ALU.mult, ALU.mult, signals=(signal("out_ready"), t + 1))


def constants():
    import numpy as np

    f = np.float32
    i = np.arange(128)
    ident = np.eye(128, dtype=f)
    tri = (i[:, None] <= i[None, :]).astype(f)
    mask = np.where(i[None, :] > i[:, None], f(-1e30), f(0)).astype(f)
    causal = np.concatenate([np.zeros((128, 128), f), mask], 1)
    seg_mask = np.ascontiguousarray(mask.T)
    ones = np.ones((128, 128), f)
    iota1 = np.broadcast_to(np.arange(1, 65, dtype=f), (128, 64))
    desc = np.broadcast_to(np.arange(16, 0, -1, dtype=f), (128, 16))
    freq = (f(10000.0) ** (-np.arange(0, 64, 2, dtype=f) / f(64))).astype(f)
    inv_freq = np.broadcast_to(freq, (128, 32))
    low = [0, 1, 2, 3, 4, 5, 6, 7] + [int(np.ceil(8 * 128 ** (j / 8) - 1e-9)) for j in range(8)]
    high = [n - 1 for n in low[1:]] + [1 << 24]
    table = [(-b, -a) for a, b in zip(low, high)] + [(max(a, 1), b) for a, b in zip(low, high)]
    buckets = np.tile(np.array(table, f), (4, 1))
    eps = np.broadcast_to(np.array([1e-5, 1e-6], f), (128, 2))
    return np.ascontiguousarray(np.concatenate([ident, tri, causal, seg_mask, ones, iota1, desc, inv_freq, buckets, eps], 1))


def band_masks():
    import numpy as np

    t, s = np.arange(256)[:, None], np.arange(256)[None, :]
    groups = [np.where(((t - s) % d == 0) & (abs(t - s) <= 64 * d), 0.0, -1e30) for d in (1, 4, 16)]
    return np.ascontiguousarray(np.stack(groups).astype(np.float32).reshape(3, 2, 128, 256).transpose(2, 0, 1, 3))


def kernel(**inputs):
    import concourse.bacc as bacc
    import numpy as np
    from concourse import mybir
    from concourse.bass_utils import run_bass_kernel_spmd

    nc = bacc.Bacc("TRN2", target_bir_lowering=False, num_devices=1)
    given = dict(inputs, consts=constants(), bands=band_masks())
    arrays, tensors = {}, {}
    for name, value in given.items():
        value = np.ascontiguousarray(value)
        arrays[f"in_{name}"] = value
        tensors[name] = nc.dram_tensor(f"in_{name}", value.shape, mybir.dt.from_np(value.dtype), kind="ExternalInput").ap()
    out = nc.dram_tensor("out", inputs["x"].shape, mybir.dt.float32, kind="ExternalOutput").ap()
    build_program(nc, tensors, out)
    done = run_bass_kernel_spmd(nc, [arrays], core_ids=[0])
    return done.results[0]["out"]
```

```python
def build_program(nc, A, out):
    from contextlib import ExitStack

    from concourse import bass, mybir

    F32 = mybir.dt.float32
    I32 = mybir.dt.int32
    ALU = mybir.AluOpType
    ACT = mybir.ActivationFunctionType
    AX = mybir.AxisListType.X

    P = 128
    S, D = A["x"].shape[1:]
    TT = S // P
    KC = D // P
    BANKS = 8
    BANK = 512
    SLOTS = 8
    SLOT = 2048
    HEADS, HD, GROUPS, STATE = 16, 64, 4, 128
    PER_GROUP = HEADS // GROUPS
    FOX_HEADS, FOX_D = 8, 64
    DIL_GROUPS, DIL_HEADS, DIL_D = 3, 8, 128
    MLA_HEADS, NOPE, ROPE = 8, 128, 64
    Q_RANK, KV_RANK = 384, 256
    E = 16
    QUADS = E // 4
    BUCKETS = 32
    ALPHA = 2 ** 0.25
    NEG = -1e30
    PI = 3.1415925
    TWO_PI = 6.283185307179586
    TWO_PI_HI = 6.28125
    MAGIC = 12582912.0

    ctx = ExitStack()
    with ctx:
        def sb(name, shape, dt=F32):
            return ctx.enter_context(nc.sbuf_tensor(name, shape, dt))

        def sem(name):
            return ctx.enter_context(nc.semaphore(name))

        ring = sb("ring", [P, SLOTS, SLOT])
        psum = ctx.enter_context(nc.psum_tensor("psum", [P, BANKS, BANK], F32))
        x = sb("x_tok", [P, TT, D])
        h = sb("h_tok", [P, TT, D])
        hT = sb("hT", [P, KC, S])
        mod = sb("mod", [P, 3, D])
        params = sb("params", [P, 2, D])
        consts = sb("consts", [P, A["consts"].shape[1]])
        vecT = sb("vecT", [P, P])
        ssd_w = sb("ssd_w", [P, KC])
        cact = sb("cact", [P, 2, KC])
        cond = sb("cond", [P, 2, KC, 64])
        mod_rows = sb("mod_rows", [P, BANK])
        UNITS = 12
        small_w = sb("small_w", [P, KC, 24])
        small_b = sb("small_b", [1, 24])
        head_v = sb("head_v", [P, 2, HEADS])
        stats = sb("stats", [P, TT, 2, 6])
        mv = sb("mv", [P, TT, 2])
        rstd = sb("rstd", [P, TT, 2])
        junk = sb("junk", [P, D])
        rows = junk[:, D - P:D]
        row_max = sb("row_max", [P, 80])
        row_sum = sb("row_sum", [P, 80])
        row_inv = sb("row_inv", [P, 80])
        prob = sb("prob", [P, 4, S])
        probT = sb("probT", [P, 4, S])
        pos_i = sb("pos_i", [P, TT], I32)
        turn = sb("turn", [P, 4, TT, ROPE // 2])
        table = sb("table", [P, P])
        affT, topped, rank_T = (probT[0:E, i, :] for i in range(3))
        best8 = sb("best8", [E, 8])
        WORK = 17968
        work = sb("work", [P, WORK])

        def view(at, *dims):
            n = 1
            for d in dims:
                n *= d
            assert at + n <= WORK, (at, dims)
            v = work[:, at:at + n]
            if len(dims) == 2:
                v = v.rearrange("p (a b) -> p a b", a=dims[0])
            elif len(dims) == 3:
                v = v.rearrange("p (a b c) -> p a b c", a=dims[0], b=dims[1])
            return v

        at = [0]

        def const(n):
            at[0] += n
            return consts[:, at[0] - n:at[0]]

        ident, tri, causal, seg_mask, ones = const(P), const(P), const(2 * P), const(P), const(P)
        iota1, desc, inv_freq, bucket_range, eps, select = const(64), const(E), const(ROPE // 2), const(2), const(2), const(32)
        ones_row = ones[0:1, :]
        eps5, eps6 = eps[:, 0:1], eps[:, 1:2]

        pe_done = sem("pe_done")
        evacuated = [sem(f"evacuated{b}") for b in range(BANKS)]
        weights_in = [sem(f"weights_in{s}") for s in range(SLOTS)]
        act_step, dve_step = sem("act_step"), sem("dve_step")

        named = {}

        def signal(name):
            if name not in named:
                named[name] = sem(name)
            return named[name]

        first_job, n_jobs = {}, [0]

        def jobs(name, n):
            first_job[name] = n_jobs[0]
            n_jobs[0] += n

        def job(name, i=0):
            if name in first_job:
                return first_job[name] + i
            chunk = f"{name}_{i // 2}"
            return first_job[chunk] + i % 2 if chunk in first_job else first_job[f"{chunk}_{i % 2}"]

        def bank(k):
            return psum[:, k % BANKS, :]

        def done(k):
            return pe_done, k + 1

        def emptied(k):
            return evacuated[k % BANKS], k // BANKS + 1

        class Turn:

            def __init__(self, eng, own):
                self.eng, self.own, self.n, self.last = eng, own, 0, None
                self.it, self.per = None, 0

            def value(self):
                return self.n if self.it is None else self.n + self.it * self.per

            def __call__(self, op, *args, signals=None, **kw):
                if self.last is not None:
                    self.eng.wait_ge(*self.last)
                ins = op(*args, **kw)
                if signals is None:
                    self.n += 1
                    ins.then_inc(self.own, 1)
                    self.last = self.own, self.value()
                else:
                    ins.then_inc(signals[0], 1)
                    self.last = signals
                return ins

            def begin_loop(self, it, per, first=0):
                self.it, self.per, self.start = it - first if first else it, per, self.n
                self.last = self.own, self.value()

            def end_loop(self, rounds):
                assert self.n - self.start == self.per, (self.n - self.start, self.per)
                self.n, self.it = self.start + rounds * self.per, None
                self.last = self.own, self.n

        class Rounds:

            def __init__(self, it, job0, per_jobs, load0=0, per_loads=0, pe_done=pe_done, evacuated=evacuated, weights_in=weights_in):
                assert per_jobs % BANKS == 0 and per_loads % SLOTS == 0
                self.it, self.job0, self.per_jobs, self.load0, self.per_loads = it, job0, per_jobs, load0, per_loads
                self.pe_done, self.evacuated, self.weights_in = pe_done, evacuated, weights_in

            def bank(self, j):
                return bank(self.job0 + j)

            def done(self, j):
                return self.pe_done, self.it * self.per_jobs + (self.job0 + j + 1)

            def emptied(self, j):
                k = self.job0 + j
                return self.evacuated[k % BANKS], self.it * (self.per_jobs // BANKS) + (k // BANKS + 1)

            def slot(self, i, dims):
                return slot(self.load0 + i, dims)

            def arrived(self, i):
                n = self.load0 + i
                return self.weights_in[n % SLOTS], self.it * (16 * self.per_loads // SLOTS) + 16 * (n // SLOTS + 1)

        loads = []

        def load(src, dims, reader):
            loads.append((src, dims, reader))
            return len(loads) - 1

        def slot(n, dims):
            a, b = dims
            return ring[:, n % SLOTS, 0:a * b].rearrange("p (a b) -> p a b", a=a)

        def arrived(n):
            return weights_in[n % SLOTS], 16 * (n // SLOTS + 1)

        chunk_loads = {}

        def load_chunk(name, w, cols, reader, kc=KC):
            width = cols.stop - cols.start
            src = w.rearrange("(p c) n -> p c n", c=kc)
            pieces = []
            for c0 in range(0, kc, 4):
                c1 = min(c0 + 4, kc)
                pieces.append((load(src[:, c0:c1, cols], (c1 - c0, width), reader), c0, c1, width))
            chunk_loads[name] = pieces

        def wide(a, b):
            return slice(a, a + b)

        Z0, XBC0 = 0, D
        DT0 = XBC0 + D + 2 * GROUPS * STATE
        Q0 = DT0 + HEADS
        K0, V0 = Q0 + FOX_HEADS * FOX_D, Q0 + 2 * FOX_HEADS * FOX_D
        F0 = V0 + FOX_HEADS * FOX_D
        GS0 = F0 + FOX_HEADS
        GA0 = GS0 + D
        w_in = A["w_in"][0]
        w_mod, w_ada = A["w_mod"][0], A["w_ada_2"][0]

        def plan_unit(u):
            jobs(f"unit{u}", 1)
            load_unit(u)

        def load_unit(u):
            for n in range(2):
                load_chunk(f"unit{u}_{n}", (w_mod, w_ada)[u // 6], wide(u % 6 * D + n * BANK, BANK), job(f"unit{u}"))

        def plan_spread(*units):
            for u in units:
                jobs(f"mod{u}", 2)

        def plan_chunks(name, w, col0, n, units=()):
            for i in range(n):
                jobs(f"{name}_{i}", 2)
                load_chunk(f"{name}_{i}", w, wide(col0 + i * BANK, BANK), job(name, 2 * i + 1))
                if i < len(units):
                    plan_unit(units[i])

        LAG_T, LAG_PV = 2, 3

        def chunk_fills(name, w, col0, n):
            return [("chunk", name, i, half, w, col0) for i in range(n) for half in range(2)]

        def fill_span(f, fills, n):
            return f * n // len(fills), (f + 1) * n // len(fills)

        def plan_attention(name, n, fills):
            ends = {fill_span(f, fills, n)[1] - 1: fill for f, fill in enumerate(fills)}
            for i in range(n + LAG_PV):
                if i < n:
                    jobs(f"{name}_qk{i}", 1)
                if 0 <= i - LAG_T < n:
                    jobs(f"{name}_t{i - LAG_T}", 1)
                if 0 <= i - LAG_PV < n:
                    jobs(f"{name}_pv{i - LAG_PV}", 1)
                if i in ends and ends[i][0] == "unit":
                    jobs(f"unit{ends[i][1]}", 1)
                elif i in ends:
                    jobs("{1}_{2}_{3}".format(*ends[i]), 1)
            for fill in fills:
                if fill[0] == "unit":
                    load_unit(fill[1])
                elif fill[3] == 0:
                    _, nm, c, _, w, col0 = fill
                    load_chunk(f"{nm}_{c}", w, wide(col0 + c * BANK, BANK), job(nm, 2 * c + 1))

        BIAS_ROUNDS, BIAS_QUERIES = 4, 8
        IN_UNITS = (2, 3, 4, 5)
        jobs("vecT", 1)
        plan_unit(0)
        jobs("bias", BIAS_ROUNDS * BANKS)
        plan_unit(1)
        plan_spread(0, 1)
        jobs("hT", 4)
        plan_chunks("xbc", w_in, XBC0, 4, IN_UNITS)
        jobs("dtf", 1)
        for name, col0, n in (("q", Q0, 1), ("k", K0, 1), ("v", V0, 1), ("z", Z0, 2)):
            plan_chunks(name, w_in, col0, n)
        jobs("cumsum", 1)
        plan_spread(2, 3, 4)
        gs_fills = chunk_fills("gs", w_in, GS0, 2)

        def plan_gs(j):
            _, nm, c, half, w, col0 = gs_fills[j]
            jobs(f"{nm}_{c}_{half}", 1)

        jobs("xs_tok", 4)
        jobs("b_tok", 1)
        jobs("cb", TT)
        for k in range(3):
            jobs(f"a_row{k}", 1)
        jobs("state", 2)
        plan_gs(0)
        jobs("y_off", 2)
        for m in range(2 * TT):
            jobs(f"y_diag{m}", 1)
            for k in range(3 + 2 * m, min(5 + 2 * m, TT * GROUPS)):
                jobs(f"a_row{k}", 1)
            if m < 3:
                plan_gs(m + 1)
        for c in range(2):
            load_chunk(f"gs_{c}", w_in, wide(GS0 + c * BANK, BANK), job("gs", 2 * c + 1))
        FOX_UNITS = FOX_HEADS * TT
        ga_fills = chunk_fills("ga", w_in, GA0, 2)
        fox_fills = [("unit", 6), ga_fills[0], ("unit", 7), ga_fills[1], ("unit", 8), ga_fills[2], ("unit", 9), ga_fills[3], ("unit", 10), ("unit", 11)]
        plan_attention("fox", FOX_UNITS, fox_fills)
        jobs("yT", 4)
        jobs("oT", 2)
        jobs("merge", 8)
        for n in range(2):
            load_chunk(f"ssd_o_{n}", A["w_ssd_o"][0], wide(n * BANK, BANK), job("merge", 4 * n + 2))
            load_chunk(f"att_o_{n}", A["w_att_o"][0], wide(n * BANK, BANK), job("merge", 4 * n + 3), kc=4)
        jobs("mT", 4)
        plan_chunks("w_o", A["w_o"][0], 0, 2)
        plan_spread(5)
        jobs("h2T", 4)
        jobs("router", 1)
        plan_spread(6, 7)
        jobs("rank", 1)

        CAP, FF = 64, A["w_gate"].shape[-1]
        MOE_ROUNDS, MOE_JOBS, MOE_LOADS = QUADS, 24, 24
        MORE_ROUNDS = (S // CAP - 1) * QUADS
        more_sems = dict(pe_done=sem("more_pe_done"), evacuated=[sem(f"more_evacuated{b}") for b in range(BANKS)],
                         weights_in=[sem(f"more_weights_in{s}") for s in range(SLOTS)])
        overflow = sb("overflow", [P, 1], I32)

        def more_tokens(eng):
            eng.wait_ge(signal("overflow_known"), 1)
            return eng.If(eng.value_load(overflow[0:1, 0:1], min_val=0, max_val=1) > 0)

        MOE_XE, MOE_GW, MOE_GATE, MOE_UP, MOE_T, MOE_DOWN, MOE_SUM = 0, 4, (6, 8), (7, 9), (10, 13), (11, 14), (16, 20)
        jobs("moe", MOE_ROUNDS * MOE_JOBS)
        moe_load0 = len(loads)
        w_gate, w_up, w_down = A["w_gate"][0], A["w_up"][0], A["w_down"][0]
        moe_loads = []
        for p in range(2):
            for w, reader in ((w_gate, MOE_GATE[p]), (w_up, MOE_UP[p])):
                for c0 in (0, 4):
                    for i in range(2):
                        moe_loads.append((w.rearrange("e (p c) f -> e p c f", c=KC)[:, :, c0:c0 + 4, :], 2 * p + i, (4, FF), reader))
        for p in range(2):
            for c0 in (0, 2):
                for i in range(2):
                    moe_loads.append((w_down.rearrange("e (c p) n -> e p c n", p=P)[:, :, c0:c0 + 2, :], 2 * p + i, (2, D), MOE_DOWN[p] + 1))
        assert len(moe_loads) == MOE_LOADS
        loads.extend([None] * (MOE_ROUNDS * MOE_LOADS))

        w_in2 = A["w_in_2"][0]
        LAT = Q_RANK + KV_RANK + ROPE
        DIL0 = LAT
        GATE0 = DIL0 + DIL_GROUPS * 3 * DIL_HEADS * DIL_D
        jobs("h3T", 4)
        jobs("lat", 4)
        load_chunk("lat_0", w_in2, wide(0, BANK), job("lat", 1))
        load_chunk("lat_1", w_in2, wide(BANK, LAT - BANK), job("lat", 3))
        jobs("latT", 4)
        jobs("q_nope", 4)
        jobs("q_pe", 2)
        q_loads = [load(A["w_uq_2"][0].rearrange("(c p) n -> p c n", p=P)[:, :, wide(i * 384, 384)], (3, 384), job("q_pe", 1)) for i in range(4)]
        jobs("k_nope", 4)
        jobs("v_mla", 4)
        kv_loads = [load(A["w_ukv_2"][0].rearrange("(c p) n -> p c n", p=P)[:, :, wide(i * 1024, 1024)], (2, 1024), job("v_mla", 2 * i + 1)) for i in range(2)]
        jobs("q_peT", 2)
        MLA_UNITS = MLA_HEADS * TT
        DIL_UNITS = DIL_HEADS * TT

        def dil_col(g, i):
            return DIL0 + (3 * g + i) * DIL_HEADS * DIL_D

        def next_fills(g):
            if g == DIL_GROUPS:
                return chunk_fills("gates2", w_in2, GATE0, 4)
            return chunk_fills(f"dil_q{g}", w_in2, dil_col(g, 0), 2) + chunk_fills(f"dil_k{g}", w_in2, dil_col(g, 1), 2)

        plan_attention("mla", MLA_UNITS, next_fills(0))
        for g in range(DIL_GROUPS):
            plan_chunks(f"dil_v{g}", w_in2, dil_col(g, 2), 2)
            plan_attention(f"dil{g}_", DIL_UNITS, next_fills(g + 1))
        plan_spread(8, 9, 10)
        jobs("mixT", 4)
        plan_chunks("w_out", A["w_out_2"][0], 0, 2)
        plan_spread(11)
        jobs("h4T", 4)
        jobs("router2", 1)
        jobs("affT", 1)
        jobs("rank2", 1)

        CAP2, FF2 = 2 * S // E, A["w_gate_2"].shape[-1]
        assert CAP2 * 4 == P
        EC_ROUNDS, EC_JOBS, EC_LOADS = QUADS, 24, 96
        EC_XE, EC_GW, EC_GATE, EC_UP, EC_T, EC_DOWN, EC_SUM = 0, 4, (6, 12), (8, 14), (10, 16), 18, 20
        jobs("ec", EC_ROUNDS * EC_JOBS)
        ec_load0 = len(loads)
        w_gate2, w_up2, w_down2 = A["w_gate_2"][0], A["w_up_2"][0], A["w_down_2"][0]
        ec_loads, EC_PIECES = [], 0

        def plan_pieces(n, src_of, dims, last_job):
            nonlocal EC_PIECES
            for i in range(n):
                reader = last_job if i == n - 1 else ("piece", EC_PIECES)
                EC_PIECES += i < n - 1
                ec_loads.extend((src_of(i), e, dims, reader) for e in range(4))

        for fp in range(2):
            for w, last_job in ((w_gate2, EC_GATE[fp] + 1), (w_up2, EC_UP[fp] + 1)):
                rows_first = w.rearrange("e (p c) f -> e p c f", c=KC)[:, :, :, wide(fp * 1024, 1024)]
                plan_pieces(KC // 2, lambda i: rows_first[:, :, 2 * i:2 * i + 2, :], (2, 1024), last_job)
        chunks_first = w_down2.rearrange("e (c p) n -> e p c n", p=P)
        plan_pieces(FF2 // P // 2, lambda i: chunks_first[:, :, 2 * i:2 * i + 2, :], (2, D), EC_DOWN + 1)
        assert len(ec_loads) == EC_LOADS
        loads.extend([None] * (EC_ROUNDS * EC_LOADS))

        pieces_used = sem("pieces_used")

        block = ctx.enter_context(nc.Block())

        @block.sync
        def _(sp):
            def fetch_rounds(rounds, todo, job0, per_jobs, load0, pe_done=pe_done, weights_in=weights_in, free=None):
                per = len(todo)

                def place(i):
                    return (load0 + i) % SLOTS

                def fetch_expert(i, quad, used):
                    which, used = used
                    src, e, dims, _ = todo[i % per]
                    if not isinstance(quad, int):
                        used = sp.lower_val(sp.snap(used))
                    sp.dma_start(slot(place(i), dims), src[quad * 4 + e]).wait_op(which, used, "sem-ge").then_inc(weights_in[place(i)], 16)

                def used(i, it):
                    reader = todo[i - SLOTS][3]
                    if isinstance(reader, tuple):
                        return pieces_used, it * EC_PIECES + (reader[1] + 1)
                    return pe_done, it * per_jobs + (job0 + reader + 1)

                for i in range(SLOTS):
                    fetch_expert(i, 0, free or done(prior_reader(load0 + i - SLOTS)))
                with sp.Fori(0, rounds - 1) as it:
                    for i in range(SLOTS, per):
                        fetch_expert(i, quad_of(it), used(i, it))
                    for i in range(per, per + SLOTS):
                        fetch_expert(i, quad_of(it + 1), used(i, it))
                for i in range(SLOTS, per):
                    fetch_expert(i, (rounds - 1) % QUADS, used(i, rounds - 1))

            def quad_of(it):
                return it & (QUADS - 1)

            def prior_reader(n):
                if n < moe_load0:
                    return loads[n][2]
                if n < moe_load0 + MOE_ROUNDS * MOE_LOADS:
                    r, i = divmod(n - moe_load0, MOE_LOADS)
                    return job("moe") + r * MOE_JOBS + moe_loads[i][3]
                return loads[n][2]

            def fetch_run(first, end):
                for n in range(first, end):
                    src, dims, _ = loads[n]
                    if n >= SLOTS:
                        sp.wait_ge(*done(prior_reader(n - SLOTS)))
                    sp.dma_start(slot(n, dims), src).then_inc(weights_in[n % SLOTS], 16)

            fetch_run(0, moe_load0)
            fetch_rounds(MOE_ROUNDS, moe_loads, job("moe"), MOE_JOBS, moe_load0)
            with more_tokens(sp):
                fetch_rounds(MORE_ROUNDS, moe_loads, 0, MOE_JOBS, 0, more_sems["pe_done"], more_sems["weights_in"],
                             done(job("moe", MOE_ROUNDS * MOE_JOBS - 1)))
                sp.wait_ge(more_sems["pe_done"], MORE_ROUNDS * MOE_JOBS)
            fetch_run(moe_load0 + MOE_ROUNDS * MOE_LOADS, ec_load0)
            fetch_rounds(EC_ROUNDS, ec_loads, job("ec"), EC_JOBS, ec_load0)
            for t in range(TT):
                sp.wait_ge(signal("out_ready"), t + 1)
                sp.dma_start(out[0, wide(t * P, P), :], h[:, t, :]).then_inc(signal("out_stored"), 16)
            sp.wait_ge(signal("out_stored"), 16 * TT)

        one_hot = [view(i * BIAS_QUERIES * S, BIAS_QUERIES, S) for i in range(2)]
        staged = [view(at, BIAS_QUERIES * S) for at in (4096, 14384)]
        pos_rows = junk[:, 512:512 + S + S // 4].bitcast(I32)
        pos_all, pos_quarter = junk[:, 0:S], junk[:, S:S + S // 4]
        bias_dram = nc.dram_tensor("bias_dram", [DIL_GROUPS * DIL_HEADS, S, S], F32, kind="Internal").ap()
        BIAS_STORES = 16 * 4
        bias_stored = [sem(f"bias_stored{i}") for i in range(2)]
        bias_in = [sem(f"bias_in{i}") for i in range(4)]
        mla_unit0, dil_unit0 = FOX_UNITS, FOX_UNITS + MLA_UNITS

        lat = view(0, TT, LAT)
        c_qT, c_kvT = view(1408, 3, S), view(2176, 2, S)
        q_nopeT, k_nopeT = view(2688, MLA_HEADS, S), view(4736, MLA_HEADS, S)
        v_mla = view(6784, TT, MLA_HEADS * NOPE)
        q_pe = view(8832, TT, MLA_HEADS * ROPE)
        k_pe = view(9856, TT, 2 * ROPE)
        q_peT, k_peT = view(10112, MLA_HEADS // 2, S), view(11136, S)
        rope_tmp = view(11392, 2, MLA_HEADS * ROPE // 2)
        o_mla = h
        q_dilT = [view(at, DIL_HEADS, S) for at in (15872, 0, 15872)]
        k_dilT = [mod[:, 0:2, :].rearrange("p a d -> p (a d)").rearrange("p (h s) -> p h s", h=DIL_HEADS), view(2048, DIL_HEADS, S)]
        k_dilT.append(k_dilT[0])
        v_dil = view(4096, TT, DIL_HEADS * DIL_D)
        o_dil = [view(6144 + 2048 * g, TT, D) for g in range(DIL_GROUPS)]
        bias_tile = view(12288, 4, TT * S)
        dil_w = table[:, 0:DIL_GROUPS * TT * DIL_HEADS].rearrange("p (g u) -> p g u", g=DIL_GROUPS)
        bands = view(14336, DIL_GROUPS, TT * S)
        sig_ab = view(0, 2 * TT * D)
        sig_a, sig_b = view(0, TT, D), view(2048, TT, D)

        pick, pick_gate = view(0, TT, 4 * 64), view(512, TT, 4 * 64)
        gate_T = view(1024, 2, S)
        x_e = view(1536, KC, 4 * 64)
        silu_g, hid = view(3584, 2, BANK), view(4608, 2, BANK)
        hidT = view(5632, 16, P)
        y_e = view(7680, 2, D)
        y_sum = view(9728, TT, D)

        @block.gpsimd
        def _(pool):
            pool.wait_ge(signal("zeros_ready"), 1)
            for b, name in enumerate(("b_mod", "b_ada_2")):
                halves = A[name][0].rearrange("(u n k) -> n u k", n=2, k=BANK)
                for n in range(2):
                    pool.dma_start(mod_rows[wide(64 * n + 6 * b, 6), :], halves[n]).then_inc(signal("mod_bias_in"), 16)
            with nc.allow_non_contiguous_dma(reason="256 numbers"):
                pool.dma_start(pos_i[:], A["positions_2"][0].rearrange("(t p) -> p t", p=P)).then_inc(signal("pos_tok_in"), 16)
            pool.dma_start(rows[0:64, :], A["conv_w"][0].rearrange("j (t p) -> (j t) p", p=P)).then_inc(signal("rows_in"), 16)
            pool.dma_start(rows[64:80, :], A["conv_b"][0].rearrange("(t p) -> t p", p=P)).then_inc(signal("rows_in"), 16)
            pool.dma_start(rows[80:83, :], A["g_q_lat_2"][0].rearrange("(t p) -> t p", p=P)).then_inc(signal("rows_in"), 16)
            pool.dma_start(rows[83:85, :], A["g_kv_lat_2"][0].rearrange("(t p) -> t p", p=P)).then_inc(signal("rows_in"), 16)
            with nc.allow_non_contiguous_dma(reason="24 columns"):
                pool.dma_start(small_w[:, :, 0:HEADS], w_in.rearrange("(p c) n -> p c n", c=KC)[:, :, wide(DT0, HEADS)]).then_inc(signal("dtf_in"), 16)
                pool.dma_start(small_w[:, :, HEADS:24], w_in.rearrange("(p c) n -> p c n", c=KC)[:, :, wide(F0, FOX_HEADS)]).then_inc(signal("dtf_in"), 16)
            pool.dma_start(small_b[:, 0:HEADS], A["dt_bias"]).then_inc(signal("dtf_in"), 16)
            pool.dma_start(small_b[:, HEADS:24], A["forget_b"]).then_inc(signal("dtf_in"), 16)
            pool.dma_start(head_v[:, 0, :], A["a_log"].to_broadcast([P, HEADS])).then_inc(signal("head_in"), 16)
            pool.dma_start(head_v[:, 1, :], A["d_skip"].to_broadcast([P, HEADS])).then_inc(signal("head_in"), 16)
            pool.dma_start(ssd_w[:], A["ssd_norm_w"][0].rearrange("(p c) -> p c", c=KC)).then_inc(signal("ssd_w_in"), 16)

            with pool.Fori(0, BIAS_ROUNDS) as it:
                R = Rounds(it, job("bias"), BANKS)
                for half in range(2):
                    for j in range(4):
                        pool.wait_ge(*R.emptied(4 * half + j))
                    for q in range(4):
                        queries = bass.ds(it * (2 * BIAS_QUERIES) + (q * (S // 4) + half * BIAS_QUERIES), BIAS_QUERIES)
                        pool.dma_start(bias_dram[:, queries, :], staged[half][wide(q * 32, DIL_GROUPS * DIL_HEADS), :].rearrange("p (q s) -> p q s", s=S)).then_inc(bias_stored[half], 16)

            pool.wait_ge(signal("y_ssd_ready"), 2)
            pool.dma_start(params[:, 0, :], A["ln1_g"].to_broadcast([P, D])).then_inc(signal("params_in"), 16)
            pool.dma_start(params[:, 1, :], A["ln1_b"].to_broadcast([P, D])).then_inc(signal("params_in"), 16)
            with nc.allow_non_contiguous_dma(reason="20 columns"):
                pool.dma_start(small_w[:, :, 0:4], A["w_router_group"][0].rearrange("(p c) n -> p c n", c=KC)).then_inc(signal("router_in"), 16)
                pool.dma_start(small_w[:, :, 4:20], A["w_router_expert"][0].rearrange("(p c) n -> p c n", c=KC)).then_inc(signal("router_in"), 16)
            pool.dma_start(small_b[:, 0:4], A["b_router_group"]).then_inc(signal("router_in"), 16)
            pool.dma_start(small_b[:, 4:20], A["b_router_expert"]).then_inc(signal("router_in"), 16)

            def two_rows(ready, value, first, second):
                pool.wait_ge(signal(ready), value)
                for i, name in enumerate((first, second)):
                    row = A[name] if len(A[name].shape) == 2 else A[name].unsqueeze(0)
                    pool.dma_start(params[:, i, :], row.to_broadcast([P, D])).then_inc(signal("params_in"), 16)

            two_rows("x_mid_ready", 1, "ln2_g", "ln2_b")
            two_rows("x_b1_ready", 1, "g_norm_mix_2", "g_norm_ffn_2")
            pool.dma_start(bands[:], A["bands"].rearrange("p g t s -> p g (t s)")).then_inc(signal("bands_in"), 16)
            for half in range(2):
                pool.wait_ge(bias_stored[half], BIAS_ROUNDS * BIAS_STORES)
            pool.wait_ge(signal("bands_in"), 16)

            def mask_bias(n):
                pool.wait_ge(bias_in[n % 4], 16 * (n // 4 + 1))
                nc.gpsimd.tensor_tensor(bias_tile[:, n % 4, :], bias_tile[:, n % 4, :], bands[:, n // DIL_HEADS, :], ALU.add).then_inc(signal("bias_masked"), 1)

            for n in range(DIL_GROUPS * DIL_HEADS):
                if n >= 4:
                    pool.wait_ge(signal("max_ready"), dil_unit0 + (n - 3) * TT)
                pool.dma_start(bias_tile[:, n % 4, :].rearrange("p (t s) -> p t s", t=TT), bias_dram[n].rearrange("(t p) s -> p t s", p=P)).then_inc(bias_in[n % 4], 16)
                if n:
                    mask_bias(n - 1)
            mask_bias(DIL_GROUPS * DIL_HEADS - 1)
            with nc.allow_non_contiguous_dma(reason="16 columns"):
                pool.dma_start(small_w[:, :, 0:E], A["w_router_2"][0].rearrange("(p c) n -> p c n", c=KC)).then_inc(signal("router2_in"), 16)
            two_rows("h4_ready", TT, "g_final_2", "g_final_2")

        silu_z, sig_gs, sig_ga = view(0, TT, D), view(2048, TT, D), view(4096, TT, D)
        sig_both = view(2048, 2 * TT * D)
        u_pad = view(6144, 16, S + 3)
        xcT = view(10288, 16, S)
        qT, kT, v_tok = view(14384, 4, S), view(15408, 4, S), view(16432, TT, 512)
        b_tok = view(17456, GROUPS, STATE)
        xs_tok, xdt = view(6144, TT, D), view(8192, TT, D)
        x_end, prev = view(10288, D), view(11312, D)
        o_fox = view(10288, TT, 512)
        cb = junk[:].rearrange("p (t g l) -> p t g l", t=TT, g=GROUPS)
        decay = [prob[:, 0:2, :].rearrange("p a b -> p (a b)"), prob[:, 2:4, :].rearrange("p a b -> p (a b)"),
                 probT[:, 0:2, :].rearrange("p a b -> p (a b)")]
        y_tok = h
        dtf = sb("dtf", [P, TT, 24])
        dtf_e = sb("dtf_e", [P, TT, 24])
        cum_in = sb("cum_in", [P, TT, 24])
        a_cs = sb("a_cs", [P, TT, HEADS])
        neg_F = sb("neg_F", [P, TT, FOX_HEADS])
        a_exp = sb("a_exp", [P, 2, HEADS])

        ATT_BUF = 4
        oT = view(14384, 4, S)
        silu_junk = junk
        mv2 = sb("mv2", [P, TT, 2])
        posf = sb("posf", [P, TT])
        dil_top = sb("dil_top", [P, DIL_UNITS])
        pass_shift = sb("pass_shift", [P, QUADS])
        chosen = sb("chosen", [P, TT, E])
        gates = sb("gates", [P, TT, E])
        rank = sb("rank", [P, TT, E])
        logits, in_group = sb("logits", [P, TT, 20]), sb("in_group", [P, TT, E])
        hot_g, hot1, hot2, e_in = sb("hot_g", [P, TT, 4]), sb("hot1", [P, TT, 4]), sb("hot2", [P, TT, 4]), sb("e_in", [P, TT, 4])
        route_g, route_2, route_top = sb("route_g", [P, TT, 4]), sb("route_2", [P, TT]), sb("route_top", [P, TT])
        top1, top2 = sb("top1", [P, TT]), sb("top2", [P, TT])

        @block.tensor
        def _(pe):
            next_job = [0]

            def begin(k):
                assert k == next_job[0], (k, next_job[0], [n for n, v in first_job.items() if v <= k][-1])
                next_job[0] += 1
                if k >= BANKS:
                    pe.wait_ge(*emptied(k - BANKS))
                return bank(k)

            def end(mm):
                mm.then_inc(pe_done, 1)

            def claim(k):
                assert next_job[0] <= k < next_job[0] + BANKS
                if k >= BANKS:
                    pe.wait_ge(*emptied(k - BANKS))
                return bank(k)

            def finish(k, mm):
                assert k == next_job[0]
                next_job[0] += 1
                end(mm)

            def in_one(steps):
                for _ in steps:
                    pass

            def pieces(name):
                for n, c0, c1, width in chunk_loads[name]:
                    pe.wait_ge(*arrived(n))
                    for c in range(c0, c1):
                        yield c, slot(n, (c1 - c0, width))[:, c - c0, :]

            def chunks(name):
                return [(c, slot(n, (c1 - c0, width))[:, c - c0, :]) for n, c0, c1, width in chunk_loads[name] for c in range(c0, c1)]

            units_done = []

            def modulation(u):
                k = job(f"unit{u}")
                pe.wait_ge(signal("cond_ready"), 1)
                o = claim(k)
                weights = [dict(pieces(f"unit{u}_{n}")) for n in range(2)]
                for c in range(KC // 2):
                    for n in range(2):
                        for half in range(2):
                            mm = pe.matmul(o[wide(64 * n + 32 * half, 32), :], cond[:, u // 6, half * (KC // 2) + c, 31 - u:63 - u], weights[n][half * (KC // 2) + c],
                                           start=(c == 0), stop=(c == KC // 2 - 1))
                            if c < KC // 2 - 1 or n == 0 or half == 0:
                                yield
                units_done.append(u)
                finish(k, mm)

            def spread(*units):
                for u in units:
                    pe.wait_ge(*emptied(job(f"unit{units_done[-1]}")))
                    for n in range(2):
                        o = begin(job(f"mod{u}", n))
                        end(pe.matmul(o, select[:, n * 16 + u:n * 16 + u + 1].to_broadcast([P, P]), mod_rows[:], start=True, stop=True))

            def transpose_tokens(name, src):
                for t in range(TT):
                    for c0 in range(0, KC, 4):
                        o = begin(job(name, t * 2 + c0 // 4))
                        for c in range(c0, c0 + 4):
                            mm = pe.transpose(o[:, wide((c - c0) * P, P)], src[:, t, c::KC], ident)
                        end(mm)

            def channel_job(name, i, half, actT):
                k = job(name, 2 * i + half)
                o = claim(k)
                for j in range(2):
                    ch = wide((2 * half + j) * P, P)
                    for c, w in pieces(f"{name}_{i}") if half == j == 0 else chunks(f"{name}_{i}"):
                        mm = pe.matmul(o[:, wide(j * S, S)], w[:, ch], actT[:, c, :], start=(c == 0), stop=(c == KC - 1))
                        if j == 0 or c < KC - 1:
                            yield
                finish(k, mm)

            def token_job(name, i, t, actT):
                k = job(name, 2 * i + t)
                o = claim(k)
                for c, w in pieces(f"{name}_{i}") if t == 0 else chunks(f"{name}_{i}"):
                    mm = pe.matmul(o, actT[:, c, wide(t * P, P)], w, start=(c == 0), stop=(c == KC - 1))
                    if c < KC - 1:
                        yield
                finish(k, mm)

            def channel_major(name, n, actT, units=()):
                for i in range(n):
                    for half in range(2):
                        in_one(channel_job(name, i, half, actT))
                    if i < len(units):
                        in_one(modulation(units[i]))

            def token_major(name, n, actT):
                for i in range(n):
                    for t in range(TT):
                        in_one(token_job(name, i, t, actT))

            def fill_job(fill):
                if fill[0] == "unit":
                    return modulation(fill[1]), 2 * KC
                _, name, i, half, _, _ = fill
                if name.startswith("dil"):
                    return channel_job(name, i, half, hT), 2 * KC
                return token_job(name, i, half, hT), KC

            def attention(name, n, unit0, scores, values, keys, fills):
                shares = {}
                for f, fill in enumerate(fills):
                    first, end_ = fill_span(f, fills, n)
                    steps, count = fill_job(fill)
                    parts = 3 * (end_ - first)
                    for part in range(parts):
                        shares[3 * first + part] = steps, count * (part + 1) // parts - count * part // parts

                def share(part):
                    steps, count = shares.get(part, ((), 0))
                    for _ in range(count):
                        next(steps, None)

                for i in range(n + LAG_PV):
                    if i < n:
                        o = begin(job(f"{name}_qk{i}"))
                        end(scores(o, i))
                    share(3 * i)
                    if 0 <= (j := i - LAG_T) < n:
                        o = begin(job(f"{name}_t{j}"))
                        pe.wait_ge(signal("probs_ready"), unit0 + j + 1)
                        for t in range(keys(j)):
                            mm = pe.transpose(o[:, wide(t * P, P)], prob[:, (unit0 + j) % ATT_BUF, wide(t * P, P)], ident)
                        end(mm)
                    share(3 * i + 1)
                    if 0 <= (j := i - LAG_PV) < n:
                        o = begin(job(f"{name}_pv{j}"))
                        pe.wait_ge(*emptied(job(f"{name}_t{j}")))
                        end(values(o, j))
                    share(3 * i + 2)

            pe.wait_ge(signal("const_in"), 16)
            pe.wait_ge(signal("rows_in"), 64)
            o = begin(job("vecT"))
            end(pe.transpose(o[:, 0:85], rows[0:85, :], ident[0:85, 0:85]))
            in_one(modulation(0))

            def bias_round(it):
                R = Rounds(it, job("bias"), BANKS)
                for j in range(BANKS):
                    k = job("bias", j)
                    if j % 4 == 0:
                        pe.wait_ge(signal("one_hot_ready"), it * 2 + (j // 4 + 1))
                    if not isinstance(it, int) or k >= BANKS:
                        pe.wait_ge(evacuated[k % BANKS], it + k // BANKS)
                    end(pe.matmul(R.bank(j), table[:], one_hot[j // 4][:, wide(j % 4 * 2, 2), :], start=True, stop=True))

            pe.wait_ge(signal("table_in"), 64)
            bias_round(0)
            with pe.Fori(1, BIAS_ROUNDS) as it:
                bias_round(it)
            next_job[0] += BIAS_ROUNDS * BANKS

            in_one(modulation(1))
            spread(0, 1)

            pe.wait_ge(signal("h_ready"), TT)
            transpose_tokens("hT", h)

            for k in range(4):
                pe.wait_ge(*emptied(job("hT", k)))
            channel_major("xbc", 4, hT, IN_UNITS)
            pe.wait_ge(signal("dtf_in"), 64)
            o = begin(job("dtf"))
            for t in range(TT):
                pe.matmul(o[:, wide(t * 24, 24)], ones_row, small_b[0:1, :], start=True, stop=False)
                for c in range(KC):
                    mm = pe.matmul(o[:, wide(t * 24, 24)], hT[:, c, wide(t * P, P)], small_w[:, c, :], start=False, stop=(c == KC - 1))
            end(mm)
            channel_major("q", 1, hT)
            channel_major("k", 1, hT)
            token_major("v", 1, hT)
            token_major("z", 2, hT)

            pe.wait_ge(signal("cum_in_ready"), 1)
            o = begin(job("cumsum"))
            pe.matmul(o[:, 0:24], tri, cum_in[:, 0, :], start=True, stop=True)
            pe.matmul(o[:, 32:48], tri, cum_in[:, 1, 0:HEADS], start=True, stop=True)
            pe.matmul(o[:, 64:72], tri, cum_in[:, 1, HEADS:24], start=True, stop=False)
            pe.matmul(o[:, 64:72], ones, cum_in[:, 0, HEADS:24], start=False, stop=True)
            end(pe.matmul(o[:, 96:112], ones, cum_in[:, 0, 0:HEADS], start=True, stop=True))
            spread(2, 3, 4)

            pe.wait_ge(signal("conv_ready"), 16)
            for t in range(TT):
                for c0 in range(0, KC, 4):
                    o = begin(job("xs_tok", 2 * t + c0 // 4))
                    for c in range(c0, c0 + 4):
                        mm = pe.transpose(o[:, wide((c - c0) * P, P)], xcT[:, c, wide(t * P, P)], ident)
                    end(mm)
            o = begin(job("b_tok"))
            for g in range(GROUPS):
                mm = pe.transpose(o[:, wide(g * P, P)], xcT[:, KC + g, 0:P], ident)
            end(mm)
            for t in range(TT):
                o = begin(job("cb", t))
                for g in range(GROUPS):
                    mm = pe.matmul(o[:, wide(g * P, P)], xcT[:, KC + g, wide(t * P, P)], xcT[:, KC + GROUPS + g, wide(t * P, P)], start=True, stop=True)
                end(mm)
            def a_row(k):
                t, g = divmod(k, GROUPS)
                o = begin(job(f"a_row{k}"))
                for r in range(PER_GROUP):
                    hd = g * PER_GROUP + r
                    mm = pe.matmul(o[:, wide(r * P, P)], cum_in[:, t, hd:hd + 1].to_broadcast([P, P]), tri, start=True, stop=True)
                end(mm)

            for k in range(3):
                a_row(k)
            pe.wait_ge(signal("x_end_ready"), 1)
            pe.wait_ge(*emptied(job("b_tok")))
            for half in range(2):
                o = begin(job("state", half))
                for g in (2 * half, 2 * half + 1):
                    mm = pe.matmul(o[:, wide((g % 2) * S, S)], b_tok[:, g, :], x_end[:, wide(g * S, S)], start=True, stop=True)
                end(mm)
            in_one(fill_job(gs_fills[0])[0])
            for half in range(2):
                o = begin(job("y_off", half))
                pe.wait_ge(*emptied(job("state", half)))
                for g in (2 * half, 2 * half + 1):
                    mm = pe.matmul(o[:, wide((g % 2) * S, S)], xcT[:, KC + GROUPS + g, P:S], prev[:, wide(g * S, S)], start=True, stop=True)
                end(mm)
            for m in range(2 * TT):
                t, half = divmod(m, 2)
                o = begin(job(f"y_diag{m}"))
                for k in (2 * m, 2 * m + 1):
                    pe.wait_ge(signal("decay_ready"), k + 1)
                    for r in range(PER_GROUP):
                        hd = (k % GROUPS) * PER_GROUP + r
                        mm = pe.matmul(o[:, wide((hd % 8) * HD, HD)], decay[k % 3][:, wide(r * P, P)], xdt[:, t, wide(hd * HD, HD)], start=True, stop=True)
                end(mm)
                for k in range(3 + 2 * m, min(5 + 2 * m, TT * GROUPS)):
                    a_row(k)
                if m < 3:
                    in_one(fill_job(gs_fills[m + 1])[0])

            def fox_scores(o, i):
                hd, t = divmod(i, TT)
                part, n = wide((hd % 2) * HD, HD), (t + 1) * P
                if i == 0:
                    for nm in ("q", "k"):
                        for j in range(2):
                            pe.wait_ge(*emptied(job(nm, j)))
                pe.matmul(o[:, 0:n], qT[part, hd // 2, wide(t * P, P)], kT[part, hd // 2, 0:n], start=True, stop=False)
                for s in range(t + 1):
                    lhs = cum_in[:, s, HEADS + hd:HEADS + hd + 1].to_broadcast([P, P])
                    mm = pe.matmul(o[:, s * P:(s + 1) * P], lhs, tri, start=False, stop=(s == t))
                    if s < t:
                        mm = pe.matmul(o[:, P:2 * P], lhs, ones, start=False, stop=False)
                return mm

            def fox_values(o, i):
                hd, t = divmod(i, TT)
                if i == 0:
                    for j in range(2):
                        pe.wait_ge(*emptied(job("v", j)))
                for s in range(t + 1):
                    mm = pe.matmul(o[:, 0:FOX_D], probT[:, i % ATT_BUF, wide(s * P, P)], v_tok[:, s, wide(hd * FOX_D, FOX_D)], start=(s == 0), stop=(s == t))
                return mm

            attention("fox", FOX_UNITS, 0, fox_scores, fox_values, lambda i: i % TT + 1, fox_fills)

            pe.wait_ge(signal("y_ssd_ready"), 2)
            transpose_tokens("yT", y_tok)
            for t in range(TT):
                o = begin(job("oT", t))
                for i in range(t, FOX_UNITS, TT):
                    pe.wait_ge(*emptied(job(f"fox_pv{i}")))
                for c in range(4):
                    mm = pe.transpose(o[:, wide(c * P, P)], o_fox[:, t, c::4], ident)
                end(mm)
            for k in range(4):
                pe.wait_ge(*emptied(job("yT", k)))
            for k in range(2):
                pe.wait_ge(*emptied(job("oT", k)))
            for n in range(2):
                for t in range(TT):
                    o = begin(job("merge", 4 * n + 2 * t))
                    for c, w in pieces(f"ssd_o_{n}"):
                        mm = pe.matmul(o, hT[:, c, wide(t * P, P)], w, start=(c == 0), stop=(c == KC - 1))
                    end(mm)
                    o = begin(job("merge", 4 * n + 2 * t + 1))
                    for c, w in pieces(f"att_o_{n}"):
                        mm = pe.matmul(o, oT[:, c, wide(t * P, P)], w, start=(c == 0), stop=(c == 3))
                    end(mm)
            pe.wait_ge(signal("merged_ready"), 4)
            transpose_tokens("mT", h)
            for k in range(4):
                pe.wait_ge(*emptied(job("mT", k)))
            token_major("w_o", 2, hT)
            pe.wait_ge(signal("x_mid_ready"), 1)
            spread(5)
            pe.wait_ge(signal("h2_ready"), TT)
            transpose_tokens("h2T", h)
            for k in range(4):
                pe.wait_ge(*emptied(job("h2T", k)))
            pe.wait_ge(signal("router_in"), 64)
            o = begin(job("router"))
            for t in range(TT):
                pe.matmul(o[:, wide(t * 20, 20)], ones_row, small_b[0:1, 0:20], start=True, stop=False)
                for c in range(KC):
                    mm = pe.matmul(o[:, wide(t * 20, 20)], hT[:, c, wide(t * P, P)], small_w[:, c, 0:20], start=False, stop=(c == KC - 1))
            end(mm)
            spread(6, 7)
            pe.wait_ge(signal("chosen_ready"), 1)
            o = begin(job("rank"))
            pe.matmul(o[:, 0:E], tri, chosen[:, 0, :], start=True, stop=True)
            pe.matmul(o[:, E:2 * E], tri, chosen[:, 1, :], start=True, stop=False)
            pe.matmul(o[:, E:2 * E], ones, chosen[:, 0, :], start=False, stop=True)
            pe.matmul(o[:, 2 * E:3 * E], ones, chosen[:, 0, :], start=True, stop=False)
            end(pe.matmul(o[:, 2 * E:3 * E], ones, chosen[:, 1, :], start=False, stop=True))

            def ffn_products(o, lhs, w, parts, width, start, stop):
                for (i, ws) in enumerate(w):
                    mm = pe.matmul(o[wide(parts[i] * width, width), :], lhs(i), ws, start=start, stop=stop)
                return mm

            def loop_begin(R, j):
                k = R.job0 + j
                if k >= BANKS:
                    pe.wait_ge(R.evacuated[k % BANKS], R.it * (R.per_jobs // BANKS) + k // BANKS)
                return R.bank(j)

            assert next_job[0] == job("moe")
            def moe_round(R, picked):
                pe.wait_ge(picked, R.it + 1)
                for j in range(4):
                    o = loop_begin(R, MOE_XE + j)
                    for c in (2 * j, 2 * j + 1):
                        for t in range(TT):
                            mm = pe.matmul(o[:, wide((c % 2) * S, S)], h[:, t, c::KC], pick[:, t, :], start=(t == 0), stop=(t == TT - 1))
                    mm.then_inc(R.pe_done, 1)
                for p in range(2):
                    o = loop_begin(R, MOE_GW + p)
                    for t in range(TT):
                        mm = pe.transpose(o[:, wide(t * P, P)], pick_gate[:, t, wide(p * P, P)], ident)
                    mm.then_inc(R.pe_done, 1)
                for j in range(4):
                    pe.wait_ge(*R.emptied(MOE_XE + j))
                for p in range(2):
                    for what, j in ((0, MOE_GATE[p]), (1, MOE_UP[p])):
                        o = loop_begin(R, j)
                        for half in range(2):
                            n = 8 * p + 4 * what + 2 * half
                            for i in range(2):
                                pe.wait_ge(*R.arrived(n + i))
                            for c in range(4):
                                for i in range(2):
                                    mm = pe.matmul(o[wide(i * CAP, CAP), :], x_e[:, 4 * half + c, wide((2 * p + i) * CAP, CAP)],
                                                   R.slot(n + i, (4, FF))[:, c, :], start=(half == c == 0), stop=(half == 1 and c == 3))
                        mm.then_inc(R.pe_done, 1)
                for p in range(2):
                    o = loop_begin(R, MOE_T[p])
                    pe.wait_ge(*R.emptied(MOE_UP[p]))
                    for c in range(4):
                        mm = pe.transpose(o[:, wide(c * P, P)], hid[:, p, wide(c * P, P)], ident)
                    mm.then_inc(R.pe_done, 1)
                    out2 = [loop_begin(R, MOE_DOWN[p] + n) for n in range(2)]
                    pe.wait_ge(*R.emptied(MOE_T[p]))
                    for half in range(2):
                        l = 16 + 4 * p + 2 * half
                        for i in range(2):
                            pe.wait_ge(*R.arrived(l + i))
                        for c in range(2):
                            for n in range(2):
                                for i in range(2):
                                    mm = pe.matmul(out2[n][wide(i * CAP, CAP), :], hidT[:, 4 * p + 2 * half + c, wide(i * CAP, CAP)],
                                                   R.slot(l + i, (2, D))[:, c, wide(n * BANK, BANK)], start=(half == c == 0), stop=(half == c == 1))
                                if half == c == 1:
                                    mm.then_inc(R.pe_done, 1)
                for p in range(2):
                    for n in range(2):
                        pe.wait_ge(*R.emptied(MOE_DOWN[p] + n))
                    for n in range(2):
                        for t in range(TT):
                            o = loop_begin(R, MOE_SUM[p] + 2 * n + t)
                            pe.matmul(o, gate_T[:, p, wide(t * P, P)], y_e[:, p, wide(n * BANK, BANK)], start=True, stop=True).then_inc(R.pe_done, 1)

            with pe.Fori(0, MOE_ROUNDS) as it:
                moe_round(Rounds(it, job("moe"), MOE_JOBS, moe_load0, MOE_LOADS), signal("pick_ready"))
            with more_tokens(pe):
                with pe.Fori(0, MORE_ROUNDS) as it:
                    moe_round(Rounds(it, 0, MOE_JOBS, 0, MOE_LOADS, **more_sems), signal("more_pick_ready"))
            next_job[0] += MOE_ROUNDS * MOE_JOBS

            pe.wait_ge(signal("h3_ready"), TT)
            transpose_tokens("h3T", h)
            for k in range(4):
                pe.wait_ge(*emptied(job("h3T", k)))
            for i in range(2):
                for t in range(TT):
                    o = begin(job("lat", 2 * i + t))
                    for c, w in pieces(f"lat_{i}") if t == 0 else chunks(f"lat_{i}"):
                        mm = pe.matmul(o[:, 0:w.shape[-1]], hT[:, c, wide(t * P, P)], w, start=(c == 0), stop=(c == KC - 1))
                    end(mm)
            pe.wait_ge(signal("lat_ready"), 1)
            for t in range(TT):
                o = begin(job("latT", 2 * t))
                for c in range(3):
                    mm = pe.transpose(o[:, wide(c * P, P)], lat[:, t, wide(c * P, P)], ident)
                end(mm)
                o = begin(job("latT", 2 * t + 1))
                for c in range(2):
                    mm = pe.transpose(o[:, wide(c * P, P)], lat[:, t, wide(Q_RANK + c * P, P)], ident)
                end(pe.transpose(o[:, 2 * P:3 * P], k_pe[:, t, :], ident))
            for k in range(4):
                pe.wait_ge(*emptied(job("latT", k)))
            for i, n in enumerate(q_loads):
                pe.wait_ge(*arrived(n))
                o = begin(job("q_nope", i))
                for j in range(2):
                    for c in range(3):
                        mm = pe.matmul(o[:, wide(j * S, S)], slot(n, (3, 384))[:, c, wide(j * (NOPE + ROPE), NOPE)], c_qT[:, c, :], start=(c == 0), stop=(c == 2))
                end(mm)
            for t in range(TT):
                o = begin(job("q_pe", t))
                for i, n in enumerate(q_loads):
                    for c in range(3):
                        w = slot(n, (3, 384))[:, c, :].rearrange("p (h d) -> p h d", h=2)[:, :, NOPE:NOPE + ROPE]
                        mm = pe.matmul(o[:, wide(i * P, P)], c_qT[:, c, wide(t * P, P)], w, start=(c == 0), stop=(c == 2))
                end(mm)
            for i, n in enumerate(kv_loads):
                pe.wait_ge(*arrived(n))
                for half in range(2):
                    o = begin(job("k_nope", 2 * i + half))
                    for j in range(2):
                        for c in range(2):
                            mm = pe.matmul(o[:, wide(j * S, S)], slot(n, (2, 1024))[:, c, wide((2 * half + j) * 2 * NOPE, NOPE)], c_kvT[:, c, :], start=(c == 0), stop=(c == 1))
                    end(mm)
            for i, n in enumerate(kv_loads):
                for t in range(TT):
                    o = begin(job("v_mla", 2 * i + t))
                    for c in range(2):
                        w = slot(n, (2, 1024))[:, c, :].rearrange("p (h d) -> p h d", h=4)[:, :, NOPE:2 * NOPE]
                        mm = pe.matmul(o, c_kvT[:, c, wide(t * P, P)], w, start=(c == 0), stop=(c == 1))
                    end(mm)
            for t in range(TT):
                pe.wait_ge(signal("q_pe_ready"), t + 1)
                o = begin(job("q_peT", t))
                for c in range(MLA_HEADS // 2):
                    mm = pe.transpose(o[:, wide(c * P, P)], q_pe[:, t, wide(c * P, P)], ident)
                end(mm)

            def mla_scores(o, i):
                hd, t = divmod(i, TT)
                if i == 0:
                    for nm, n in (("q_nope", 4), ("k_nope", 4), ("v_mla", 4), ("q_peT", 2)):
                        for j in range(n):
                            pe.wait_ge(*emptied(job(nm, j)))
                part = wide((hd % 2) * ROPE, ROPE)
                pe.matmul(o[:, 0:S], q_nopeT[:, hd, wide(t * P, P)], k_nopeT[:, hd, :], start=True, stop=False)
                return pe.matmul(o[:, 0:S], q_peT[part, hd // 2, wide(t * P, P)], k_peT[part, :], start=False, stop=True)

            def wide_values(v, unit0):
                def values(o, i):
                    for s in range(TT):
                        mm = pe.matmul(o[:, 0:P], probT[:, (unit0 + i) % ATT_BUF, wide(s * P, P)], v[:, s, wide(i // TT * P, P)], start=(s == 0), stop=(s == 1))
                    return mm
                return values

            attention("mla", MLA_UNITS, mla_unit0, mla_scores, wide_values(v_mla, mla_unit0), lambda i: TT, next_fills(0))

            for g in range(DIL_GROUPS):
                token_major(f"dil_v{g}", 2, hT)

                def dil_scores(o, i):
                    hd, t = divmod(i, TT)
                    if i == 0:
                        for nm in "qkv":
                            for j in range(4):
                                pe.wait_ge(*emptied(job(f"dil_{nm}{g}", j)))
                    return pe.matmul(o[:, 0:S], q_dilT[g][:, hd, wide(t * P, P)], k_dilT[g][:, hd, :], start=True, stop=True)

                unit0 = dil_unit0 + g * DIL_UNITS
                attention(f"dil{g}_", DIL_UNITS, unit0, dil_scores, wide_values(v_dil, unit0), lambda i: TT, next_fills(g + 1))
            spread(8, 9, 10)
            pe.wait_ge(signal("mix_ready"), TT)
            transpose_tokens("mixT", h)
            for k in range(4):
                pe.wait_ge(*emptied(job("mixT", k)))
            token_major("w_out", 2, hT)
            spread(11)
            pe.wait_ge(signal("h4_ready"), TT)
            transpose_tokens("h4T", h)
            for k in range(4):
                pe.wait_ge(*emptied(job("h4T", k)))
            pe.wait_ge(signal("router2_in"), 16)
            o = begin(job("router2"))
            for t in range(TT):
                for c in range(KC):
                    mm = pe.matmul(o[:, wide(t * E, E)], hT[:, c, wide(t * P, P)], small_w[:, c, 0:E], start=(c == 0), stop=(c == KC - 1))
            end(mm)
            pe.wait_ge(signal("aff_ready"), 1)
            o = begin(job("affT"))
            for t in range(TT):
                mm = pe.transpose(o[0:E, wide(t * P, P)], gates[:, t, :], ident)
            end(mm)
            pe.wait_ge(signal("rank_T_ready"), 1)
            o = begin(job("rank2"))
            for t in range(TT):
                mm = pe.transpose(o[:, wide(t * E, E)], rank_T[:, wide(t * P, P)], ident[0:E, 0:E])
            end(mm)

            assert next_job[0] == job("ec")
            with pe.Fori(0, EC_ROUNDS) as it:
                R = Rounds(it, job("ec"), EC_JOBS, ec_load0, EC_LOADS)
                pe.wait_ge(signal("pick_ready"), it + (MOE_ROUNDS + 1))
                for j in range(4):
                    o = loop_begin(R, EC_XE + j)
                    for c in (2 * j, 2 * j + 1):
                        for t in range(TT):
                            mm = pe.matmul(o[:, wide((c % 2) * P, P)], h[:, t, c::KC], pick[:, t, 0:P], start=(t == 0), stop=(t == TT - 1))
                    end(mm)
                for t in range(TT):
                    o = loop_begin(R, EC_GW + t)
                    end(pe.transpose(o[:, 0:P], pick_gate[:, t, 0:P], ident))
                for j in range(4):
                    pe.wait_ge(*R.emptied(EC_XE + j))

                def ec_products(outs, lhs, l0, n_loads, width):
                    for n in range(n_loads):
                        for i in range(4):
                            pe.wait_ge(*R.arrived(l0 + 4 * n + i))
                        for c in range(2):
                            for b in range(2):
                                for i in range(4):
                                    mm = pe.matmul(outs[b][wide(i * CAP2, CAP2), :], lhs(2 * n + c, i), R.slot(l0 + 4 * n + i, (2, width))[:, c, wide(b * BANK, BANK)],
                                                   start=(n == c == 0), stop=(n == n_loads - 1 and c == 1))
                                if n == n_loads - 1 and c == 1:
                                    end(mm)
                        if n < n_loads - 1:
                            mm.then_inc(pieces_used, 1)

                for fp in range(2):
                    for l0, j in ((32 * fp, EC_GATE[fp]), (32 * fp + 16, EC_UP[fp])):
                        ec_products([loop_begin(R, j + b) for b in range(2)], lambda c, i: x_e[:, c, wide(i * CAP2, CAP2)], l0, 4, 1024)
                    for b in range(2):
                        o = loop_begin(R, EC_T[fp] + b)
                        pe.wait_ge(*R.emptied(EC_UP[fp] + b))
                        for c in range(4):
                            mm = pe.transpose(o[:, wide(c * P, P)], hid[:, b, wide(c * P, P)], ident)
                        end(mm)
                for fp in range(2):
                    for b in range(2):
                        pe.wait_ge(*R.emptied(EC_T[fp] + b))
                ec_products([loop_begin(R, EC_DOWN + b) for b in range(2)], lambda c, i: hidT[:, c, wide(i * CAP2, CAP2)], 64, 8, D)
                for n in range(2):
                    pe.wait_ge(*R.emptied(EC_DOWN + n))
                for n in range(2):
                    for t in range(TT):
                        o = loop_begin(R, EC_SUM + 2 * n + t)
                        end(pe.matmul(o, gate_T[:, 0, wide(t * P, P)], y_e[:, 0, wide(n * BANK, BANK)], start=True, stop=True))

        @block.scalar
        def _(act):
            step = Turn(act, act_step)
            a = nc.scalar

            def take(k, out, func=ACT.Copy, src=None, **kw):
                act.wait_ge(*done(k))
                step(a.activation, out, bank(k) if src is None else src(bank(k)), func, signals=emptied(k), **kw)

            def rstd_of(n, eps_col, squares=None):
                act.wait_ge(signal("var_ready"), n + 1)
                step(a.activation, rstd[:, :, 0], mv[:, :, 1], ACT.Ln, bias=eps_col)
                step(a.activation, rstd[:, :, 1], rstd[:, :, 0], ACT.Exp, scale=-0.5, signals=(signal("rstd_ready"), n + 1))

            def attention(name, n, unit0, keys, fills):
                due = {fill_span(f, fills, n)[1]: fill for f, fill in enumerate(fills)}
                for i in range(n + LAG_PV):
                    if i < n:
                        u = unit0 + i
                        act.wait_ge(signal("max_ready"), u + 1)
                        step(a.activation, prob[:, u % ATT_BUF, 0:keys(i) * P], prob[:, u % ATT_BUF, 0:keys(i) * P], ACT.Exp,
                             bias=row_max[:, u:u + 1], accum_out=row_sum[:, u:u + 1], signals=(signal("probs_ready"), u + 1))
                    if 0 <= (j := i - LAG_T) < n:
                        if j >= ATT_BUF:
                            act.wait_ge(*done(job(f"{name}_pv{j - ATT_BUF}")))
                        w = keys(j) * P
                        take(job(f"{name}_t{j}"), probT[:, (unit0 + j) % ATT_BUF, 0:w], src=lambda o: o[:, 0:w])
                    if i in due:
                        due[i]()

            a.dma_start(cact[:, 0, :], A["c"][0].rearrange("(p c) -> p c", c=KC)).then_inc(signal("c_in"), 16)
            a.dma_start(cact[:, 1, :], A["c_2"][0].rearrange("(p c) -> p c", c=KC)).then_inc(signal("c_in"), 16)
            a.dma_start(consts[:], A["consts"]).then_inc(signal("const_in"), 16)
            a.dma_start(pos_rows[:, 0:S], A["positions_2"].to_broadcast([P, S])).then_inc(signal("pos_in"), 16)
            for q in range(4):
                a.dma_start(pos_rows[wide(q * BUCKETS, BUCKETS), S:S + S // 4], A["positions_2"][:, wide(q * S // 4, S // 4)].to_broadcast([BUCKETS, S // 4])).then_inc(signal("pos_in"), 16)
            a.dma_start(x[:], A["x"][0].rearrange("(t p) d -> p t d", p=P)).then_inc(signal("x_in"), 16)
            act.wait_ge(signal("zeros_ready"), 1)
            for q in range(4):
                a.dma_start(table[wide(q * BUCKETS, BUCKETS), wide(q * BUCKETS, DIL_GROUPS * DIL_HEADS)], A["rel_bias_2"]).then_inc(signal("table_in"), 16)
            act.wait_ge(signal("c_in"), 32)
            step(a.activation, cact[:], cact[:], ACT.Silu, signals=(signal("cact_ready"), 1))

            def bias_round(it):
                R = Rounds(it, job("bias"), BANKS)
                for half in range(2):
                    act.wait_ge(signal("distance_ready"), it * 2 + (half + 1))
                    a.activation(one_hot[half], one_hot[half], ACT.Abs).then_inc(signal("distance_abs_ready"), 1)
                for j in range(BANKS):
                    act.wait_ge(*R.done(j))
                    if j % 4 == 0 and not isinstance(it, int):
                        act.wait_ge(bias_stored[j // 4], it * BIAS_STORES)
                    a.activation(staged[j // 4][:, wide(j % 4 * BANK, BANK)], R.bank(j), ACT.Copy).then_inc(R.emptied(j)[0], 1)

            bias_round(0)
            with act.Fori(1, BIAS_ROUNDS) as it:
                bias_round(it)
            act.wait_ge(signal("const_in"), 16)
            rstd_of(0, eps5)
            for n in range(2):
                take(job("mod0", n), mod[:, 0, wide(n * BANK, BANK)])
            for n in range(2):
                take(job("mod1", n), mod[:, 1, wide(n * BANK, BANK)], ACT.Identity, bias=1.0)
            act.wait_ge(signal("pad_ready"), 1)

            def conv_silu(j):
                for ct in (2 * j, 2 * j + 1):
                    act.wait_ge(signal("conv_sum_ready"), ct + 1)
                    step(a.activation, xcT[:, ct, :], prob[:, ct % ATT_BUF, :], ACT.Silu, signals=(signal("conv_ready"), ct + 1))

            for j in range(8):
                take(job("xbc", j), u_pad[:, 2 * j:2 * j + 2, 3:3 + S], src=lambda o: o.rearrange("p (c t) -> p c t", c=2))
                if j:
                    conv_silu(j - 1)
            for half in range(2):
                act.wait_ge(bias_stored[half], BIAS_ROUNDS * BIAS_STORES)
            for j in range(2):
                take(job("q", j), qT[:, 2 * j:2 * j + 2, :], src=lambda o: o.rearrange("p (c t) -> p c t", c=2), scale=FOX_D ** -0.5)
            conv_silu(7)
            for j in range(2):
                take(job("k", j), kT[:, 2 * j:2 * j + 2, :], src=lambda o: o.rearrange("p (c t) -> p c t", c=2))
            act.wait_ge(signal("neg_abs_ready"), 1)
            step(a.activation, dtf_e[:], dtf_e[:], ACT.Exp)
            step(a.activation, dtf_e[:], dtf_e[:], ACT.Ln, bias=1.0)
            act.wait_ge(signal("head_in"), 32)
            step(a.activation, head_v[:, 0, :], head_v[:, 0, :], ACT.Exp, signals=(signal("softplus_ready"), 1))
            for j in range(4):
                take(job("z", j), silu_z[:, j % 2, wide(j // 2 * BANK, BANK)], ACT.Silu)
            act.wait_ge(*emptied(job("cumsum")))
            step(a.activation, a_exp[:], a_exp[:], ACT.Exp, signals=(signal("a_exp_ready"), 1))
            for j in range(4):
                t, half = divmod(j, 2)
                take(job("xs_tok", j), xs_tok[:, t, wide(half * BANK, BANK)])
            take(job("b_tok"), b_tok[:].rearrange("p g n -> p (g n)"))
            for t in range(TT):
                take(job("cb", t), cb[:, t].rearrange("p g l -> p (g l)"))

            def decay_exp(k):
                act.wait_ge(*emptied(job(f"a_row{k}")))
                step(a.activation, decay[k % 3], decay[k % 3], ACT.Exp, signals=(signal("decay_exp_ready"), k + 1))

            for k in range(3):
                decay_exp(k)
            act.wait_ge(signal("x_end_ready"), 1)
            for half in range(2):
                take(job("state", half), prev[:, wide(half * BANK, BANK)])

            def take_gate(name, j, to, which=0):
                take(job(name, 4 * which + j), to[:, j % 2, wide(j // 2 * BANK, BANK)])

            take_gate("gs", 0, sig_gs)
            for k in range(3, TT * GROUPS):
                decay_exp(k)
                if k % 2 == 0:
                    take_gate("gs", k // 2 - 1, sig_gs)
            take_gate("gs", 3, sig_gs)
            for t in range(TT):
                act.wait_ge(signal("gated_ready"), t + 1)
                step(a.activation, silu_z[:, t, :], y_tok[:, t, :], ACT.Square, scale=D ** -0.5, accum_out=mv[:, t, 1:2])
            act.wait_ge(act_step, step.n)
            step(a.activation, rstd[:, :, 0], mv[:, :, 1], ACT.Ln, bias=eps5)
            step(a.activation, rstd[:, :, 1], rstd[:, :, 0], ACT.Exp, scale=-0.5, signals=(signal("rms_ready"), 1))
            attention("fox", FOX_UNITS, 0, lambda i: i % TT + 1,
                      [(lambda: None) if fill[0] == "unit" else (lambda fill=fill: take_gate("ga", 2 * fill[2] + fill[3], sig_ga)) for fill in fox_fills])
            step(a.activation, sig_both, sig_both, ACT.Sigmoid, signals=(signal("gates_ready"), 1))
            for t in range(TT):
                take(job("oT", t), oT[:, :, wide(t * P, P)], src=lambda o: o.rearrange("p (c t) -> p c t", c=4))
            for j in range(4):
                t, half = divmod(j, 2)
                take(job("mT", j), hT[:, 4 * half:4 * half + 4, wide(t * P, P)], src=lambda o: o.rearrange("p (c t) -> p c t", c=4))
            rstd_of(1, eps5)
            for n in range(2):
                take(job("mod5", n), mod[:, 2, wide(n * BANK, BANK)], ACT.Identity, bias=1.0)
            rstd_of(2, eps5)
            for j in range(4):
                t, half = divmod(j, 2)
                take(job("h2T", j), hT[:, 4 * half:4 * half + 4, wide(t * P, P)], src=lambda o: o.rearrange("p (c t) -> p c t", c=4))
            act.wait_ge(signal("route_logits_ready"), 1)
            step(a.activation, route_g[:], route_g[:], ACT.Exp)
            step(a.activation, route_2[:], route_2[:], ACT.Exp, signals=(signal("route_exp_ready"), 1))

            for n in range(2):
                take(job("mod6", n), mod[:, 0, wide(n * BANK, BANK)])
            for n in range(2):
                take(job("mod7", n), mod[:, 1, wide(n * BANK, BANK)], ACT.Identity, bias=1.0)

            def moe_round(R):
                step.begin_loop(R.it, 0)
                step.last = None

                def take_round(j, out, func=ACT.Copy, width=BANK):
                    act.wait_ge(*R.done(j))
                    step(a.activation, out, R.bank(j)[:, 0:width], func, signals=R.emptied(j))

                for p in range(2):
                    take_round(MOE_GW + p, gate_T[:, p, :], width=S)
                for p in range(2):
                    take_round(MOE_GATE[p], silu_g[:, p, :], ACT.Silu)
                for p in range(2):
                    take_round(MOE_T[p], hidT[:, 4 * p:4 * p + 4, :].rearrange("p c t -> p (c t)"))
                    for n in range(2):
                        take_round(MOE_DOWN[p] + n, y_e[:, p, wide(n * BANK, BANK)])
                step.end_loop(0)
                step.last = None

            with act.Fori(0, MOE_ROUNDS) as it:
                moe_round(Rounds(it, job("moe"), MOE_JOBS))
            with more_tokens(act):
                with act.Fori(0, MORE_ROUNDS) as it:
                    moe_round(Rounds(it, 0, MOE_JOBS, **more_sems))

            rstd_of(3, eps5)

            def square_means(n, srcs):
                for t in range(TT):
                    for src, to, width in srcs:
                        step(a.activation, silu_junk[:, 0:width], src(t), ACT.Square, scale=width ** -0.5, accum_out=to[:, t, 1:2])
                act.wait_ge(act_step, step.n)
                for _, to, _ in srcs:
                    step(a.activation, rstd[:, :, 0], to[:, :, 1], ACT.Ln, bias=eps6)
                    step(a.activation, to[:, :, 0], rstd[:, :, 0], ACT.Exp, scale=-0.5)
                act.wait_ge(act_step, step.n)
                step(a.activation, rstd[:, :, 0], to[:, :, 1], ACT.Copy, signals=(signal("rms2_ready"), n + 1))

            act.wait_ge(signal("x_b1_ready"), 1)
            step(a.activation, turn[:, 2:4].rearrange("p a t f -> p (a t f)"), turn[:, 0:2].rearrange("p a t f -> p (a t f)"), ACT.Sin, signals=(signal("sin_ready"), 1))
            square_means(0, [(lambda t: x[:, t, :], mv, D)])
            for j in range(4):
                t, half = divmod(j, 2)
                take(job("h3T", j), hT[:, 4 * half:4 * half + 4, wide(t * P, P)], src=lambda o: o.rearrange("p (c t) -> p c t", c=4))
            for j in range(4):
                i, t = divmod(j, 2)
                w = min(BANK, LAT - i * BANK)
                take(job("lat", j), lat[:, t, wide(i * BANK, w)], src=lambda o: o[:, 0:w])
            square_means(1, [(lambda t: lat[:, t, 0:Q_RANK], mv, Q_RANK), (lambda t: lat[:, t, wide(Q_RANK, KV_RANK)], mv2, KV_RANK)])

            def two_tiles(o):
                return o.rearrange("p (c t) -> p c t", c=2)

            for j in range(4):
                take(job("q_nope", j), q_nopeT[:, 2 * j:2 * j + 2, :], src=two_tiles)
            for j in range(4):
                take(job("k_nope", j), k_nopeT[:, 2 * j:2 * j + 2, :], src=two_tiles)
            for j in range(4):
                half, t = divmod(j, 2)
                take(job("v_mla", j), v_mla[:, t, wide(half * BANK, BANK)])
            for t in range(TT):
                take(job("q_peT", t), q_peT[:, :, wide(t * P, P)], src=lambda o: o.rearrange("p (c t) -> p c t", c=4))

            def take_next(g):
                if g == DIL_GROUPS:
                    return [lambda j=j: take_gate("gates2", j % 4, (sig_a, sig_b)[j // 4], j // 4) for j in range(8)]
                return [lambda nm=nm, to=to, j=j: take(job(f"dil_{nm}{g}", j), to[g][:, 2 * j:2 * j + 2, :], src=two_tiles)
                        for nm, to in (("q", q_dilT), ("k", k_dilT)) for j in range(4)]

            attention("mla", MLA_UNITS, mla_unit0, lambda i: TT, take_next(0))
            for g in range(DIL_GROUPS):
                for j in range(4):
                    take(job(f"dil_v{g}", j), v_dil[:, j % 2, wide(j // 2 * BANK, BANK)])
                attention(f"dil{g}_", DIL_UNITS, dil_unit0 + g * DIL_UNITS, lambda i: TT, take_next(g + 1))
            step(a.activation, sig_ab, sig_ab, ACT.Sigmoid, signals=(signal("gates2_ready"), 1))
            act.wait_ge(signal("dil_shift_ready"), 1)
            step(a.activation, dil_w.rearrange("p g u -> p (g u)"), dil_w.rearrange("p g u -> p (g u)"), ACT.Exp, signals=(signal("dil_exp_ready"), 1))
            for unit in (8, 9, 10):
                for n in range(2):
                    take(job(f"mod{unit}", n), mod[:, (2, 0, 1)[unit - 8], wide(n * BANK, BANK)], ACT.Identity, bias=1.0 if unit == 10 else 0.0)
            for j in range(4):
                t, half = divmod(j, 2)
                take(job("mixT", j), hT[:, 4 * half:4 * half + 4, wide(t * P, P)], src=lambda o: o.rearrange("p (c t) -> p c t", c=4))
            act.wait_ge(signal("x2_ready"), 1)
            square_means(2, [(lambda t: x[:, t, :], mv, D)])
            for n in range(2):
                take(job("mod11", n), mod[:, 2, wide(n * BANK, BANK)])
            for j in range(4):
                t, half = divmod(j, 2)
                take(job("h4T", j), hT[:, 4 * half:4 * half + 4, wide(t * P, P)], src=lambda o: o.rearrange("p (c t) -> p c t", c=4))
            act.wait_ge(signal("aff_logits_ready"), 1)
            step(a.activation, gates[:], gates[:], ACT.Exp, signals=(signal("aff_exp_ready"), 1))

            with act.Fori(0, EC_ROUNDS) as it:
                R = Rounds(it, job("ec"), EC_JOBS)
                step.begin_loop(it, 0)
                step.last = None

                def take_ec(j, out, func=ACT.Copy, width=BANK):
                    act.wait_ge(*R.done(j))
                    step(a.activation, out, R.bank(j)[:, 0:width], func, signals=R.emptied(j))

                for t in range(TT):
                    take_ec(EC_GW + t, gate_T[:, 0, wide(t * P, P)], width=P)
                for fp in range(2):
                    for b in range(2):
                        take_ec(EC_GATE[fp] + b, silu_g[:, b, :], ACT.Silu)
                    for b in range(2):
                        take_ec(EC_T[fp] + b, hidT[:, 8 * fp + 4 * b:8 * fp + 4 * b + 4, :].rearrange("p c t -> p (c t)"))
                for n in range(2):
                    take_ec(EC_DOWN + n, y_e[:, 0, wide(n * BANK, BANK)])
                step.end_loop(EC_ROUNDS)
                step.last = None
            act.wait_ge(signal("x3_ready"), 1)
            square_means(3, [(lambda t: x[:, t, :], mv, D)])

        @block.vector
        def _(dve):
            step = Turn(dve, dve_step)
            v = nc.vector

            def take(k, op, *args, **kw):
                dve.wait_ge(*done(k))
                step(op, *args, signals=emptied(k), **kw)

            def norm_stats(src, n):
                for t in range(TT):
                    for half in range(2):
                        step(v.bn_stats, stats[:, t, half, :], src[:, t, wide(half * 512, 512)])
                    step(v.bn_aggr, mv[:, t, :], stats[:, t].rearrange("p a b -> p (a b)"), signals=(signal("var_ready"), n + 1) if t == TT - 1 else None)

            def normalize(dst, src, n, t):
                if t == 0:
                    dve.wait_ge(signal("rstd_ready"), n + 1)
                step(v.tensor_scalar, dst[:, t, :], src[:, t, :], mv[:, t, 0:1], rstd[:, t, 1:2], ALU.subtract, ALU.mult)

            def attention(name, n, unit0, masked, keys, out, fills=()):
                due = {fill_span(f, fills, n)[1]: fill for f, fill in enumerate(fills)}
                for i in range(n + LAG_PV):
                    if i < n:
                        u, k, w = unit0 + i, job(f"{name}_qk{i}"), keys(i) * P
                        if i >= ATT_BUF:
                            dve.wait_ge(*done(job(f"{name}_t{i - ATT_BUF}")))
                        dve.wait_ge(*done(k))
                        masked(i, prob[:, u % ATT_BUF, 0:w], bank(k)[:, 0:w], emptied(k))
                        step(v.tensor_reduce, row_max[:, u:u + 1], prob[:, u % ATT_BUF, 0:w], AX, ALU.max, negate=True, signals=(signal("max_ready"), u + 1))
                    if 0 <= (j := i - LAG_PV) < n:
                        u, k = unit0 + j, job(f"{name}_pv{j}")
                        step(v.reciprocal, row_inv[:, u:u + 1], row_sum[:, u:u + 1])
                        take(k, v.tensor_scalar, out(j), bank(k)[:, 0:out(j).shape[-1]], row_inv[:, u:u + 1], None, ALU.mult)
                    if i in due and due[i][0] == "unit":
                        add_row(due[i][1])

            step(v.memset, mod_rows[:], 0.0)
            step(v.memset, table[:], 0.0, signals=(signal("zeros_ready"), 1))
            step(v.memset, cond[:], 0.0)
            dve.wait_ge(signal("cact_ready"), 1)
            step(v.tensor_copy, cond[:, :, :, 31], cact[:], signals=(signal("cond_ready"), 1))
            dve.wait_ge(signal("pos_in"), 80)
            dve.wait_ge(signal("const_in"), 16)
            step(v.tensor_copy, pos_all, pos_rows[:, 0:S])
            step(v.tensor_copy, pos_quarter, pos_rows[:, S:S + S // 4])
            step(v.tensor_scalar, pos_quarter, pos_quarter, bucket_range[:, 0:1], None, ALU.add)
            dve.wait_ge(signal("x_in"), 16)
            norm_stats(x, 0)

            def bias_round(it):
                for half in range(2):
                    if not isinstance(it, int):
                        dve.wait_ge(pe_done, it * BANKS + (job("bias") - BANKS + 4 * half + 4))
                    queries = pos_quarter[:, bass.ds(it * (2 * BIAS_QUERIES) + half * BIAS_QUERIES, BIAS_QUERIES)]
                    step(v.tensor_tensor, one_hot[half], pos_all.unsqueeze(1).to_broadcast([P, BIAS_QUERIES, S]), queries.unsqueeze(2).to_broadcast([P, BIAS_QUERIES, S]), ALU.subtract,
                         signals=(signal("distance_ready"), it * 2 + (half + 1)))
                for half in range(2):
                    dve.wait_ge(signal("distance_abs_ready"), it * 2 + (half + 1))
                    step(v.tensor_scalar, one_hot[half], one_hot[half], bucket_range[:, 1:2], None, ALU.is_le, signals=(signal("one_hot_ready"), it * 2 + (half + 1)))

            bias_round(0)
            take(job("vecT"), v.tensor_copy, vecT[:, 0:85], bank(job("vecT"))[:, 0:85])
            dve.wait_ge(signal("mod_bias_in"), 64)

            def add_row(u):
                k = job(f"unit{u}")
                take(k, v.tensor_tensor, mod_rows[:], bank(k), mod_rows[:], ALU.add)

            add_row(0)
            with dve.Fori(1, BIAS_ROUNDS) as it:
                step.begin_loop(it, 0, first=1)
                bias_round(it)
                step.end_loop(BIAS_ROUNDS - 1)
            step(v.memset, u_pad[:, :, 0:3], 0.0, signals=(signal("pad_ready"), 1))
            for t in range(TT):
                normalize(h, x, 0, t)
            add_row(1)
            for unit in ("mod0", "mod1"):
                for n in range(2):
                    dve.wait_ge(*emptied(job(unit, n)))
            for t in range(TT):
                step(v.tensor_tensor, h[:, t, :], h[:, t, :], mod[:, 1, :], ALU.mult)
                step(v.tensor_tensor, h[:, t, :], h[:, t, :], mod[:, 0, :], ALU.add, signals=(signal("h_ready"), t + 1))
            for j in range(4):
                t, half = divmod(j, 2)
                take(job("hT", j), v.tensor_copy, hT[:, 4 * half:4 * half + 4, wide(t * P, P)], bank(job("hT", j)).rearrange("p (c t) -> p c t", c=4))

            for ct in range(16):
                dve.wait_ge(*emptied(job("xbc", ct // 2)))
                if ct >= ATT_BUF:
                    dve.wait_ge(signal("conv_ready"), ct - ATT_BUF + 1)
                acc = prob[:, ct % ATT_BUF, :]
                step(v.tensor_scalar, acc, u_pad[:, ct, 0:S], vecT[:, ct:ct + 1], vecT[:, 64 + ct:65 + ct], ALU.mult, ALU.add)
                for j in range(1, 4):
                    step(v.scalar_tensor_tensor, acc, u_pad[:, ct, j:j + S], vecT[:, 16 * j + ct:16 * j + ct + 1], acc, ALU.mult, ALU.add,
                         signals=(signal("conv_sum_ready"), ct + 1) if j == 3 else None)
                if ct % 4 == 3:
                    add_row(IN_UNITS[ct // 4])
            k = job("dtf")
            dve.wait_ge(*done(k))
            both = bank(k)[:, 0:TT * 24].rearrange("p (t c) -> p t c", t=TT)
            step(v.tensor_copy, dtf[:, :, 0:HEADS], both[:, :, 0:HEADS])
            step(v.tensor_scalar, dtf[:, :, HEADS:24], both[:, :, HEADS:24], -1.0, None, ALU.mult, signals=emptied(k))
            step(v.scalar_tensor_tensor, dtf_e[:], dtf[:], -1.0, dtf[:], ALU.mult, ALU.min, signals=(signal("neg_abs_ready"), 1))
            for j in range(2):
                take(job("v", j), v.tensor_copy, v_tok[:, j, :], bank(job("v", j)))
            dve.wait_ge(signal("pos_tok_in"), 16)
            step(v.tensor_copy, posf[:], pos_i[:])
            for t in range(TT):
                step(v.tensor_scalar, turn[:, 0, t, :], inv_freq, posf[:, t:t + 1], None, ALU.mult)
            step(v.tensor_scalar, turn[:, 2], turn[:, 0], 1.0 / TWO_PI, MAGIC, ALU.mult, ALU.add)
            step(v.tensor_scalar, turn[:, 2], turn[:, 2], MAGIC, None, ALU.subtract)
            step(v.scalar_tensor_tensor, turn[:, 0], turn[:, 2], -TWO_PI_HI, turn[:, 0], ALU.mult, ALU.add)
            step(v.scalar_tensor_tensor, turn[:, 0], turn[:, 2], -(TWO_PI - TWO_PI_HI), turn[:, 0], ALU.mult, ALU.add)
            step(v.tensor_scalar, turn[:, 1], turn[:, 0], TWO_PI / 4, None, ALU.add)
            step(v.tensor_scalar, turn[:, 2], turn[:, 1], PI, -TWO_PI, ALU.is_gt, ALU.mult)
            step(v.tensor_tensor, turn[:, 1], turn[:, 1], turn[:, 2], ALU.add)
            step(v.tensor_scalar, turn[:, 0:2], turn[:, 0:2], PI, -PI, ALU.min, ALU.max)
            dve.wait_ge(signal("softplus_ready"), 1)
            step(v.scalar_tensor_tensor, dtf[:], dtf[:], 0.0, dtf_e[:], ALU.max, ALU.add)
            step(v.tensor_copy, cum_in[:, :, HEADS:24], dtf[:, :, HEADS:24])
            step(v.scalar_tensor_tensor, cum_in[:, :, 0:HEADS], dtf[:, :, 0:HEADS], -1.0, head_v[:, 0:1, :].to_broadcast([P, TT, HEADS]), ALU.mult, ALU.mult,
                 signals=(signal("cum_in_ready"), 1))
            k = job("cumsum")
            dve.wait_ge(*done(k))
            step(v.tensor_copy, a_cs[:], bank(k)[:, 0:64].rearrange("p (t c) -> p t c", t=TT)[:, :, 0:HEADS])
            step(v.tensor_copy, neg_F[:, 0, :], bank(k)[:, 16:24])
            step(v.tensor_copy, neg_F[:, 1, :], bank(k)[:, 64:72])
            step(v.tensor_copy, a_exp[:, 0, :], a_cs[:, 1, :])
            step(v.tensor_tensor, a_exp[:, 1, :], bank(k)[:, 96:112], a_cs[:, 0, :], ALU.subtract, signals=emptied(k))
            for unit in (2, 3, 4):
                for n in range(2):
                    k = job(f"mod{unit}", n)
                    take(k, v.tensor_scalar, mod[:, (2, 0, 1)[unit - 2], wide(n * BANK, BANK)], bank(k), 0.0 if unit == 3 else 1.0, None, ALU.add)
            for j in range(4):
                t, half = divmod(j, 2)
                dve.wait_ge(*emptied(job("xs_tok", j)))
                step(v.tensor_tensor, xdt[:, t, wide(half * BANK, BANK)].rearrange("p (g d) -> p g d", d=HD), xs_tok[:, t, wide(half * BANK, BANK)].rearrange("p (g d) -> p g d", d=HD),
                     dtf[:, t, wide(half * 8, 8)].unsqueeze(2).to_broadcast([P, 8, HD]), ALU.mult)
            dve.wait_ge(signal("a_exp_ready"), 1)
            step(v.tensor_tensor, x_end.rearrange("p (g d) -> p g d", d=HD), xdt[:, 0, :].rearrange("p (g d) -> p g d", d=HD),
                 a_exp[:, 1, :].unsqueeze(2).to_broadcast([P, HEADS, HD]), ALU.mult, signals=(signal("x_end_ready"), 1))

            def segments(k):
                t, g = divmod(k, GROUPS)
                dve.wait_ge(*done(job(f"a_row{k}")))
                if k >= 3:
                    dve.wait_ge(*done(job(f"y_diag{(k - 3) // 2}")))
                for r in range(PER_GROUP):
                    hd = g * PER_GROUP + r
                    last = r == PER_GROUP - 1
                    step(v.scalar_tensor_tensor, decay[k % 3][:, wide(r * P, P)], bank(job(f"a_row{k}"))[:, wide(r * P, P)], a_cs[:, t, hd:hd + 1], seg_mask,
                         ALU.subtract, ALU.add, signals=emptied(job(f"a_row{k}")) if last else None)

            def masked_cb(k):
                t, g = divmod(k, GROUPS)
                dve.wait_ge(signal("decay_exp_ready"), k + 1)
                if k == 0:
                    for j in range(TT):
                        dve.wait_ge(*emptied(job("cb", j)))
                step(v.tensor_tensor, decay[k % 3].rearrange("p (r l) -> p r l", r=PER_GROUP), decay[k % 3].rearrange("p (r l) -> p r l", r=PER_GROUP),
                     cb[:, t, g:g + 1, :].to_broadcast([P, PER_GROUP, P]), ALU.mult, signals=(signal("decay_ready"), k + 1))

            y_off = params[:, 0, :]

            def heads_of(ap):
                return ap.rearrange("p (g d) -> p g d", d=HD)

            def assemble(m):
                t, half = divmod(m, 2)
                cols, k = wide(half * BANK, BANK), job(f"y_diag{m}")
                step(v.tensor_tensor, heads_of(y_tok[:, t, cols]), heads_of(xs_tok[:, t, cols]), head_v[:, 1, wide(half * 8, 8)].unsqueeze(2).to_broadcast([P, 8, HD]), ALU.mult)
                take(k, v.tensor_tensor, y_tok[:, t, cols], bank(k), y_tok[:, t, cols], ALU.add)
                if t:
                    step(v.tensor_tensor, y_tok[:, t, cols], y_tok[:, t, cols], y_off[:, cols], ALU.add)
                if m == 0:
                    for j in range(4):
                        dve.wait_ge(*emptied(job("z", j)))
                step(v.tensor_tensor, y_tok[:, t, cols], y_tok[:, t, cols], silu_z[:, t, cols], ALU.mult, signals=(signal("gated_ready"), t + 1) if half else None)

            segments(0)
            segments(1)
            masked_cb(0)
            segments(2)
            masked_cb(1)
            for half in range(2):
                k = job("y_off", half)
                take(k, v.tensor_tensor, heads_of(y_off[:, wide(half * BANK, BANK)]), heads_of(bank(k)), a_exp[:, 0, wide(half * 8, 8)].unsqueeze(2).to_broadcast([P, 8, HD]), ALU.mult)
            for m in range(2 * TT):
                assemble(m)
                for k in range(3 + 2 * m, min(5 + 2 * m, TT * GROUPS)):
                    segments(k)
                    masked_cb(k - 1)
                if m == 2:
                    masked_cb(TT * GROUPS - 1)
            dve.wait_ge(signal("rms_ready"), 1)
            for t in range(TT):
                step(v.tensor_scalar, y_tok[:, t, :], y_tok[:, t, :], rstd[:, t, 1:2], None, ALU.mult, signals=(signal("y_ssd_ready"), t + 1))

            def fox_mask(i, dst, src, taken):
                hd, t = divmod(i, TT)
                step(v.scalar_tensor_tensor, dst, src, neg_F[:, t, hd:hd + 1], causal[:, (1 - t) * P:2 * P], ALU.subtract, ALU.add, signals=taken)

            attention("fox", FOX_UNITS, 0, fox_mask, lambda i: i % TT + 1, lambda i: o_fox[:, i % TT, wide(i // TT * FOX_D, FOX_D)], fox_fills)
            dve.wait_ge(signal("ssd_w_in"), 16)
            for j in range(4):
                t, half = divmod(j, 2)
                k = job("yT", j)
                take(k, v.tensor_tensor, hT[:, 4 * half:4 * half + 4, wide(t * P, P)], bank(k).rearrange("p (c t) -> p c t", c=4),
                     ssd_w[:, 4 * half:4 * half + 4].unsqueeze(2).to_broadcast([P, 4, P]), ALU.mult)
            for j in range(4):
                n, t = divmod(j, 2)
                cols = wide(n * BANK, BANK)
                if j == 0:
                    dve.wait_ge(signal("gates_ready"), 1)
                k = job("merge", 2 * j)
                take(k, v.tensor_tensor, h[:, t, cols], bank(k), sig_gs[:, t, cols], ALU.mult)
                k = job("merge", 2 * j + 1)
                take(k, v.tensor_tensor, junk[:, 0:BANK], bank(k), sig_ga[:, t, cols], ALU.mult)
                step(v.tensor_tensor, h[:, t, cols], h[:, t, cols], junk[:, 0:BANK], ALU.add, signals=(signal("merged_ready"), j + 1))

            def residual(name):
                for j in range(4):
                    n, t = divmod(j, 2)
                    cols, k = wide(n * BANK, BANK), job(name, j)
                    take(k, v.tensor_tensor, junk[:, 0:BANK], bank(k), mod[:, 2, cols], ALU.mult)
                    step(v.scalar_tensor_tensor, x[:, t, cols], x[:, t, cols], ALPHA, junk[:, 0:BANK], ALU.mult, ALU.add)

            residual("w_o")
            norm_stats(x, 1)
            for t in range(TT):
                normalize(x, x, 1, t)
                if t == 0:
                    dve.wait_ge(signal("params_in"), 32)
                step(v.tensor_tensor, x[:, t, :], x[:, t, :], params[:, 0, :], ALU.mult)
                step(v.tensor_tensor, x[:, t, :], x[:, t, :], params[:, 1, :], ALU.add, signals=(signal("x_mid_ready"), 1) if t else None)
            norm_stats(x, 2)
            for t in range(TT):
                normalize(h, x, 2, t)
                step(v.tensor_tensor, h[:, t, :], h[:, t, :], mod[:, 1, :], ALU.mult)
                step(v.tensor_tensor, h[:, t, :], h[:, t, :], mod[:, 0, :], ALU.add, signals=(signal("h2_ready"), t + 1))

            def first_of(dst, vals, top, n):
                step(v.tensor_reduce, top, vals, AX, ALU.max)
                step(v.tensor_tensor, dst, vals, top.unsqueeze(2).to_broadcast([P, TT, n]), ALU.is_equal)
                step(v.tensor_tensor, dst, dst, desc[:, E - n:E].unsqueeze(1).to_broadcast([P, TT, n]), ALU.mult)
                step(v.tensor_reduce, route_top[:], dst, AX, ALU.max)
                step(v.tensor_tensor, dst, dst, route_top[:].unsqueeze(2).to_broadcast([P, TT, n]), ALU.is_equal)

            k = job("router")
            dve.wait_ge(*done(k))
            step(v.tensor_copy, logits[:], bank(k)[:, 0:TT * 20].rearrange("p (t c) -> p t c", t=TT), signals=emptied(k))
            first_of(hot_g[:], logits[:, :, 0:4], top1[:], 4)
            step(v.tensor_tensor, route_g[:], logits[:, :, 0:4], top1[:].unsqueeze(2).to_broadcast([P, TT, 4]), ALU.subtract)
            for t in range(TT):
                step(v.tensor_tensor, in_group[:, t].rearrange("p (g e) -> p g e", g=4), logits[:, t, 4:20].rearrange("p (g e) -> p g e", g=4), hot_g[:, t, :].unsqueeze(2).to_broadcast([P, 4, 4]), ALU.mult)
                step(v.tensor_reduce, e_in[:, t, :], in_group[:, t].rearrange("p (g e) -> p e g", g=4), AX, ALU.add)
            first_of(hot1[:], e_in[:], top1[:], 4)
            step(v.scalar_tensor_tensor, e_in[:], hot1[:], NEG, e_in[:], ALU.mult, ALU.add)
            first_of(hot2[:], e_in[:], top2[:], 4)
            step(v.tensor_tensor, route_2[:], top2[:], top1[:], ALU.subtract, signals=(signal("route_logits_ready"), 1))
            step(v.tensor_tensor, e_in[:], hot1[:], hot2[:], ALU.add)
            for t in range(TT):
                step(v.tensor_tensor, chosen[:, t].rearrange("p (g e) -> p g e", g=4), hot_g[:, t, :].unsqueeze(2).to_broadcast([P, 4, 4]),
                     e_in[:, t, :].unsqueeze(1).to_broadcast([P, 4, 4]), ALU.mult, signals=(signal("chosen_ready"), 1) if t else None)
            dve.wait_ge(signal("route_exp_ready"), 1)
            step(v.tensor_reduce, top1[:], route_g[:], AX, ALU.add)
            step(v.scalar_tensor_tensor, top1[:], route_2[:], 1.0, top1[:], ALU.add, ALU.mult)
            step(v.reciprocal, top1[:], top1[:])
            step(v.tensor_tensor, top2[:], route_2[:], top1[:], ALU.mult)
            step(v.tensor_tensor, hot1[:], hot1[:], top1[:].unsqueeze(2).to_broadcast([P, TT, 4]), ALU.mult)
            step(v.tensor_tensor, hot2[:], hot2[:], top2[:].unsqueeze(2).to_broadcast([P, TT, 4]), ALU.mult)
            step(v.tensor_tensor, hot1[:], hot1[:], hot2[:], ALU.add)
            for t in range(TT):
                step(v.tensor_tensor, gates[:, t].rearrange("p (g e) -> p g e", g=4), hot_g[:, t, :].unsqueeze(2).to_broadcast([P, 4, 4]),
                     hot1[:, t, :].unsqueeze(1).to_broadcast([P, 4, 4]), ALU.mult)
            k = job("rank")
            dve.wait_ge(*done(k))
            step(v.tensor_reduce, top1[:, 0:1], bank(k)[:, TT * E:(TT + 1) * E], AX, ALU.max)
            step(v.tensor_scalar, overflow[:], top1[:, 0:1], float(CAP), None, ALU.is_gt, signals=(signal("overflow_known"), 1))
            step(v.tensor_tensor, rank[:], bank(k)[:, 0:TT * E].rearrange("p (t e) -> p t e", t=TT), chosen[:], ALU.mult, signals=emptied(k))

            step(v.memset, y_sum, 0.0)

            def one_hots(step, quad, width, signalled):
                for t in range(TT):
                    step(v.tensor_tensor, pick[:, t, 0:4 * width].rearrange("p (e j) -> p e j", e=4), iota1[:, 0:width].unsqueeze(1).to_broadcast([P, 4, width]),
                         rank[:, t, bass.ds(quad * 4, 4)].unsqueeze(2).to_broadcast([P, 4, width]), ALU.is_equal)
                for t in range(TT):
                    step(v.tensor_tensor, pick_gate[:, t, 0:4 * width].rearrange("p (e j) -> p e j", e=4), pick[:, t, 0:4 * width].rearrange("p (e j) -> p e j", e=4),
                         gates[:, t, bass.ds(quad * 4, 4)].unsqueeze(2).to_broadcast([P, 4, width]), ALU.mult, signals=signalled if t else None)

            def moe_sums(step, R):
                for j in range(4):
                    dve.wait_ge(*R.done(MOE_XE + j))
                    step(v.tensor_copy, x_e[:, 2 * j:2 * j + 2, :].rearrange("p c t -> p (c t)"), R.bank(MOE_XE + j), signals=R.emptied(MOE_XE + j))
                for p in range(2):
                    dve.wait_ge(*R.emptied(MOE_GATE[p]))
                    dve.wait_ge(*R.done(MOE_UP[p]))
                    step(v.tensor_tensor, hid[:, p, :], R.bank(MOE_UP[p]), silu_g[:, p, :], ALU.mult, signals=R.emptied(MOE_UP[p]))
                for p in range(2):
                    for n in range(2):
                        for t in range(TT):
                            j, cols = MOE_SUM[p] + 2 * n + t, wide(n * BANK, BANK)
                            dve.wait_ge(*R.done(j))
                            step(v.tensor_tensor, y_sum[:, t, cols], R.bank(j), y_sum[:, t, cols], ALU.add, signals=R.emptied(j))

            with dve.Fori(0, MOE_ROUNDS) as it:
                step.begin_loop(it, 3)
                one_hots(step, it, CAP, (signal("pick_ready"), it + 1))
                moe_sums(step, Rounds(it, job("moe"), MOE_JOBS))
                step.end_loop(MOE_ROUNDS)
            moe_over = [emptied(job("moe", (MOE_ROUNDS - 1) * MOE_JOBS + MOE_SUM[0] + j)) for j in range(BANKS)]
            for taken in moe_over:
                dve.wait_ge(*taken)
            with more_tokens(dve):
                more = Turn(dve, sem("more_dve_step"))
                more(v.memset, pass_shift[:], 0.0)
                more(v.memset, pass_shift[:, 0:1], float(CAP))
                with dve.Fori(0, MORE_ROUNDS) as it:
                    R = Rounds(it, 0, MOE_JOBS, **more_sems)
                    more.begin_loop(it, 4)
                    quad = it & (QUADS - 1)
                    more(v.tensor_tensor, rank[:], rank[:], pass_shift[:, bass.ds(quad, 1)].unsqueeze(2).to_broadcast([P, TT, E]), ALU.subtract)
                    one_hots(more, quad, CAP, (signal("more_pick_ready"), it + 1))
                    moe_sums(more, R)
                    more.end_loop(MORE_ROUNDS)
                for j in range(BANKS):
                    dve.wait_ge(more_sems["evacuated"][j], MORE_ROUNDS * MOE_JOBS // BANKS)

            def residual_sum(alpha):
                for t in range(TT):
                    step(v.tensor_tensor, y_sum[:, t, :], y_sum[:, t, :], mod[:, 2, :], ALU.mult)
                    step(v.scalar_tensor_tensor, x[:, t, :], x[:, t, :], alpha, y_sum[:, t, :], ALU.mult, ALU.add)

            residual_sum(ALPHA)
            norm_stats(x, 3)
            for t in range(TT):
                normalize(x, x, 3, t)
                if t == 0:
                    dve.wait_ge(signal("params_in"), 64)
                step(v.tensor_tensor, x[:, t, :], x[:, t, :], params[:, 0, :], ALU.mult)
                step(v.tensor_tensor, x[:, t, :], x[:, t, :], params[:, 1, :], ALU.add, signals=(signal("x_b1_ready"), 1) if t else None)

            def rms_modulated(n, gain, ready, value):
                dve.wait_ge(signal("rms2_ready"), n + 1)
                for t in range(TT):
                    step(v.scalar_tensor_tensor, h[:, t, :], x[:, t, :], mv[:, t, 0:1], gain, ALU.mult, ALU.mult)
                    step(v.tensor_tensor, h[:, t, :], h[:, t, :], mod[:, 1, :], ALU.mult)
                    step(v.tensor_tensor, h[:, t, :], h[:, t, :], mod[:, 0, :], ALU.add, signals=(signal(ready), t + 1))

            dve.wait_ge(signal("params_in"), 96)
            for unit in ("mod6", "mod7"):
                for n in range(2):
                    dve.wait_ge(*emptied(job(unit, n)))
            rms_modulated(0, params[:, 0, :], "h3_ready", 1)

            def rotate(dst, src, t, heads, taken=None):
                half = ROPE // 2
                n = heads * half
                sin, cos = (turn[:, i, t, :].unsqueeze(1).to_broadcast([P, heads, half]) for i in (2, 3))
                one, two = (rope_tmp[:, i, 0:n].rearrange("p (h d) -> p h d", h=heads) for i in (0, 1))
                s1, s2, d1, d2 = src[:, :, 0:half], src[:, :, half:ROPE], dst[:, :, 0:half], dst[:, :, half:ROPE]
                step(v.tensor_tensor, one, s1, cos, ALU.mult)
                step(v.tensor_tensor, two, s2, sin, ALU.mult)
                step(v.tensor_tensor, d1, one, two, ALU.subtract)
                step(v.tensor_tensor, one, s1, sin, ALU.mult)
                step(v.tensor_tensor, two, s2, cos, ALU.mult, signals=taken)
                return d2, one, two

            for i in range(4):
                dve.wait_ge(*emptied(job("lat", i)))
            dve.wait_ge(signal("rms2_ready"), 2)
            dve.wait_ge(signal("sin_ready"), 1)
            for t in range(TT):
                d2, one, two = rotate(k_pe[:, t, 0:ROPE].unsqueeze(1), lat[:, t, LAT - ROPE:LAT].unsqueeze(1), t, 1)
                step(v.tensor_tensor, d2, one, two, ALU.add)
                step(v.tensor_copy, k_pe[:, t, ROPE:2 * ROPE], k_pe[:, t, 0:ROPE])
                step(v.tensor_scalar, lat[:, t, 0:Q_RANK], lat[:, t, 0:Q_RANK], mv[:, t, 0:1], None, ALU.mult)
                step(v.tensor_scalar, lat[:, t, wide(Q_RANK, KV_RANK)], lat[:, t, wide(Q_RANK, KV_RANK)], mv2[:, t, 0:1], None, ALU.mult,
                     signals=(signal("lat_ready"), 1) if t else None)
            for t in range(TT):
                k = job("latT", 2 * t)
                take(k, v.tensor_tensor, c_qT[:, :, wide(t * P, P)], bank(k)[:, 0:3 * P].rearrange("p (c t) -> p c t", c=3),
                     vecT[:, 80:83].unsqueeze(2).to_broadcast([P, 3, P]), ALU.mult)
                k = job("latT", 2 * t + 1)
                dve.wait_ge(*done(k))
                step(v.tensor_copy, k_peT[:, wide(t * P, P)], bank(k)[:, 2 * P:3 * P])
                step(v.tensor_tensor, c_kvT[:, :, wide(t * P, P)], bank(k)[:, 0:2 * P].rearrange("p (c t) -> p c t", c=2),
                     vecT[:, 83:85].unsqueeze(2).to_broadcast([P, 2, P]), ALU.mult, signals=emptied(k))
            for t in range(TT):
                k = job("q_pe", t)
                dve.wait_ge(*done(k))
                by_head = q_pe[:, t, :].rearrange("p (h d) -> p h d", h=MLA_HEADS)
                d2, one, two = rotate(by_head, bank(k).rearrange("p (h d) -> p h d", h=MLA_HEADS), t, MLA_HEADS, emptied(k))
                dve.wait_ge(dve_step, step.n)
                step(v.tensor_tensor, d2, one, two, ALU.add, signals=(signal("q_pe_ready"), t + 1))

            def mla_scaled(i, dst, src, taken):
                step(v.tensor_scalar, dst, src, (NOPE + ROPE) ** -0.5, None, ALU.mult, signals=taken)

            attention("mla", MLA_UNITS, mla_unit0, mla_scaled, lambda i: TT, lambda i: o_mla[:, i % TT, wide(i // TT * P, P)])

            for g in range(DIL_GROUPS):
                unit0 = dil_unit0 + g * DIL_UNITS

                def dil_biased(i, dst, src, taken):
                    hd, t = divmod(i, TT)
                    n = g * DIL_HEADS + hd
                    if t == 0:
                        dve.wait_ge(signal("bias_masked"), n + 1)
                    step(v.scalar_tensor_tensor, dst, src, DIL_D ** -0.5, bias_tile[:, n % 4, wide(t * S, S)], ALU.mult, ALU.add, signals=taken)

                attention(f"dil{g}_", DIL_UNITS, unit0, dil_biased, lambda i: TT, lambda i: o_dil[g][:, i % TT, wide(i // TT * P, P)])
            top = dil_top[:]
            stat = [wide(dil_unit0 + g * DIL_UNITS, DIL_UNITS) for g in range(DIL_GROUPS)]
            step(v.tensor_tensor, top, row_max[:, stat[0]], row_max[:, stat[1]], ALU.min)
            step(v.tensor_tensor, top, top, row_max[:, stat[2]], ALU.min)
            for g in range(DIL_GROUPS):
                step(v.tensor_tensor, dil_w[:, g, :], top, row_max[:, stat[g]], ALU.subtract, signals=(signal("dil_shift_ready"), 1) if g == 2 else None)
            dve.wait_ge(signal("dil_exp_ready"), 1)
            for g in range(DIL_GROUPS):
                step(v.tensor_tensor, dil_w[:, g, :], dil_w[:, g, :], row_sum[:, stat[g]], ALU.mult)
            step(v.tensor_tensor, top, dil_w[:, 0, :], dil_w[:, 1, :], ALU.add)
            step(v.tensor_tensor, top, top, dil_w[:, 2, :], ALU.add)
            step(v.reciprocal, top, top)
            for g in range(DIL_GROUPS):
                step(v.tensor_tensor, dil_w[:, g, :], dil_w[:, g, :], top, ALU.mult)

            def by_head(ap):
                return ap.rearrange("p (h d) -> p h d", h=DIL_HEADS)

            dve.wait_ge(signal("gates2_ready"), 1)
            for t in range(TT):
                for g in range(DIL_GROUPS):
                    w = dil_w[:, g, t:DIL_UNITS:TT].unsqueeze(2).to_broadcast([P, DIL_HEADS, DIL_D])
                    step(v.tensor_tensor, by_head(o_dil[g][:, t, :]), by_head(o_dil[g][:, t, :]), w, ALU.mult)
                for g in (1, 2):
                    step(v.tensor_tensor, o_dil[0][:, t, :], o_dil[0][:, t, :], o_dil[g][:, t, :], ALU.add)
                step(v.tensor_tensor, o_dil[0][:, t, :], o_dil[0][:, t, :], sig_b[:, t, :], ALU.mult)
                step(v.tensor_tensor, o_mla[:, t, :], o_mla[:, t, :], sig_a[:, t, :], ALU.mult)
                step(v.tensor_tensor, h[:, t, :], o_mla[:, t, :], o_dil[0][:, t, :], ALU.add, signals=(signal("mix_ready"), t + 1))
            for n in range(2):
                dve.wait_ge(*emptied(job("mod8", n)))
            for j in range(4):
                n, t = divmod(j, 2)
                cols, k = wide(n * BANK, BANK), job("w_out", j)
                take(k, v.tensor_tensor, junk[:, 0:BANK], bank(k), mod[:, 2, cols], ALU.mult)
                step(v.tensor_tensor, x[:, t, cols], x[:, t, cols], junk[:, 0:BANK], ALU.add, signals=(signal("x2_ready"), 1) if j == 3 else None)
            for unit in ("mod9", "mod10"):
                for n in range(2):
                    dve.wait_ge(*emptied(job(unit, n)))
            rms_modulated(2, params[:, 1, :], "h4_ready", 1)

            k = job("router2")
            dve.wait_ge(*done(k))
            step(v.tensor_copy, gates[:], bank(k)[:, 0:TT * E].rearrange("p (t e) -> p t e", t=TT), signals=emptied(k))
            step(v.tensor_reduce, top1[:], gates[:], AX, ALU.max)
            step(v.tensor_tensor, gates[:], gates[:], top1[:].unsqueeze(2).to_broadcast([P, TT, E]), ALU.subtract, signals=(signal("aff_logits_ready"), 1))
            dve.wait_ge(signal("aff_exp_ready"), 1)
            step(v.tensor_reduce, top1[:], gates[:], AX, ALU.add)
            step(v.reciprocal, top1[:], top1[:])
            step(v.tensor_tensor, gates[:], gates[:], top1[:].unsqueeze(2).to_broadcast([P, TT, E]), ALU.mult, signals=(signal("aff_ready"), 1))
            k = job("affT")
            take(k, v.tensor_copy, affT[:], bank(k)[0:E, 0:S])
            for i in range(CAP2 // 8):
                src, dst = (affT, topped) if i % 2 == 0 else (topped, affT)
                step(v.max, best8[:], src[:])
                step(v.match_replace, dst[:], best8[:], src[:], -1.0)
            step(v.tensor_scalar, affT[:], affT[:], 0.0, None, ALU.is_lt)
            step(v.memset, topped[:], 1.0)
            step(v.tensor_tensor_scan, rank_T[:], topped[:], affT[:], 0.0, ALU.mult, ALU.add)
            step(v.tensor_tensor, rank_T[:], rank_T[:], affT[:], ALU.mult, signals=(signal("rank_T_ready"), 1))
            k = job("rank2")
            take(k, v.tensor_copy, rank[:], bank(k)[:, 0:TT * E].rearrange("p (t e) -> p t e", t=TT))

            step(v.memset, y_sum, 0.0)
            with dve.Fori(0, EC_ROUNDS) as it:
                R = Rounds(it, job("ec"), EC_JOBS)
                step.begin_loop(it, 3)
                one_hots(step, it, CAP2, (signal("pick_ready"), it + (MOE_ROUNDS + 1)))
                for j in range(4):
                    dve.wait_ge(*R.done(EC_XE + j))
                    step(v.tensor_copy, x_e[:, 2 * j:2 * j + 2, 0:P], R.bank(EC_XE + j)[:, 0:2 * P].rearrange("p (c t) -> p c t", c=2), signals=R.emptied(EC_XE + j))
                for fp in range(2):
                    for b in range(2):
                        dve.wait_ge(*R.emptied(EC_GATE[fp] + b))
                        dve.wait_ge(*R.done(EC_UP[fp] + b))
                        if fp:
                            dve.wait_ge(*R.done(EC_T[0] + b))
                        step(v.tensor_tensor, hid[:, b, :], R.bank(EC_UP[fp] + b), silu_g[:, b, :], ALU.mult, signals=R.emptied(EC_UP[fp] + b))
                for n in range(2):
                    for t in range(TT):
                        j, cols = EC_SUM + 2 * n + t, wide(n * BANK, BANK)
                        dve.wait_ge(*R.done(j))
                        step(v.tensor_tensor, y_sum[:, t, cols], R.bank(j), y_sum[:, t, cols], ALU.add, signals=R.emptied(j))
                step.end_loop(EC_ROUNDS)
                step.last = None
            for j in range(4):
                dve.wait_ge(evacuated[(job("ec") + EC_SUM + j) % BANKS], (job("ec") + (EC_ROUNDS - 1) * EC_JOBS + EC_SUM + j) // BANKS + 1)
            for n in range(2):
                dve.wait_ge(*emptied(job("mod11", n)))
            for t in range(TT):
                step(v.tensor_tensor, y_sum[:, t, :], y_sum[:, t, :], mod[:, 2, :], ALU.mult)
                step(v.tensor_tensor, x[:, t, :], x[:, t, :], y_sum[:, t, :], ALU.add, signals=(signal("x3_ready"), 1) if t else None)
            dve.wait_ge(signal("rms2_ready"), 4)
            dve.wait_ge(signal("params_in"), 128)
            for t in range(TT):
                step(v.scalar_tensor_tensor, h[:, t, :], x[:, t, :], mv[:, t, 0:1], params[:, 0, :], ALU.mult, ALU.mult, signals=(signal("out_ready"), t + 1))


def constants():
    import numpy as np

    f = np.float32
    i = np.arange(128)
    ident = np.eye(128, dtype=f)
    tri = (i[:, None] <= i[None, :]).astype(f)
    mask = np.where(i[None, :] > i[:, None], f(-1e30), f(0)).astype(f)
    causal = np.concatenate([np.zeros((128, 128), f), mask], 1)
    seg_mask = np.ascontiguousarray(mask.T)
    ones = np.ones((128, 128), f)
    iota1 = np.broadcast_to(np.arange(1, 65, dtype=f), (128, 64))
    desc = np.broadcast_to(np.arange(16, 0, -1, dtype=f), (128, 16))
    freq = (f(10000.0) ** (-np.arange(0, 64, 2, dtype=f) / f(64))).astype(f)
    inv_freq = np.broadcast_to(freq, (128, 32))
    low = [0, 1, 2, 3, 4, 5, 6, 7] + [int(np.ceil(8 * 128 ** (j / 8) - 1e-9)) for j in range(8)]
    high = [n - 1 for n in low[1:]] + [low[-1] + (1 << 23)]
    table = [(-b, -a) for a, b in zip(low, high)] + [(max(a, 1), b) for a, b in zip(low, high)]
    buckets = np.tile(np.array([((a + b) / 2, (b - a) / 2) for a, b in table], f), (4, 1))
    eps = np.broadcast_to(np.array([1e-5, 1e-6], f), (128, 2))
    col = np.arange(32)
    select = ((i[:, None] // 64 == col // 16) & (i[:, None] % 32 == col % 16)).astype(f)
    return np.ascontiguousarray(np.concatenate([ident, tri, causal, seg_mask, ones, iota1, desc, inv_freq, buckets, eps, select], 1))


def band_masks():
    import numpy as np

    t, s = np.arange(256)[:, None], np.arange(256)[None, :]
    groups = [np.where(((t - s) % d == 0) & (abs(t - s) <= 64 * d), 0.0, -1e30) for d in (1, 4, 16)]
    return np.ascontiguousarray(np.stack(groups).astype(np.float32).reshape(3, 2, 128, 256).transpose(2, 0, 1, 3))


def kernel(**inputs):
    import concourse.bacc as bacc
    import numpy as np
    from concourse import mybir
    from concourse.bass_utils import run_bass_kernel_spmd

    nc = bacc.Bacc("TRN2", target_bir_lowering=False, num_devices=1)
    given = dict(inputs, consts=constants(), bands=band_masks())
    arrays, tensors = {}, {}
    for name, value in given.items():
        value = np.ascontiguousarray(value)
        arrays[f"in_{name}"] = value
        tensors[name] = nc.dram_tensor(f"in_{name}", value.shape, mybir.dt.from_np(value.dtype), kind="ExternalInput").ap()
    out = nc.dram_tensor("out", inputs["x"].shape, mybir.dt.float32, kind="ExternalOutput").ap()
    build_program(nc, tensors, out)
    done = run_bass_kernel_spmd(nc, [arrays], core_ids=[0])
    return done.results[0]["out"]
```

```python
def build_program(nc, A, out):
    from contextlib import ExitStack

    from concourse import bass, mybir

    F32 = mybir.dt.float32
    I32 = mybir.dt.int32
    ALU = mybir.AluOpType
    ACT = mybir.ActivationFunctionType
    AX = mybir.AxisListType.X

    P = 128
    S, D = A["x"].shape[1:]
    TT = S // P
    KC = D // P
    BANKS = 8
    BANK = 512
    SLOTS = 8
    SLOT = 2048
    HEADS, HD, GROUPS, STATE = 16, 64, 4, 128
    PER_GROUP = HEADS // GROUPS
    FOX_HEADS, FOX_D = 8, 64
    DIL_GROUPS, DIL_HEADS, DIL_D = 3, 8, 128
    MLA_HEADS, NOPE, ROPE = 8, 128, 64
    Q_RANK, KV_RANK = 384, 256
    E = 16
    QUADS = E // 4
    BUCKETS = 32
    ALPHA = 2 ** 0.25
    NEG = -1e30
    PI = 3.1415925
    TWO_PI = 6.283185307179586
    TWO_PI_HI = 6.28125
    MAGIC = 12582912.0

    ctx = ExitStack()
    with ctx:
        def sb(name, shape, dt=F32):
            return ctx.enter_context(nc.sbuf_tensor(name, shape, dt))

        def sem(name):
            return ctx.enter_context(nc.semaphore(name))

        ring = sb("ring", [P, SLOTS, SLOT])
        psum = ctx.enter_context(nc.psum_tensor("psum", [P, BANKS, BANK], F32))
        x = sb("x_tok", [P, TT, D])
        h = sb("h_tok", [P, TT, D])
        hT = sb("hT", [P, KC, S])
        mod = sb("mod", [P, 3, D])
        params = sb("params", [P, 2, D])
        consts = sb("consts", [P, A["consts"].shape[1]])
        vecT = sb("vecT", [P, P])
        ssd_w = sb("ssd_w", [P, KC])
        cact = sb("cact", [P, 2, KC])
        cond = sb("cond", [P, 2, KC, 64])
        mod_rows = sb("mod_rows", [P, BANK])
        UNITS = 12
        small_w = sb("small_w", [P, KC, 24])
        small_b = sb("small_b", [1, 24])
        head_v = sb("head_v", [P, 2, HEADS])
        stats = sb("stats", [P, TT, 2, 6])
        mv = sb("mv", [P, TT, 2])
        rstd = sb("rstd", [P, TT, 2])
        junk = sb("junk", [P, D])
        rows = junk[:, D - P:D]
        row_max = sb("row_max", [P, 80])
        row_sum = sb("row_sum", [P, 80])
        row_inv = sb("row_inv", [P, 80])
        prob = sb("prob", [P, 4, S])
        probT = sb("probT", [P, 4, S])
        pos_i = sb("pos_i", [P, TT], I32)
        turn = sb("turn", [P, 4, TT, ROPE // 2])
        table = sb("table", [P, P])
        affT, topped, rank_T = (probT[0:E, i, :] for i in range(3))
        best8 = sb("best8", [E, 8])
        WORK = 17968
        work = sb("work", [P, WORK])

        def view(at, *dims):
            n = 1
            for d in dims:
                n *= d
            assert at + n <= WORK, (at, dims)
            v = work[:, at:at + n]
            if len(dims) == 2:
                v = v.rearrange("p (a b) -> p a b", a=dims[0])
            elif len(dims) == 3:
                v = v.rearrange("p (a b c) -> p a b c", a=dims[0], b=dims[1])
            return v

        at = [0]

        def const(n):
            at[0] += n
            return consts[:, at[0] - n:at[0]]

        ident, tri, causal, seg_mask, ones = const(P), const(P), const(2 * P), const(P), const(P)
        iota1, desc, inv_freq, bucket_range, eps, select = const(64), const(E), const(ROPE // 2), const(2), const(2), const(32)
        ones_row = ones[0:1, :]
        eps5, eps6 = eps[:, 0:1], eps[:, 1:2]

        pe_done = sem("pe_done")
        evacuated = [sem(f"evacuated{b}") for b in range(BANKS)]
        weights_in = [sem(f"weights_in{s}") for s in range(SLOTS)]
        WIDE = 12
        expert_in = [sem(f"expert_in{s}") for s in range(WIDE)]
        more_slots = [*(work[:, 11776 + i * SLOT:11776 + (i + 1) * SLOT] for i in range(3)), hT[:].rearrange("p c t -> p (c t)")]
        act_step, dve_step = sem("act_step"), sem("dve_step")

        named = {}

        def signal(name):
            if name not in named:
                named[name] = sem(name)
            return named[name]

        first_job, n_jobs = {}, [0]

        def jobs(name, n):
            first_job[name] = n_jobs[0]
            n_jobs[0] += n

        def job(name, i=0):
            if name in first_job:
                return first_job[name] + i
            chunk = f"{name}_{i // 2}"
            return first_job[chunk] + i % 2 if chunk in first_job else first_job[f"{chunk}_{i % 2}"]

        def bank(k):
            return psum[:, k % BANKS, :]

        def done(k):
            return pe_done, k + 1

        def emptied(k):
            return evacuated[k % BANKS], k // BANKS + 1

        class Turn:

            def __init__(self, eng, own):
                self.eng, self.own, self.n, self.last = eng, own, 0, None
                self.it, self.per = None, 0

            def value(self):
                return self.n if self.it is None else self.n + self.it * self.per

            def __call__(self, op, *args, signals=None, **kw):
                if self.last is not None:
                    self.eng.wait_ge(*self.last)
                ins = op(*args, **kw)
                if signals is None:
                    self.n += 1
                    ins.then_inc(self.own, 1)
                    self.last = self.own, self.value()
                else:
                    ins.then_inc(signals[0], 1)
                    self.last = signals
                return ins

            def begin_loop(self, it, per, first=0):
                self.it, self.per, self.start = it - first if first else it, per, self.n
                self.last = self.own, self.value()

            def end_loop(self, rounds):
                assert self.n - self.start == self.per, (self.n - self.start, self.per)
                self.n, self.it = self.start + rounds * self.per, None
                self.last = self.own, self.n

        class Rounds:

            def __init__(self, it, job0, per_jobs, load0=0, per_loads=0, pe_done=pe_done, evacuated=evacuated, weights_in=expert_in):
                assert per_jobs % BANKS == 0 and per_loads % WIDE == 0
                self.it, self.job0, self.per_jobs, self.load0, self.per_loads = it, job0, per_jobs, load0, per_loads
                self.pe_done, self.evacuated, self.weights_in = pe_done, evacuated, weights_in

            def bank(self, j):
                return bank(self.job0 + j)

            def done(self, j):
                return self.pe_done, self.it * self.per_jobs + (self.job0 + j + 1)

            def emptied(self, j):
                k = self.job0 + j
                return self.evacuated[k % BANKS], self.it * (self.per_jobs // BANKS) + (k // BANKS + 1)

            def slot(self, i, dims):
                return expert_slot(self.load0 + i, dims)

            def arrived(self, i):
                n = self.load0 + i
                return self.weights_in[n % WIDE], self.it * (16 * self.per_loads // WIDE) + 16 * (n // WIDE + 1)


        loads = []

        def load(src, dims, reader):
            loads.append((src, dims, reader))
            return len(loads) - 1

        def slot(n, dims):
            a, b = dims
            return ring[:, n % SLOTS, 0:a * b].rearrange("p (a b) -> p a b", a=a)

        def expert_slot(n, dims):
            a, b = dims
            s = n % WIDE
            place = ring[:, s, :] if s < SLOTS else more_slots[s - SLOTS]
            return place[:, 0:a * b].rearrange("p (a b) -> p a b", a=a)

        def arrived(n):
            return weights_in[n % SLOTS], 16 * (n // SLOTS + 1)

        chunk_loads = {}

        def load_chunk(name, w, cols, reader, kc=KC):
            width = cols.stop - cols.start
            src = w.rearrange("(p c) n -> p c n", c=kc)
            pieces = []
            for c0 in range(0, kc, 4):
                c1 = min(c0 + 4, kc)
                pieces.append((load(src[:, c0:c1, cols], (c1 - c0, width), reader), c0, c1, width))
            chunk_loads[name] = pieces

        def wide(a, b):
            return slice(a, a + b)

        Z0, XBC0 = 0, D
        DT0 = XBC0 + D + 2 * GROUPS * STATE
        Q0 = DT0 + HEADS
        K0, V0 = Q0 + FOX_HEADS * FOX_D, Q0 + 2 * FOX_HEADS * FOX_D
        F0 = V0 + FOX_HEADS * FOX_D
        GS0 = F0 + FOX_HEADS
        GA0 = GS0 + D
        w_in = A["w_in"][0]
        w_mod, w_ada = A["w_mod"][0], A["w_ada_2"][0]

        def plan_unit(u):
            jobs(f"unit{u}", 1)
            load_unit(u)

        def load_unit(u):
            for n in range(2):
                load_chunk(f"unit{u}_{n}", (w_mod, w_ada)[u // 6], wide(u % 6 * D + n * BANK, BANK), job(f"unit{u}"))

        def plan_spread(*units):
            for u in units:
                jobs(f"mod{u}", 2)

        def plan_chunks(name, w, col0, n, units=()):
            for i in range(n):
                jobs(f"{name}_{i}", 2)
                load_chunk(f"{name}_{i}", w, wide(col0 + i * BANK, BANK), job(name, 2 * i + 1))
                if i < len(units):
                    plan_unit(units[i])

        LAG_T, LAG_PV = 2, 3

        def chunk_fills(name, w, col0, n):
            return [("chunk", name, i, half, w, col0) for i in range(n) for half in range(2)]

        def fill_span(f, fills, n):
            first = f * n // len(fills)
            return first, min(first + 2, (f + 1) * n // len(fills))

        def plan_attention(name, n, fills):
            ends = {fill_span(f, fills, n)[1] - 1: fill for f, fill in enumerate(fills)}
            for i in range(n + LAG_PV):
                if i < n:
                    jobs(f"{name}_qk{i}", 1)
                if 0 <= i - LAG_T < n:
                    jobs(f"{name}_t{i - LAG_T}", 1)
                if 0 <= i - LAG_PV < n:
                    jobs(f"{name}_pv{i - LAG_PV}", 1)
                if i in ends and ends[i][0] == "unit":
                    jobs(f"unit{ends[i][1]}", 1)
                elif i in ends:
                    jobs("{1}_{2}_{3}".format(*ends[i]), 1)
            for fill in fills:
                if fill[0] == "unit":
                    load_unit(fill[1])
                elif fill[3] == 0:
                    _, nm, c, _, w, col0 = fill
                    load_chunk(f"{nm}_{c}", w, wide(col0 + c * BANK, BANK), job(nm, 2 * c + 1))

        BIAS_ROUNDS, BIAS_STEPS, BIAS_QUERIES = 4, 4, 4
        IN_UNITS = dict(xbc=(2, 3, 4, 5), q=(6,), k=(7,), v=(8,), z=(9,))
        jobs("bias", BIAS_ROUNDS * BANKS)
        plan_unit(0)
        plan_unit(1)
        jobs("vecT", 1)
        plan_spread(0, 1)
        jobs("hT", 4)
        plan_chunks("xbc", w_in, XBC0, 4, IN_UNITS["xbc"])
        jobs("dtf", 1)
        for name, col0, n in (("q", Q0, 1), ("k", K0, 1), ("v", V0, 1), ("z", Z0, 2)):
            plan_chunks(name, w_in, col0, n, IN_UNITS[name])
        jobs("cumsum", 1)
        plan_spread(2, 3, 4)
        gs_fills = chunk_fills("gs", w_in, GS0, 2)

        def plan_gs(j):
            _, nm, c, half, w, col0 = gs_fills[j]
            jobs(f"{nm}_{c}_{half}", 1)

        jobs("xs_tok", 4)
        jobs("b_tok", 1)
        jobs("cb", TT)
        for k in range(3):
            jobs(f"a_row{k}", 1)
        jobs("state", 2)
        plan_gs(0)
        jobs("y_off", 2)
        for m in range(2 * TT):
            jobs(f"y_diag{m}", 1)
            for k in range(3 + 2 * m, min(5 + 2 * m, TT * GROUPS)):
                jobs(f"a_row{k}", 1)
            if m < 3:
                plan_gs(m + 1)
        for c in range(2):
            load_chunk(f"gs_{c}", w_in, wide(GS0 + c * BANK, BANK), job("gs", 2 * c + 1))
        FOX_UNITS = FOX_HEADS * TT
        ga_fills = chunk_fills("ga", w_in, GA0, 2)
        fox_fills = [ga_fills[0], ga_fills[1], ("unit", 10), ga_fills[2], ga_fills[3], ("unit", 11)]
        plan_attention("fox", FOX_UNITS, fox_fills)
        jobs("yT", 4)
        jobs("oT", 2)
        jobs("merge", 8)
        for n in range(2):
            load_chunk(f"ssd_o_{n}", A["w_ssd_o"][0], wide(n * BANK, BANK), job("merge", 4 * n + 2))
            load_chunk(f"att_o_{n}", A["w_att_o"][0], wide(n * BANK, BANK), job("merge", 4 * n + 3), kc=4)
        jobs("mT", 4)
        plan_chunks("w_o", A["w_o"][0], 0, 2)
        jobs("h2T", 4)
        jobs("router", 1)
        plan_spread(5, 6, 7)
        jobs("rank", 1)

        CAP, FF = 64, A["w_gate"].shape[-1]
        MOE_ROUNDS, MOE_JOBS, MOE_LOADS = QUADS, 24, 24
        MORE_ROUNDS = (S // CAP - 1) * QUADS
        more_sems = dict(pe_done=sem("more_pe_done"), evacuated=[sem(f"more_evacuated{b}") for b in range(BANKS)],
                         weights_in=[sem(f"more_weights_in{s}") for s in range(WIDE)])
        overflow = sb("overflow", [P, 1], I32)

        def more_tokens(eng):
            eng.wait_ge(signal("overflow_known"), 1)
            return eng.If(eng.value_load(overflow[0:1, 0:1], min_val=0, max_val=1) > 0)

        MOE_GW, MOE_GATE, MOE_UP, MOE_XE, MOE_T, MOE_DOWN, MOE_SUM = 0, (2, 4), (3, 5), 6, (10, 13), (11, 14), (16, 20)
        jobs("moe_first", KC)
        jobs("moe", MOE_ROUNDS * MOE_JOBS)
        moe_load0 = len(loads)
        w_gate, w_up, w_down = A["w_gate"][0], A["w_up"][0], A["w_down"][0]
        moe_loads = []
        for p in range(2):
            for w, reader in ((w_gate, MOE_GATE[p]), (w_up, MOE_UP[p])):
                for c0 in (0, 4):
                    for i in range(2):
                        moe_loads.append((w.rearrange("e (p c) f -> e p c f", c=KC)[:, :, c0:c0 + 4, :], 2 * p + i, (4, FF), reader))
        for p in range(2):
            for c0 in (0, 2):
                for i in range(2):
                    moe_loads.append((w_down.rearrange("e (c p) n -> e p c n", p=P)[:, :, c0:c0 + 2, :], 2 * p + i, (2, D), MOE_DOWN[p] + 1))
        assert len(moe_loads) == MOE_LOADS

        w_in2 = A["w_in_2"][0]
        LAT = Q_RANK + KV_RANK + ROPE
        DIL0 = LAT
        GATE0 = DIL0 + DIL_GROUPS * 3 * DIL_HEADS * DIL_D
        jobs("h3T", 4)
        jobs("lat", 4)
        load_chunk("lat_0", w_in2, wide(0, BANK), job("lat", 1))
        load_chunk("lat_1", w_in2, wide(BANK, LAT - BANK), job("lat", 3))
        jobs("latT", 4)
        jobs("q_nope", 4)
        jobs("q_pe", 2)
        q_loads = [load(A["w_uq_2"][0].rearrange("(c p) n -> p c n", p=P)[:, :, wide(i * 384, 384)], (3, 384), job("q_pe", 1)) for i in range(4)]
        jobs("k_nope", 4)
        jobs("v_mla", 4)
        kv_loads = [load(A["w_ukv_2"][0].rearrange("(c p) n -> p c n", p=P)[:, :, wide(i * 1024, 1024)], (2, 1024), job("v_mla", 2 * i + 1)) for i in range(2)]
        jobs("q_peT", 2)
        MLA_UNITS = MLA_HEADS * TT
        DIL_UNITS = DIL_HEADS * TT

        def dil_col(g, i):
            return DIL0 + (3 * g + i) * DIL_HEADS * DIL_D

        def next_fills(g):
            if g == DIL_GROUPS:
                return chunk_fills("gates2", w_in2, GATE0, 4)
            return chunk_fills(f"dil_q{g}", w_in2, dil_col(g, 0), 2) + chunk_fills(f"dil_k{g}", w_in2, dil_col(g, 1), 2)

        plan_attention("mla", MLA_UNITS, next_fills(0))
        for g in range(DIL_GROUPS):
            plan_chunks(f"dil_v{g}", w_in2, dil_col(g, 2), 2)
            plan_attention(f"dil{g}_", DIL_UNITS, next_fills(g + 1))
        plan_spread(8, 9, 10)
        jobs("mixT", 4)
        plan_chunks("w_out", A["w_out_2"][0], 0, 2)
        plan_spread(11)
        jobs("h4T", 4)
        jobs("router2", 1)
        jobs("affT", 1)
        jobs("rank2", 1)

        CAP2, FF2 = 2 * S // E, A["w_gate_2"].shape[-1]
        assert CAP2 * 4 == P
        EC_ROUNDS, EC_JOBS, EC_LOADS = QUADS, 24, 96
        EC_GW, EC_GATE, EC_UP, EC_XE, EC_T, EC_DOWN, EC_SUM = 0, (2, 8), (4, 10), 12, (6, 16), 18, 20
        jobs("ec_first", KC)
        jobs("ec", EC_ROUNDS * EC_JOBS)
        ec_load0 = len(loads)
        w_gate2, w_up2, w_down2 = A["w_gate_2"][0], A["w_up_2"][0], A["w_down_2"][0]
        ec_loads, EC_PIECES = [], 0

        def plan_pieces(n, src_of, dims, last_job):
            nonlocal EC_PIECES
            for i in range(n):
                reader = last_job if i == n - 1 else ("piece", EC_PIECES)
                EC_PIECES += i < n - 1
                ec_loads.extend((src_of(i), e, dims, reader) for e in range(4))

        for fp in range(2):
            for w, last_job in ((w_gate2, EC_GATE[fp] + 1), (w_up2, EC_UP[fp] + 1)):
                rows_first = w.rearrange("e (p c) f -> e p c f", c=KC)[:, :, :, wide(fp * 1024, 1024)]
                plan_pieces(KC // 2, lambda i: rows_first[:, :, 2 * i:2 * i + 2, :], (2, 1024), last_job)
        chunks_first = w_down2.rearrange("e (c p) n -> e p c n", p=P)
        plan_pieces(FF2 // P // 2, lambda i: chunks_first[:, :, 2 * i:2 * i + 2, :], (2, D), EC_DOWN + 1)
        assert len(ec_loads) == EC_LOADS

        pieces_used = sem("pieces_used")

        block = ctx.enter_context(nc.Block())

        one_hot = [view(i * BIAS_QUERIES * S, BIAS_QUERIES, S) for i in range(BIAS_STEPS)]
        staged = [view(at, BIAS_QUERIES * S) for at in (4096, 5120, 14384, 15408)]
        pos_rows = junk[:, 512:512 + S + S // 4].bitcast(I32)
        pos_all, pos_quarter = junk[:, 0:S], junk[:, S:S + S // 4]
        bias_dram = nc.dram_tensor("bias_dram", [DIL_GROUPS * DIL_HEADS, S, S], F32, kind="Internal").ap()
        BIAS_STORES = 16 * 4
        bias_stored = [sem(f"bias_stored{i}") for i in range(BIAS_STEPS)]
        bias_in = [sem(f"bias_in{i}") for i in range(4)]
        mla_unit0, dil_unit0 = FOX_UNITS, FOX_UNITS + MLA_UNITS

        lat = view(0, TT, LAT)
        c_qT, c_kvT = view(1408, 3, S), view(2176, 2, S)
        q_nopeT, k_nopeT = view(2688, MLA_HEADS, S), view(4736, MLA_HEADS, S)
        v_mla = view(6784, TT, MLA_HEADS * NOPE)
        q_pe = view(8832, TT, MLA_HEADS * ROPE)
        k_pe = view(9856, TT, 2 * ROPE)
        q_peT, k_peT = view(10112, MLA_HEADS // 2, S), view(11136, S)
        rope_tmp = view(11392, 2, MLA_HEADS * ROPE // 2)
        o_mla = h
        q_dilT = [view(at, DIL_HEADS, S) for at in (15872, 0, 15872)]
        k_dilT = [mod[:, 0:2, :].rearrange("p a d -> p (a d)").rearrange("p (h s) -> p h s", h=DIL_HEADS), view(2048, DIL_HEADS, S)]
        k_dilT.append(k_dilT[0])
        v_dil = view(4096, TT, DIL_HEADS * DIL_D)
        o_dil = [view(6144 + 2048 * g, TT, D) for g in range(DIL_GROUPS)]
        bias_tile = view(12288, 4, TT * S)
        dil_w = table[:, 0:DIL_GROUPS * TT * DIL_HEADS].rearrange("p (g u) -> p g u", g=DIL_GROUPS)
        mix_gain = probT[:].rearrange("p a b -> p (a b)")
        bands = view(14336, DIL_GROUPS, TT * S)
        sig_a, sig_b = view(0, TT, D), view(2048, TT, D)

        pick, pick_gate = view(0, TT, 4 * 64), view(512, TT, 4 * 64)
        gate_T = view(1024, 2, S)
        x_e = view(1536, KC, 4 * 64)
        silu_g, hid = view(3584, 2, BANK), view(4608, 2, BANK)
        hidT = view(5632, 16, P)
        y_e = view(7680, 2, D)
        y_sum = view(9728, TT, D)

        @block.sync
        def _(sp):
            def fetch_rounds(rounds, todo, job0, per_jobs, free, pe_done=pe_done, weights_in=expert_in):
                per = len(todo)

                def fetch_expert(i, quad, used):
                    which, used = used
                    src, e, dims, _ = todo[i % per]
                    if not isinstance(quad, int):
                        used = sp.lower_val(sp.snap(used))
                    sp.dma_start(expert_slot(i, dims), src[quad * 4 + e]).wait_op(which, used, "sem-ge").then_inc(weights_in[i % WIDE], 16)

                def used(i, it):
                    reader = todo[i - WIDE][3]
                    if isinstance(reader, tuple):
                        return pieces_used, it * EC_PIECES + (reader[1] + 1)
                    return pe_done, it * per_jobs + (job0 + reader + 1)

                for i in range(WIDE):
                    fetch_expert(i, 0, free[i])
                with sp.Fori(0, rounds - 1) as it:
                    for i in range(WIDE, per):
                        fetch_expert(i, quad_of(it), used(i, it))
                    for i in range(per, per + WIDE):
                        fetch_expert(i, quad_of(it + 1), used(i, it))
                for i in range(WIDE, per):
                    fetch_expert(i, (rounds - 1) % QUADS, used(i, rounds - 1))

            def quad_of(it):
                return it & (QUADS - 1)

            def fetch_run(first, end):
                for n in range(first, end):
                    src, dims, _ = loads[n]
                    if moe_load0 <= n < moe_load0 + SLOTS:
                        reader = moe_loads[MOE_LOADS - WIDE + n % SLOTS][3]
                        sp.wait_ge(*done(job("moe", (MOE_ROUNDS - 1) * MOE_JOBS + reader)))
                    elif n >= SLOTS:
                        sp.wait_ge(*done(loads[n - SLOTS][2]))
                    sp.dma_start(slot(n, dims), src).then_inc(weights_in[n % SLOTS], 16)

            def ring_free(end):
                return [done(next(loads[n][2] for n in range(end - 1, -1, -1) if n % SLOTS == s)) for s in range(SLOTS)]

            sp.wait_ge(signal("zeros_ready"), 1)
            for q in range(4):
                sp.dma_start(table[wide(q * BUCKETS, BUCKETS), wide(q * BUCKETS, DIL_GROUPS * DIL_HEADS)], A["rel_bias_2"]).then_inc(signal("table_in"), 16)
            sp.wait_ge(signal("const_in"), 16)
            sp.wait_ge(signal("pos_in"), 80)
            sp.dma_start(x[:], A["x"][0].rearrange("(t p) d -> p t d", p=P)).then_inc(signal("x_in"), 16)
            fetch_run(0, SLOTS // 2)

            def store_bias(first, end):
                with sp.Fori(first, end) as it:
                    R = Rounds(it, job("bias"), BANKS)
                    for n in range(BIAS_STEPS):
                        for j in range(2):
                            sp.wait_ge(*R.emptied(2 * n + j))
                        for q in range(4):
                            queries = bass.ds(it * (BIAS_STEPS * BIAS_QUERIES) + (q * (S // 4) + n * BIAS_QUERIES), BIAS_QUERIES)
                            sp.dma_start(bias_dram[:, queries, :], staged[n][wide(q * 32, DIL_GROUPS * DIL_HEADS), :].rearrange("p (q s) -> p q s", s=S)).then_inc(bias_stored[n], 16)

            store_bias(0, 1)
            fetch_run(SLOTS // 2, SLOTS - 2)
            store_bias(1, 2)
            fetch_run(SLOTS - 2, SLOTS)
            store_bias(2, BIAS_ROUNDS)
            fetch_run(SLOTS, moe_load0)
            fetch_rounds(MOE_ROUNDS, moe_loads, job("moe"), MOE_JOBS, ring_free(moe_load0) + 3 * [done(job("merge", 7))] + [done(job("router"))])
            with more_tokens(sp):
                fetch_rounds(MORE_ROUNDS, moe_loads, KC, MOE_JOBS, WIDE * [done(job("moe", MOE_ROUNDS * MOE_JOBS - 1))],
                             more_sems["pe_done"], more_sems["weights_in"])
                sp.wait_ge(more_sems["pe_done"], KC + MORE_ROUNDS * MOE_JOBS)
            fetch_run(moe_load0, ec_load0)
            fetch_rounds(EC_ROUNDS, ec_loads, job("ec"), EC_JOBS, ring_free(ec_load0) + 3 * [(signal("mix_ready"), TT)] + [done(job("router2"))])
            for t in range(TT):
                sp.wait_ge(signal("out_ready"), t + 1)
                sp.dma_start(out[0, wide(t * P, P), :], h[:, t, :]).then_inc(signal("out_stored"), 16)
            sp.wait_ge(signal("out_stored"), 16 * TT)

        @block.gpsimd
        def _(pool):
            def distances(it, n):
                if not isinstance(it, int):
                    pool.wait_ge(pe_done, it * BANKS + (job("bias") - BANKS + 2 * n + 2))
                queries = pos_quarter[:, bass.ds(it * (BIAS_STEPS * BIAS_QUERIES) + n * BIAS_QUERIES, BIAS_QUERIES)]
                nc.gpsimd.tensor_tensor(one_hot[n], pos_all.unsqueeze(1).to_broadcast([P, BIAS_QUERIES, S]), queries.unsqueeze(2).to_broadcast([P, BIAS_QUERIES, S]),
                                        ALU.subtract).then_inc(signal("distance_ready"), 1)

            pool.wait_ge(signal("positions_ready"), 1)
            for n in range(BIAS_STEPS):
                distances(0, n)
            with pool.Fori(1, BIAS_ROUNDS) as it:
                for n in range(BIAS_STEPS):
                    distances(it, n)
            pool.wait_ge(signal("zeros_ready"), 1)
            for b, name in enumerate(("b_mod", "b_ada_2")):
                halves = A[name][0].rearrange("(u n k) -> n u k", n=2, k=BANK)
                for n in range(2):
                    pool.dma_start(mod_rows[wide(64 * n + 6 * b, 6), :], halves[n]).then_inc(signal("mod_bias_in"), 16)
            with nc.allow_non_contiguous_dma(reason="256 numbers"):
                pool.dma_start(pos_i[:], A["positions_2"][0].rearrange("(t p) -> p t", p=P)).then_inc(signal("pos_tok_in"), 16)
            pool.dma_start(rows[0:64, :], A["conv_w"][0].rearrange("j (t p) -> (j t) p", p=P)).then_inc(signal("rows_in"), 16)
            pool.dma_start(rows[64:80, :], A["conv_b"][0].rearrange("(t p) -> t p", p=P)).then_inc(signal("rows_in"), 16)
            pool.dma_start(rows[80:83, :], A["g_q_lat_2"][0].rearrange("(t p) -> t p", p=P)).then_inc(signal("rows_in"), 16)
            pool.dma_start(rows[83:85, :], A["g_kv_lat_2"][0].rearrange("(t p) -> t p", p=P)).then_inc(signal("rows_in"), 16)
            with nc.allow_non_contiguous_dma(reason="24 columns"):
                pool.dma_start(small_w[:, :, 0:HEADS], w_in.rearrange("(p c) n -> p c n", c=KC)[:, :, wide(DT0, HEADS)]).then_inc(signal("dtf_in"), 16)
                pool.dma_start(small_w[:, :, HEADS:24], w_in.rearrange("(p c) n -> p c n", c=KC)[:, :, wide(F0, FOX_HEADS)]).then_inc(signal("dtf_in"), 16)
            pool.dma_start(small_b[:, 0:HEADS], A["dt_bias"]).then_inc(signal("dtf_in"), 16)
            pool.dma_start(small_b[:, HEADS:24], A["forget_b"]).then_inc(signal("dtf_in"), 16)
            pool.dma_start(head_v[:, 0, :], A["a_log"].to_broadcast([P, HEADS])).then_inc(signal("head_in"), 16)
            pool.dma_start(head_v[:, 1, :], A["d_skip"].to_broadcast([P, HEADS])).then_inc(signal("head_in"), 16)
            pool.dma_start(ssd_w[:], A["ssd_norm_w"][0].rearrange("(p c) -> p c", c=KC)).then_inc(signal("ssd_w_in"), 16)

            pool.wait_ge(signal("y_ssd_ready"), 2)
            pool.dma_start(params[:, 0, :], A["ln1_g"].to_broadcast([P, D])).then_inc(signal("params_in"), 16)
            pool.dma_start(params[:, 1, :], A["ln1_b"].to_broadcast([P, D])).then_inc(signal("params_in"), 16)
            with nc.allow_non_contiguous_dma(reason="20 columns"):
                pool.dma_start(small_w[:, :, 0:4], A["w_router_group"][0].rearrange("(p c) n -> p c n", c=KC)).then_inc(signal("router_in"), 16)
                pool.dma_start(small_w[:, :, 4:20], A["w_router_expert"][0].rearrange("(p c) n -> p c n", c=KC)).then_inc(signal("router_in"), 16)
            pool.dma_start(small_b[:, 0:4], A["b_router_group"]).then_inc(signal("router_in"), 16)
            pool.dma_start(small_b[:, 4:20], A["b_router_expert"]).then_inc(signal("router_in"), 16)

            def two_rows(ready, value, first, second):
                pool.wait_ge(signal(ready), value)
                for i, name in enumerate((first, second)):
                    row = A[name] if len(A[name].shape) == 2 else A[name].unsqueeze(0)
                    pool.dma_start(params[:, i, :], row.to_broadcast([P, D])).then_inc(signal("params_in"), 16)

            two_rows("x_mid_ready", 1, "ln2_g", "ln2_b")
            pool.dma_start(mix_gain, A["g_norm_mix_2"].to_broadcast([P, D])).then_inc(signal("mix_gain_in"), 16)
            two_rows("x_b1_ready", TT, "g_norm_ffn_2", "g_final_2")
            pool.dma_start(bands[:], A["bands"].rearrange("p g t s -> p g (t s)")).then_inc(signal("bands_in"), 16)
            for stored in bias_stored:
                pool.wait_ge(stored, BIAS_ROUNDS * BIAS_STORES)
            pool.wait_ge(signal("bands_in"), 16)

            def mask_bias(n):
                pool.wait_ge(bias_in[n % 4], 16 * (n // 4 + 1))
                nc.gpsimd.tensor_tensor(bias_tile[:, n % 4, :], bias_tile[:, n % 4, :], bands[:, n // DIL_HEADS, :], ALU.add).then_inc(signal("bias_masked"), 1)

            for n in range(DIL_GROUPS * DIL_HEADS):
                if n >= 4:
                    pool.wait_ge(signal("max_ready"), dil_unit0 + (n - 3) * TT)
                pool.dma_start(bias_tile[:, n % 4, :].rearrange("p (t s) -> p t s", t=TT), bias_dram[n].rearrange("(t p) s -> p t s", p=P)).then_inc(bias_in[n % 4], 16)
                if n:
                    mask_bias(n - 1)
            mask_bias(DIL_GROUPS * DIL_HEADS - 1)
            with nc.allow_non_contiguous_dma(reason="16 columns"):
                pool.dma_start(small_w[:, :, 0:E], A["w_router_2"][0].rearrange("(p c) n -> p c n", c=KC)).then_inc(signal("router2_in"), 16)
            for t in range(TT):
                pool.wait_ge(signal("gate_a_ready"), t + 1)
                nc.gpsimd.tensor_tensor(o_mla[:, t, :], o_mla[:, t, :], sig_a[:, t, :], ALU.mult).then_inc(signal("mla_gated"), 1)

        silu_z, sig_gs, sig_ga = view(0, TT, D), view(2048, TT, D), view(4096, TT, D)
        sig_both = view(2048, 2 * TT * D)
        u_pad = view(6144, 16, S + 3)
        xcT = view(10288, 16, S)
        qT, kT, v_tok = view(14384, 4, S), view(15408, 4, S), view(16432, TT, 512)
        b_tok = view(17456, GROUPS, STATE)
        xs_tok, xdt = view(6144, TT, D), view(8192, TT, D)
        x_end, prev = view(10288, D), view(11312, D)
        o_fox = view(10288, TT, 512)
        cb = junk[:].rearrange("p (t g l) -> p t g l", t=TT, g=GROUPS)
        decay = [prob[:, 0:2, :].rearrange("p a b -> p (a b)"), prob[:, 2:4, :].rearrange("p a b -> p (a b)"),
                 probT[:, 0:2, :].rearrange("p a b -> p (a b)")]
        y_tok = h
        dtf = sb("dtf", [P, TT, 24])
        dtf_e = sb("dtf_e", [P, TT, 24])
        cum_in = sb("cum_in", [P, TT, 24])
        a_cs = sb("a_cs", [P, TT, HEADS])
        neg_F = sb("neg_F", [P, TT, FOX_HEADS])
        a_exp = sb("a_exp", [P, 2, HEADS])

        ATT_BUF = 4
        oT = view(14384, 4, S)
        square_junk = prob[:].rearrange("p a b -> p (a b)")
        mv2 = sb("mv2", [P, TT, 2])
        posf = sb("posf", [P, TT])
        dil_top, dil_sum = sb("dil_top", [P, DIL_UNITS]), sb("dil_sum", [P, DIL_UNITS])
        pass_shift = sb("pass_shift", [P, QUADS])
        chosen = sb("chosen", [P, TT, E])
        gates = sb("gates", [P, TT, E])
        rank = sb("rank", [P, TT, E])
        logits, in_group = sb("logits", [P, TT, 20]), sb("in_group", [P, TT, E])
        hot_g, hot1, hot2, e_in = sb("hot_g", [P, TT, 4]), sb("hot1", [P, TT, 4]), sb("hot2", [P, TT, 4]), sb("e_in", [P, TT, 4])
        route_g, route_2, route_top = sb("route_g", [P, TT, 4]), sb("route_2", [P, TT]), sb("route_top", [P, TT])
        top1, top2 = sb("top1", [P, TT]), sb("top2", [P, TT])

        @block.tensor
        def _(pe):
            next_job = [0]

            def begin(k):
                assert k == next_job[0], (k, next_job[0], [n for n, v in first_job.items() if v <= k][-1])
                next_job[0] += 1
                if k >= BANKS:
                    pe.wait_ge(*emptied(k - BANKS))
                return bank(k)

            def end(mm):
                mm.then_inc(pe_done, 1)

            def claim(k):
                assert next_job[0] <= k < next_job[0] + BANKS
                if k >= BANKS:
                    pe.wait_ge(*emptied(k - BANKS))
                return bank(k)

            def finish(k, mm):
                assert k == next_job[0]
                next_job[0] += 1
                end(mm)

            def in_one(steps):
                for _ in steps:
                    pass

            def pieces(name):
                for n, c0, c1, width in chunk_loads[name]:
                    pe.wait_ge(*arrived(n))
                    for c in range(c0, c1):
                        yield c, slot(n, (c1 - c0, width))[:, c - c0, :]

            def chunks(name):
                return [(c, slot(n, (c1 - c0, width))[:, c - c0, :]) for n, c0, c1, width in chunk_loads[name] for c in range(c0, c1)]

            units_done = []

            def modulation(u):
                k = job(f"unit{u}")
                pe.wait_ge(signal("cond_ready"), 1)
                o = claim(k)
                weights = [dict(pieces(f"unit{u}_{n}")) for n in range(2)]
                for c in range(KC // 2):
                    for n in range(2):
                        for half in range(2):
                            mm = pe.matmul(o[wide(64 * n + 32 * half, 32), :], cond[:, u // 6, half * (KC // 2) + c, 31 - u:63 - u], weights[n][half * (KC // 2) + c],
                                           start=(c == 0), stop=(c == KC // 2 - 1))
                            if c < KC // 2 - 1 or n == 0 or half == 0:
                                yield
                units_done.append(u)
                finish(k, mm)

            def spread(*units):
                for u in units:
                    pe.wait_ge(*emptied(job(f"unit{units_done[-1]}")))
                    for n in range(2):
                        o = begin(job(f"mod{u}", n))
                        end(pe.matmul(o, select[:, n * 16 + u:n * 16 + u + 1].to_broadcast([P, P]), mod_rows[:], start=True, stop=True))

            def transpose_tokens(name, src, ready):
                for t in range(TT):
                    pe.wait_ge(signal(ready), t + 1)
                    for c0 in range(0, KC, 4):
                        o = begin(job(name, t * 2 + c0 // 4))
                        for c in range(c0, c0 + 4):
                            mm = pe.transpose(o[:, wide((c - c0) * P, P)], src[:, t, c::KC], ident)
                        end(mm)

            def channel_job(name, i, half, actT):
                k = job(name, 2 * i + half)
                o = claim(k)
                for j in range(2):
                    ch = wide((2 * half + j) * P, P)
                    for c, w in pieces(f"{name}_{i}") if half == j == 0 else chunks(f"{name}_{i}"):
                        mm = pe.matmul(o[:, wide(j * S, S)], w[:, ch], actT[:, c, :], start=(c == 0), stop=(c == KC - 1))
                        if j == 0 or c < KC - 1:
                            yield
                finish(k, mm)

            def token_job(name, i, t, actT):
                k = job(name, 2 * i + t)
                o = claim(k)
                for c, w in pieces(f"{name}_{i}") if t == 0 else chunks(f"{name}_{i}"):
                    mm = pe.matmul(o, actT[:, c, wide(t * P, P)], w, start=(c == 0), stop=(c == KC - 1))
                    if c < KC - 1:
                        yield
                finish(k, mm)

            def channel_major(name, n, actT, units=()):
                for i in range(n):
                    for half in range(2):
                        in_one(channel_job(name, i, half, actT))
                    if i < len(units):
                        in_one(modulation(units[i]))

            def token_major(name, n, actT, units=()):
                for i in range(n):
                    for t in range(TT):
                        in_one(token_job(name, i, t, actT))
                    if i < len(units):
                        in_one(modulation(units[i]))

            def fill_job(fill):
                if fill[0] == "unit":
                    return modulation(fill[1]), 2 * KC
                _, name, i, half, _, _ = fill
                if name.startswith("dil"):
                    return channel_job(name, i, half, hT), 2 * KC
                return token_job(name, i, half, hT), KC

            def attention(name, n, unit0, scores, values, keys, fills):
                shares = {}
                for f, fill in enumerate(fills):
                    first, end_ = fill_span(f, fills, n)
                    steps, count = fill_job(fill)
                    parts = 3 * (end_ - first)
                    for part in range(parts):
                        shares[3 * first + part] = steps, count * (part + 1) // parts - count * part // parts

                def share(part):
                    steps, count = shares.get(part, ((), 0))
                    for _ in range(count):
                        next(steps, None)

                for i in range(n + LAG_PV):
                    if i < n:
                        o = begin(job(f"{name}_qk{i}"))
                        end(scores(o, i))
                    share(3 * i)
                    if 0 <= (j := i - LAG_T) < n:
                        o = begin(job(f"{name}_t{j}"))
                        pe.wait_ge(signal("probs_ready"), unit0 + j + 1)
                        for t in range(keys(j)):
                            mm = pe.transpose(o[:, wide(t * P, P)], prob[:, (unit0 + j) % ATT_BUF, wide(t * P, P)], ident)
                        end(mm)
                    share(3 * i + 1)
                    if 0 <= (j := i - LAG_PV) < n:
                        o = begin(job(f"{name}_pv{j}"))
                        pe.wait_ge(*emptied(job(f"{name}_t{j}")))
                        end(values(o, j))
                    share(3 * i + 2)

            def bias_round(it):
                R = Rounds(it, job("bias"), BANKS)
                for j in range(BANKS):
                    k = job("bias", j)
                    if j % 2 == 0:
                        pe.wait_ge(signal("one_hot_ready"), it * BIAS_STEPS + (j // 2 + 1))
                    if not isinstance(it, int) or k >= BANKS:
                        pe.wait_ge(evacuated[k % BANKS], it + k // BANKS)
                    end(pe.matmul(R.bank(j), table[:], one_hot[j // 2][:, wide(j % 2 * 2, 2), :], start=True, stop=True))

            pe.wait_ge(signal("table_in"), 64)
            bias_round(0)
            with pe.Fori(1, BIAS_ROUNDS) as it:
                bias_round(it)
            next_job[0] += BIAS_ROUNDS * BANKS

            in_one(modulation(0))
            in_one(modulation(1))
            pe.wait_ge(signal("const_in"), 16)
            pe.wait_ge(signal("rows_in"), 64)
            o = begin(job("vecT"))
            end(pe.transpose(o[:, 0:85], rows[0:85, :], ident[0:85, 0:85]))
            spread(0, 1)

            transpose_tokens("hT", h, "h_ready")

            for k in range(4):
                pe.wait_ge(*emptied(job("hT", k)))
            channel_major("xbc", 4, hT, IN_UNITS["xbc"])
            pe.wait_ge(signal("dtf_in"), 64)
            o = begin(job("dtf"))
            for t in range(TT):
                pe.matmul(o[:, wide(t * 24, 24)], ones_row, small_b[0:1, :], start=True, stop=False)
                for c in range(KC):
                    mm = pe.matmul(o[:, wide(t * 24, 24)], hT[:, c, wide(t * P, P)], small_w[:, c, :], start=False, stop=(c == KC - 1))
            end(mm)
            channel_major("q", 1, hT, IN_UNITS["q"])
            channel_major("k", 1, hT, IN_UNITS["k"])
            token_major("v", 1, hT, IN_UNITS["v"])
            token_major("z", 2, hT, IN_UNITS["z"])

            pe.wait_ge(signal("cum_in_ready"), 1)
            o = begin(job("cumsum"))
            pe.matmul(o[:, 0:24], tri, cum_in[:, 0, :], start=True, stop=True)
            pe.matmul(o[:, 32:48], tri, cum_in[:, 1, 0:HEADS], start=True, stop=True)
            pe.matmul(o[:, 64:72], tri, cum_in[:, 1, HEADS:24], start=True, stop=False)
            pe.matmul(o[:, 64:72], ones, cum_in[:, 0, HEADS:24], start=False, stop=True)
            end(pe.matmul(o[:, 96:112], ones, cum_in[:, 0, 0:HEADS], start=True, stop=True))
            spread(2, 3, 4)

            pe.wait_ge(signal("conv_ready"), 16)
            for t in range(TT):
                for c0 in range(0, KC, 4):
                    o = begin(job("xs_tok", 2 * t + c0 // 4))
                    for c in range(c0, c0 + 4):
                        mm = pe.transpose(o[:, wide((c - c0) * P, P)], xcT[:, c, wide(t * P, P)], ident)
                    end(mm)
            o = begin(job("b_tok"))
            for g in range(GROUPS):
                mm = pe.transpose(o[:, wide(g * P, P)], xcT[:, KC + g, 0:P], ident)
            end(mm)
            for t in range(TT):
                o = begin(job("cb", t))
                for g in range(GROUPS):
                    mm = pe.matmul(o[:, wide(g * P, P)], xcT[:, KC + g, wide(t * P, P)], xcT[:, KC + GROUPS + g, wide(t * P, P)], start=True, stop=True)
                end(mm)
            def a_row(k):
                t, g = divmod(k, GROUPS)
                o = begin(job(f"a_row{k}"))
                for r in range(PER_GROUP):
                    hd = g * PER_GROUP + r
                    mm = pe.matmul(o[:, wide(r * P, P)], cum_in[:, t, hd:hd + 1].to_broadcast([P, P]), tri, start=True, stop=True)
                end(mm)

            for k in range(3):
                a_row(k)
            pe.wait_ge(signal("x_end_ready"), 1)
            pe.wait_ge(*emptied(job("b_tok")))
            for half in range(2):
                o = begin(job("state", half))
                for g in (2 * half, 2 * half + 1):
                    mm = pe.matmul(o[:, wide((g % 2) * S, S)], b_tok[:, g, :], x_end[:, wide(g * S, S)], start=True, stop=True)
                end(mm)
            in_one(fill_job(gs_fills[0])[0])
            for half in range(2):
                o = begin(job("y_off", half))
                pe.wait_ge(*emptied(job("state", half)))
                for g in (2 * half, 2 * half + 1):
                    mm = pe.matmul(o[:, wide((g % 2) * S, S)], xcT[:, KC + GROUPS + g, P:S], prev[:, wide(g * S, S)], start=True, stop=True)
                end(mm)
            for m in range(2 * TT):
                t, half = divmod(m, 2)
                o = begin(job(f"y_diag{m}"))
                for k in (2 * m, 2 * m + 1):
                    pe.wait_ge(signal("decay_ready"), k + 1)
                    for r in range(PER_GROUP):
                        hd = (k % GROUPS) * PER_GROUP + r
                        mm = pe.matmul(o[:, wide((hd % 8) * HD, HD)], decay[k % 3][:, wide(r * P, P)], xdt[:, t, wide(hd * HD, HD)], start=True, stop=True)
                end(mm)
                for k in range(3 + 2 * m, min(5 + 2 * m, TT * GROUPS)):
                    a_row(k)
                if m < 3:
                    in_one(fill_job(gs_fills[m + 1])[0])

            def fox_scores(o, i):
                hd, t = divmod(i, TT)
                part, n = wide((hd % 2) * HD, HD), (t + 1) * P
                if i == 0:
                    for nm in ("q", "k"):
                        for j in range(2):
                            pe.wait_ge(*emptied(job(nm, j)))
                pe.matmul(o[:, 0:n], qT[part, hd // 2, wide(t * P, P)], kT[part, hd // 2, 0:n], start=True, stop=False)
                for s in range(t + 1):
                    lhs = cum_in[:, s, HEADS + hd:HEADS + hd + 1].to_broadcast([P, P])
                    mm = pe.matmul(o[:, s * P:(s + 1) * P], lhs, tri, start=False, stop=(s == t))
                    if s < t:
                        mm = pe.matmul(o[:, P:2 * P], lhs, ones, start=False, stop=False)
                return mm

            def fox_values(o, i):
                hd, t = divmod(i, TT)
                if i == 0:
                    for j in range(2):
                        pe.wait_ge(*emptied(job("v", j)))
                for s in range(t + 1):
                    mm = pe.matmul(o[:, 0:FOX_D], probT[:, i % ATT_BUF, wide(s * P, P)], v_tok[:, s, wide(hd * FOX_D, FOX_D)], start=(s == 0), stop=(s == t))
                return mm

            attention("fox", FOX_UNITS, 0, fox_scores, fox_values, lambda i: i % TT + 1, fox_fills)

            transpose_tokens("yT", y_tok, "y_ssd_ready")
            for t in range(TT):
                o = begin(job("oT", t))
                for i in range(t, FOX_UNITS, TT):
                    pe.wait_ge(*emptied(job(f"fox_pv{i}")))
                for c in range(4):
                    mm = pe.transpose(o[:, wide(c * P, P)], o_fox[:, t, c::4], ident)
                end(mm)
            for k in range(4):
                pe.wait_ge(*emptied(job("yT", k)))
            for k in range(2):
                pe.wait_ge(*emptied(job("oT", k)))
            for n in range(2):
                for t in range(TT):
                    o = begin(job("merge", 4 * n + 2 * t))
                    for c, w in pieces(f"ssd_o_{n}"):
                        mm = pe.matmul(o, hT[:, c, wide(t * P, P)], w, start=(c == 0), stop=(c == KC - 1))
                    end(mm)
                    o = begin(job("merge", 4 * n + 2 * t + 1))
                    for c, w in pieces(f"att_o_{n}"):
                        mm = pe.matmul(o, oT[:, c, wide(t * P, P)], w, start=(c == 0), stop=(c == 3))
                    end(mm)
            transpose_tokens("mT", h, "merged_ready")
            for k in range(4):
                pe.wait_ge(*emptied(job("mT", k)))
            token_major("w_o", 2, hT)
            transpose_tokens("h2T", h, "h2_ready")
            for k in range(4):
                pe.wait_ge(*emptied(job("h2T", k)))
            pe.wait_ge(signal("router_in"), 64)
            o = begin(job("router"))
            for t in range(TT):
                pe.matmul(o[:, wide(t * 20, 20)], ones_row, small_b[0:1, 0:20], start=True, stop=False)
                for c in range(KC):
                    mm = pe.matmul(o[:, wide(t * 20, 20)], hT[:, c, wide(t * P, P)], small_w[:, c, 0:20], start=False, stop=(c == KC - 1))
            end(mm)
            spread(5, 6, 7)
            pe.wait_ge(signal("chosen_ready"), 1)
            o = begin(job("rank"))
            pe.matmul(o[:, 0:E], tri, chosen[:, 0, :], start=True, stop=True)
            pe.matmul(o[:, E:2 * E], tri, chosen[:, 1, :], start=True, stop=False)
            pe.matmul(o[:, E:2 * E], ones, chosen[:, 0, :], start=False, stop=True)
            pe.matmul(o[:, 2 * E:3 * E], ones, chosen[:, 0, :], start=True, stop=False)
            end(pe.matmul(o[:, 2 * E:3 * E], ones, chosen[:, 1, :], start=False, stop=True))

            def ffn_products(o, lhs, w, parts, width, start, stop):
                for (i, ws) in enumerate(w):
                    mm = pe.matmul(o[wide(parts[i] * width, width), :], lhs(i), ws, start=start, stop=stop)
                return mm

            def loop_begin(R, j):
                k = R.job0 + j
                pe.wait_ge(R.evacuated[k % BANKS], R.it * (R.per_jobs // BANKS) + k // BANKS)
                return R.bank(j)

            def gather(o, chunks, width):
                for i, c in enumerate(chunks):
                    for t in range(TT):
                        mm = pe.matmul(o[:, wide(i * 4 * width, 4 * width)], h[:, t, c::KC], pick[:, t, 0:4 * width], start=(t == 0), stop=(t == TT - 1))
                return mm

            def gather_first(name, picked, width):
                pe.wait_ge(picked, 1)
                for c in range(KC):
                    end(gather(begin(job(name, c)), [c], width))

            gather_first("moe_first", signal("moe_picked"), CAP)
            assert next_job[0] == job("moe")
            def moe_round(R, picked, gathered):
                pe.wait_ge(gathered, R.it + 1)
                for p in range(2):
                    o = loop_begin(R, MOE_GW + p)
                    for t in range(TT):
                        mm = pe.transpose(o[:, wide(t * P, P)], pick_gate[:, t, wide(p * P, P)], ident)
                    mm.then_inc(R.pe_done, 1)
                for p in range(2):
                    for what, j in ((0, MOE_GATE[p]), (1, MOE_UP[p])):
                        o = loop_begin(R, j)
                        for half in range(2):
                            n = 8 * p + 4 * what + 2 * half
                            for i in range(2):
                                pe.wait_ge(*R.arrived(n + i))
                            for c in range(4):
                                for i in range(2):
                                    mm = pe.matmul(o[wide(i * CAP, CAP), :], x_e[:, 4 * half + c, wide((2 * p + i) * CAP, CAP)],
                                                   R.slot(n + i, (4, FF))[:, c, :], start=(half == c == 0), stop=(half == 1 and c == 3))
                        mm.then_inc(R.pe_done, 1)
                pe.wait_ge(picked, R.it + 2)
                for j in range(4):
                    o = loop_begin(R, MOE_XE + j)
                    gather(o, (2 * j, 2 * j + 1), CAP).then_inc(R.pe_done, 1)
                for p in range(2):
                    o = loop_begin(R, MOE_T[p])
                    pe.wait_ge(*R.emptied(MOE_UP[p]))
                    for c in range(4):
                        mm = pe.transpose(o[:, wide(c * P, P)], hid[:, p, wide(c * P, P)], ident)
                    mm.then_inc(R.pe_done, 1)
                    out2 = [loop_begin(R, MOE_DOWN[p] + n) for n in range(2)]
                    pe.wait_ge(*R.emptied(MOE_T[p]))
                    for half in range(2):
                        l = 16 + 4 * p + 2 * half
                        for i in range(2):
                            pe.wait_ge(*R.arrived(l + i))
                        for c in range(2):
                            for n in range(2):
                                for i in range(2):
                                    mm = pe.matmul(out2[n][wide(i * CAP, CAP), :], hidT[:, 4 * p + 2 * half + c, wide(i * CAP, CAP)],
                                                   R.slot(l + i, (2, D))[:, c, wide(n * BANK, BANK)], start=(half == c == 0), stop=(half == c == 1))
                                if half == c == 1:
                                    mm.then_inc(R.pe_done, 1)
                for p in range(2):
                    for n in range(2):
                        pe.wait_ge(*R.emptied(MOE_DOWN[p] + n))
                    for n in range(2):
                        for t in range(TT):
                            o = loop_begin(R, MOE_SUM[p] + 2 * n + t)
                            pe.matmul(o, gate_T[:, p, wide(t * P, P)], y_e[:, p, wide(n * BANK, BANK)], start=True, stop=True).then_inc(R.pe_done, 1)

            with pe.Fori(0, MOE_ROUNDS) as it:
                moe_round(Rounds(it, job("moe"), MOE_JOBS, 0, MOE_LOADS), signal("moe_picked"), signal("moe_gathered"))
            with more_tokens(pe):
                pe.wait_ge(signal("more_picked"), 1)
                for c in range(KC):
                    gather(bank(c), [c], CAP).then_inc(more_sems["pe_done"], 1)
                with pe.Fori(0, MORE_ROUNDS) as it:
                    moe_round(Rounds(it, KC, MOE_JOBS, 0, MOE_LOADS, **more_sems), signal("more_picked"), signal("more_gathered"))
            next_job[0] += MOE_ROUNDS * MOE_JOBS

            transpose_tokens("h3T", h, "h3_ready")
            for k in range(4):
                pe.wait_ge(*emptied(job("h3T", k)))
            for i in range(2):
                for t in range(TT):
                    o = begin(job("lat", 2 * i + t))
                    for c, w in pieces(f"lat_{i}") if t == 0 else chunks(f"lat_{i}"):
                        mm = pe.matmul(o[:, 0:w.shape[-1]], hT[:, c, wide(t * P, P)], w, start=(c == 0), stop=(c == KC - 1))
                    end(mm)
            pe.wait_ge(signal("lat_ready"), 1)
            for t in range(TT):
                o = begin(job("latT", 2 * t))
                for c in range(3):
                    mm = pe.transpose(o[:, wide(c * P, P)], lat[:, t, wide(c * P, P)], ident)
                end(mm)
                o = begin(job("latT", 2 * t + 1))
                for c in range(2):
                    mm = pe.transpose(o[:, wide(c * P, P)], lat[:, t, wide(Q_RANK + c * P, P)], ident)
                end(pe.transpose(o[:, 2 * P:3 * P], k_pe[:, t, :], ident))
            for k in range(4):
                pe.wait_ge(*emptied(job("latT", k)))
            for i, n in enumerate(q_loads):
                pe.wait_ge(*arrived(n))
                o = begin(job("q_nope", i))
                for j in range(2):
                    for c in range(3):
                        mm = pe.matmul(o[:, wide(j * S, S)], slot(n, (3, 384))[:, c, wide(j * (NOPE + ROPE), NOPE)], c_qT[:, c, :], start=(c == 0), stop=(c == 2))
                end(mm)
            for t in range(TT):
                o = begin(job("q_pe", t))
                for i, n in enumerate(q_loads):
                    for c in range(3):
                        w = slot(n, (3, 384))[:, c, :].rearrange("p (h d) -> p h d", h=2)[:, :, NOPE:NOPE + ROPE]
                        mm = pe.matmul(o[:, wide(i * P, P)], c_qT[:, c, wide(t * P, P)], w, start=(c == 0), stop=(c == 2))
                end(mm)
            for i, n in enumerate(kv_loads):
                pe.wait_ge(*arrived(n))
                for half in range(2):
                    o = begin(job("k_nope", 2 * i + half))
                    for j in range(2):
                        for c in range(2):
                            mm = pe.matmul(o[:, wide(j * S, S)], slot(n, (2, 1024))[:, c, wide((2 * half + j) * 2 * NOPE, NOPE)], c_kvT[:, c, :], start=(c == 0), stop=(c == 1))
                    end(mm)
            for i, n in enumerate(kv_loads):
                for t in range(TT):
                    o = begin(job("v_mla", 2 * i + t))
                    for c in range(2):
                        w = slot(n, (2, 1024))[:, c, :].rearrange("p (h d) -> p h d", h=4)[:, :, NOPE:2 * NOPE]
                        mm = pe.matmul(o, c_kvT[:, c, wide(t * P, P)], w, start=(c == 0), stop=(c == 1))
                    end(mm)
            for t in range(TT):
                pe.wait_ge(signal("q_pe_ready"), t + 1)
                o = begin(job("q_peT", t))
                for c in range(MLA_HEADS // 2):
                    mm = pe.transpose(o[:, wide(c * P, P)], q_pe[:, t, wide(c * P, P)], ident)
                end(mm)

            def mla_scores(o, i):
                hd, t = divmod(i, TT)
                if i == 0:
                    for nm, n in (("q_nope", 4), ("k_nope", 4), ("v_mla", 4), ("q_peT", 2)):
                        for j in range(n):
                            pe.wait_ge(*emptied(job(nm, j)))
                part = wide((hd % 2) * ROPE, ROPE)
                pe.matmul(o[:, 0:S], q_nopeT[:, hd, wide(t * P, P)], k_nopeT[:, hd, :], start=True, stop=False)
                return pe.matmul(o[:, 0:S], q_peT[part, hd // 2, wide(t * P, P)], k_peT[part, :], start=False, stop=True)

            def wide_values(v, unit0):
                def values(o, i):
                    for s in range(TT):
                        mm = pe.matmul(o[:, 0:P], probT[:, (unit0 + i) % ATT_BUF, wide(s * P, P)], v[:, s, wide(i // TT * P, P)], start=(s == 0), stop=(s == 1))
                    return mm
                return values

            attention("mla", MLA_UNITS, mla_unit0, mla_scores, wide_values(v_mla, mla_unit0), lambda i: TT, next_fills(0))

            for g in range(DIL_GROUPS):
                token_major(f"dil_v{g}", 2, hT)

                def dil_scores(o, i):
                    hd, t = divmod(i, TT)
                    if i == 0:
                        for nm in "qkv":
                            for j in range(4):
                                pe.wait_ge(*emptied(job(f"dil_{nm}{g}", j)))
                    return pe.matmul(o[:, 0:S], q_dilT[g][:, hd, wide(t * P, P)], k_dilT[g][:, hd, :], start=True, stop=True)

                unit0 = dil_unit0 + g * DIL_UNITS
                attention(f"dil{g}_", DIL_UNITS, unit0, dil_scores, wide_values(v_dil, unit0), lambda i: TT, next_fills(g + 1))
            spread(8, 9, 10)
            transpose_tokens("mixT", h, "mix_ready")
            for k in range(4):
                pe.wait_ge(*emptied(job("mixT", k)))
            token_major("w_out", 2, hT)
            spread(11)
            transpose_tokens("h4T", h, "h4_ready")
            for k in range(4):
                pe.wait_ge(*emptied(job("h4T", k)))
            pe.wait_ge(signal("router2_in"), 16)
            o = begin(job("router2"))
            for t in range(TT):
                for c in range(KC):
                    mm = pe.matmul(o[:, wide(t * E, E)], hT[:, c, wide(t * P, P)], small_w[:, c, 0:E], start=(c == 0), stop=(c == KC - 1))
            end(mm)
            pe.wait_ge(signal("aff_ready"), 1)
            o = begin(job("affT"))
            for t in range(TT):
                mm = pe.transpose(o[0:E, wide(t * P, P)], gates[:, t, :], ident)
            end(mm)
            pe.wait_ge(signal("rank_T_ready"), 1)
            o = begin(job("rank2"))
            for t in range(TT):
                mm = pe.transpose(o[:, wide(t * E, E)], rank_T[:, wide(t * P, P)], ident[0:E, 0:E])
            end(mm)

            gather_first("ec_first", signal("ec_picked"), CAP2)
            assert next_job[0] == job("ec")
            with pe.Fori(0, EC_ROUNDS) as it:
                R = Rounds(it, job("ec"), EC_JOBS, MOE_ROUNDS * MOE_LOADS, EC_LOADS)
                pe.wait_ge(signal("ec_gathered"), it + 1)
                for t in range(TT):
                    o = loop_begin(R, EC_GW + t)
                    end(pe.transpose(o[:, 0:P], pick_gate[:, t, 0:P], ident))

                def ec_products(outs, lhs, l0, n_loads, width):
                    for n in range(n_loads):
                        for i in range(4):
                            pe.wait_ge(*R.arrived(l0 + 4 * n + i))
                        for c in range(2):
                            for b in range(2):
                                for i in range(4):
                                    mm = pe.matmul(outs[b][wide(i * CAP2, CAP2), :], lhs(2 * n + c, i), R.slot(l0 + 4 * n + i, (2, width))[:, c, wide(b * BANK, BANK)],
                                                   start=(n == c == 0), stop=(n == n_loads - 1 and c == 1))
                                if n == n_loads - 1 and c == 1:
                                    end(mm)
                        if n < n_loads - 1:
                            mm.then_inc(pieces_used, 1)

                for fp in range(2):
                    for l0, j in ((32 * fp, EC_GATE[fp]), (32 * fp + 16, EC_UP[fp])):
                        ec_products([loop_begin(R, j + b) for b in range(2)], lambda c, i: x_e[:, c, wide(i * CAP2, CAP2)], l0, 4, 1024)
                    if fp:
                        pe.wait_ge(signal("ec_picked"), it + 2)
                        for j in range(4):
                            o = loop_begin(R, EC_XE + j)
                            end(gather(o, (2 * j, 2 * j + 1), CAP2))
                    for b in range(2):
                        o = loop_begin(R, EC_T[fp] + b)
                        pe.wait_ge(*R.emptied(EC_UP[fp] + b))
                        for c in range(4):
                            mm = pe.transpose(o[:, wide(c * P, P)], hid[:, b, wide(c * P, P)], ident)
                        end(mm)
                for fp in range(2):
                    for b in range(2):
                        pe.wait_ge(*R.emptied(EC_T[fp] + b))
                ec_products([loop_begin(R, EC_DOWN + b) for b in range(2)], lambda c, i: hidT[:, c, wide(i * CAP2, CAP2)], 64, 8, D)
                for n in range(2):
                    pe.wait_ge(*R.emptied(EC_DOWN + n))
                for n in range(2):
                    for t in range(TT):
                        o = loop_begin(R, EC_SUM + 2 * n + t)
                        end(pe.matmul(o, gate_T[:, 0, wide(t * P, P)], y_e[:, 0, wide(n * BANK, BANK)], start=True, stop=True))

        @block.scalar
        def _(act):
            step = Turn(act, act_step)
            a = nc.scalar

            def take(k, out, func=ACT.Copy, src=None, **kw):
                act.wait_ge(*done(k))
                step(a.activation, out, bank(k) if src is None else src(bank(k)), func, signals=emptied(k), **kw)

            def logs_and_exps():
                act.preload_act_table_set("natural_log_exp_and_others")

            def rstd_of(n, t, eps_col=eps5):
                act.wait_ge(signal("var_ready"), n + 1)
                step(a.activation, rstd[:, t, 0:1], mv[:, t, 1:2], ACT.Ln, bias=eps_col)
                step(a.activation, rstd[:, t, 1:2], rstd[:, t, 0:1], ACT.Exp, scale=-0.5, signals=(signal("rstd_ready"), n + 1))

            def attention(name, n, unit0, keys, fills):
                due = {fill_span(f, fills, n)[1]: fill for f, fill in enumerate(fills)}
                for i in range(n + LAG_PV):
                    if i < n:
                        u = unit0 + i
                        act.wait_ge(signal("max_ready"), u + 1)
                        step(a.activation, prob[:, u % ATT_BUF, 0:keys(i) * P], prob[:, u % ATT_BUF, 0:keys(i) * P], ACT.Exp,
                             bias=row_max[:, u:u + 1], accum_out=row_sum[:, u:u + 1], signals=(signal("probs_ready"), u + 1))
                    if 0 <= (j := i - LAG_T) < n:
                        if j >= ATT_BUF:
                            act.wait_ge(*done(job(f"{name}_pv{j - ATT_BUF}")))
                        w = keys(j) * P
                        take(job(f"{name}_t{j}"), probT[:, (unit0 + j) % ATT_BUF, 0:w], src=lambda o: o[:, 0:w])
                    if i in due:
                        due[i]()

            a.dma_start(cact[:, 0, :], A["c"][0].rearrange("(p c) -> p c", c=KC)).then_inc(signal("c_in"), 16)
            a.dma_start(cact[:, 1, :], A["c_2"][0].rearrange("(p c) -> p c", c=KC)).then_inc(signal("c_in"), 16)
            a.dma_start(consts[:], A["consts"]).then_inc(signal("const_in"), 16)
            a.dma_start(pos_rows[:, 0:S], A["positions_2"].to_broadcast([P, S])).then_inc(signal("pos_in"), 16)
            for q in range(4):
                a.dma_start(pos_rows[wide(q * BUCKETS, BUCKETS), S:S + S // 4], A["positions_2"][:, wide(q * S // 4, S // 4)].to_broadcast([BUCKETS, S // 4])).then_inc(signal("pos_in"), 16)

            def distance_abs(it, n):
                act.wait_ge(signal("distance_ready"), it * BIAS_STEPS + (n + 1))
                a.activation(one_hot[n], one_hot[n], ACT.Abs).then_inc(signal("distance_abs_ready"), 1)

            def bias_out(it, n):
                R = Rounds(it, job("bias"), BANKS)
                for j in range(2):
                    act.wait_ge(*R.done(2 * n + j))
                    if j == 0 and not (isinstance(it, int) and it == 0):
                        act.wait_ge(bias_stored[n], it * BIAS_STORES)
                    a.activation(staged[n][:, wide(j * BANK, BANK)], R.bank(2 * n + j), ACT.Copy).then_inc(R.emptied(2 * n + j)[0], 1)

            def bias_step(it, n):
                bias_out(it - 1, n)
                distance_abs(it, n)

            for n in range(BIAS_STEPS):
                distance_abs(0, n)
            act.wait_ge(signal("c_in"), 32)
            step(a.activation, cact[:], cact[:], ACT.Silu, signals=(signal("cact_ready"), 1))
            for n in range(BIAS_STEPS):
                bias_step(1, n)
            with act.Fori(2, BIAS_ROUNDS) as it:
                for n in range(BIAS_STEPS):
                    bias_step(it, n)
            for n in range(BIAS_STEPS):
                bias_out(BIAS_ROUNDS - 1, n)
            act.wait_ge(signal("const_in"), 16)
            logs_and_exps()
            for t in range(TT):
                rstd_of(t, t)
            for n in range(2):
                take(job("mod0", n), mod[:, 0, wide(n * BANK, BANK)])
            for n in range(2):
                take(job("mod1", n), mod[:, 1, wide(n * BANK, BANK)], ACT.Identity, bias=1.0)
            act.wait_ge(signal("pad_ready"), 1)

            def conv_silu(j):
                for ct in (2 * j, 2 * j + 1):
                    act.wait_ge(signal("conv_sum_ready"), ct + 1)
                    step(a.activation, xcT[:, ct, :], prob[:, ct % ATT_BUF, :], ACT.Silu, signals=(signal("conv_ready"), ct + 1))

            for j in range(8):
                take(job("xbc", j), u_pad[:, 2 * j:2 * j + 2, 3:3 + S], src=lambda o: o.rearrange("p (c t) -> p c t", c=2))
                if j:
                    conv_silu(j - 1)
            for stored in bias_stored:
                act.wait_ge(stored, BIAS_ROUNDS * BIAS_STORES)
            for j in range(2):
                take(job("q", j), qT[:, 2 * j:2 * j + 2, :], src=lambda o: o.rearrange("p (c t) -> p c t", c=2), scale=FOX_D ** -0.5)
            conv_silu(7)
            for j in range(2):
                take(job("k", j), kT[:, 2 * j:2 * j + 2, :], src=lambda o: o.rearrange("p (c t) -> p c t", c=2))
            logs_and_exps()
            act.wait_ge(signal("neg_abs_ready"), 1)
            step(a.activation, dtf_e[:], dtf_e[:], ACT.Exp)
            step(a.activation, dtf_e[:], dtf_e[:], ACT.Ln, bias=1.0)
            act.wait_ge(signal("head_in"), 32)
            step(a.activation, head_v[:, 0, :], head_v[:, 0, :], ACT.Exp, signals=(signal("softplus_ready"), 1))
            for j in range(4):
                take(job("z", j), silu_z[:, j % 2, wide(j // 2 * BANK, BANK)], ACT.Silu)
            act.wait_ge(*emptied(job("cumsum")))
            step(a.activation, a_exp[:], a_exp[:], ACT.Exp, signals=(signal("a_exp_ready"), 1))
            for j in range(4):
                t, half = divmod(j, 2)
                take(job("xs_tok", j), xs_tok[:, t, wide(half * BANK, BANK)])
            take(job("b_tok"), b_tok[:].rearrange("p g n -> p (g n)"))
            for t in range(TT):
                take(job("cb", t), cb[:, t].rearrange("p g l -> p (g l)"))

            def decay_exp(k):
                act.wait_ge(*emptied(job(f"a_row{k}")))
                step(a.activation, decay[k % 3], decay[k % 3], ACT.Exp, signals=(signal("decay_exp_ready"), k + 1))

            logs_and_exps()
            for k in range(3):
                decay_exp(k)
            act.wait_ge(signal("x_end_ready"), 1)
            for half in range(2):
                take(job("state", half), prev[:, wide(half * BANK, BANK)])

            def take_gate(name, j, to, which=0):
                take(job(name, 4 * which + j), to[:, j % 2, wide(j // 2 * BANK, BANK)])

            take_gate("gs", 0, sig_gs)
            for k in range(3, TT * GROUPS):
                decay_exp(k)
                if k % 2 == 0:
                    take_gate("gs", k // 2 - 1, sig_gs)
            take_gate("gs", 3, sig_gs)
            for t in range(TT):
                act.wait_ge(signal("gated_ready"), t + 1)
                step(a.activation, silu_z[:, t, :], y_tok[:, t, :], ACT.Square, scale=D ** -0.5, accum_out=mv[:, t, 1:2])
            act.wait_ge(act_step, step.n)
            step(a.activation, rstd[:, :, 0], mv[:, :, 1], ACT.Ln, bias=eps5)
            step(a.activation, rstd[:, :, 1], rstd[:, :, 0], ACT.Exp, scale=-0.5, signals=(signal("rms_ready"), 1))
            attention("fox", FOX_UNITS, 0, lambda i: i % TT + 1,
                      [(lambda: None) if fill[0] == "unit" else (lambda fill=fill: take_gate("ga", 2 * fill[2] + fill[3], sig_ga)) for fill in fox_fills])
            step(a.activation, sig_both, sig_both, ACT.Sigmoid, signals=(signal("gates_ready"), 1))
            for t in range(TT):
                take(job("oT", t), oT[:, :, wide(t * P, P)], src=lambda o: o.rearrange("p (c t) -> p c t", c=4))
            logs_and_exps()
            for j in range(4):
                t, half = divmod(j, 2)
                take(job("mT", j), hT[:, 4 * half:4 * half + 4, wide(t * P, P)], src=lambda o: o.rearrange("p (c t) -> p c t", c=4))
            for t in range(TT):
                for i in range(2):
                    rstd_of(2 + 2 * t + i, t)
            for j in range(4):
                t, half = divmod(j, 2)
                take(job("h2T", j), hT[:, 4 * half:4 * half + 4, wide(t * P, P)], src=lambda o: o.rearrange("p (c t) -> p c t", c=4))
            act.wait_ge(signal("route_logits_ready"), 1)
            step(a.activation, route_g[:], route_g[:], ACT.Exp)
            step(a.activation, route_2[:], route_2[:], ACT.Exp, signals=(signal("route_exp_ready"), 1))

            for n in range(2):
                take(job("mod5", n), mod[:, 2, wide(n * BANK, BANK)], ACT.Identity, bias=1.0)
            for n in range(2):
                take(job("mod6", n), mod[:, 0, wide(n * BANK, BANK)])
            for n in range(2):
                take(job("mod7", n), mod[:, 1, wide(n * BANK, BANK)], ACT.Identity, bias=1.0)

            act.wait_ge(signal("angles_ready"), 1)
            step(a.activation, turn[:, 2:4].rearrange("p a t f -> p (a t f)"), turn[:, 0:2].rearrange("p a t f -> p (a t f)"), ACT.Sin, signals=(signal("sin_ready"), 1))

            def moe_round(R):
                step.begin_loop(R.it, 0)
                step.last = None

                def take_round(j, out, func=ACT.Copy, width=BANK):
                    act.wait_ge(*R.done(j))
                    step(a.activation, out, R.bank(j)[:, 0:width], func, signals=R.emptied(j))

                for p in range(2):
                    take_round(MOE_GW + p, gate_T[:, p, :], width=S)
                for p in range(2):
                    take_round(MOE_GATE[p], silu_g[:, p, :], ACT.Silu)
                for p in range(2):
                    take_round(MOE_T[p], hidT[:, 4 * p:4 * p + 4, :].rearrange("p c t -> p (c t)"))
                step.end_loop(0)
                step.last = None

            with act.Fori(0, MOE_ROUNDS) as it:
                moe_round(Rounds(it, job("moe"), MOE_JOBS))
            with more_tokens(act):
                with act.Fori(0, MORE_ROUNDS) as it:
                    moe_round(Rounds(it, KC, MOE_JOBS, **more_sems))


            def root_mean_square(n, t, srcs):
                for i, (src, to, width) in enumerate(srcs):
                    step(a.activation, square_junk[:, 0:width], src, ACT.Square, scale=width ** -0.5, accum_out=to[:, t, 1:2])
                    step(a.activation, rstd[:, t, 0:1], to[:, t, 1:2], ACT.Ln, bias=eps6)
                    step(a.activation, to[:, t, 0:1], rstd[:, t, 0:1], ACT.Exp, scale=-0.5, signals=(signal("rms2_ready"), n + 1) if i == len(srcs) - 1 else None)

            logs_and_exps()
            for t in range(TT):
                rstd_of(6 + t, t)
                act.wait_ge(signal("x_b1_ready"), t + 1)
                root_mean_square(t, t, [(x[:, t, :], mv, D)])
            for j in range(4):
                t, half = divmod(j, 2)
                take(job("h3T", j), hT[:, 4 * half:4 * half + 4, wide(t * P, P)], src=lambda o: o.rearrange("p (c t) -> p c t", c=4))
            for j in range(4):
                i, t = divmod(j, 2)
                w = min(BANK, LAT - i * BANK)
                take(job("lat", j), lat[:, t, wide(i * BANK, w)], src=lambda o: o[:, 0:w])
            for t in range(TT):
                root_mean_square(2 + t, t, [(lat[:, t, 0:Q_RANK], mv, Q_RANK), (lat[:, t, wide(Q_RANK, KV_RANK)], mv2, KV_RANK)])

            def two_tiles(o):
                return o.rearrange("p (c t) -> p c t", c=2)

            for j in range(4):
                take(job("q_nope", j), q_nopeT[:, 2 * j:2 * j + 2, :], src=two_tiles)
            for j in range(4):
                take(job("k_nope", j), k_nopeT[:, 2 * j:2 * j + 2, :], src=two_tiles)
            for j in range(4):
                half, t = divmod(j, 2)
                take(job("v_mla", j), v_mla[:, t, wide(half * BANK, BANK)])
            for t in range(TT):
                take(job("q_peT", t), q_peT[:, :, wide(t * P, P)], src=lambda o: o.rearrange("p (c t) -> p c t", c=4))

            def take_next(g):
                if g == DIL_GROUPS:
                    return [lambda j=j: take_gate("gates2", j % 4, (sig_a, sig_b)[j // 4], j // 4) for j in range(8)]
                return [lambda nm=nm, to=to, j=j: take(job(f"dil_{nm}{g}", j), to[g][:, 2 * j:2 * j + 2, :], src=two_tiles)
                        for nm, to in (("q", q_dilT), ("k", k_dilT)) for j in range(4)]

            attention("mla", MLA_UNITS, mla_unit0, lambda i: TT, take_next(0))
            def dil_exp(n):
                act.wait_ge(signal("dil_shift_ready"), n)
                step(a.activation, dil_w[:, 0:2, :], dil_w[:, 0:2, :], ACT.Exp, signals=(signal("dil_exp_ready"), n))

            for g in range(DIL_GROUPS):
                for j in range(4):
                    take(job(f"dil_v{g}", j), v_dil[:, j % 2, wide(j // 2 * BANK, BANK)])
                attention(f"dil{g}_", DIL_UNITS, dil_unit0 + g * DIL_UNITS, lambda i: TT, take_next(g + 1))
                if g == 1:
                    dil_exp(1)
            dil_exp(2)
            for t in range(TT):
                step(a.activation, sig_a[:, t, :], sig_a[:, t, :], ACT.Sigmoid, signals=(signal("gate_a_ready"), t + 1))
                step(a.activation, sig_b[:, t, :], sig_b[:, t, :], ACT.Sigmoid, signals=(signal("gate_b_ready"), t + 1))
            logs_and_exps()
            for unit in (8, 9, 10):
                for n in range(2):
                    take(job(f"mod{unit}", n), mod[:, (2, 0, 1)[unit - 8], wide(n * BANK, BANK)], ACT.Identity, bias=1.0 if unit == 10 else 0.0)
            for j in range(4):
                t, half = divmod(j, 2)
                take(job("mixT", j), hT[:, 4 * half:4 * half + 4, wide(t * P, P)], src=lambda o: o.rearrange("p (c t) -> p c t", c=4))
            for t in range(TT):
                act.wait_ge(signal("x2_ready"), t + 1)
                root_mean_square(4 + t, t, [(x[:, t, :], mv, D)])
            for n in range(2):
                take(job("mod11", n), mod[:, 2, wide(n * BANK, BANK)])
            for j in range(4):
                t, half = divmod(j, 2)
                take(job("h4T", j), hT[:, 4 * half:4 * half + 4, wide(t * P, P)], src=lambda o: o.rearrange("p (c t) -> p c t", c=4))
            act.wait_ge(signal("aff_logits_ready"), 1)
            step(a.activation, gates[:], gates[:], ACT.Exp, signals=(signal("aff_exp_ready"), 1))

            with act.Fori(0, EC_ROUNDS) as it:
                R = Rounds(it, job("ec"), EC_JOBS)
                step.begin_loop(it, 0)
                step.last = None

                def take_ec(j, out, func=ACT.Copy, width=BANK):
                    act.wait_ge(*R.done(j))
                    step(a.activation, out, R.bank(j)[:, 0:width], func, signals=R.emptied(j))

                for t in range(TT):
                    take_ec(EC_GW + t, gate_T[:, 0, wide(t * P, P)], width=P)
                for fp in range(2):
                    for b in range(2):
                        take_ec(EC_GATE[fp] + b, silu_g[:, b, :], ACT.Silu)
                    for b in range(2):
                        take_ec(EC_T[fp] + b, hidT[:, 8 * fp + 4 * b:8 * fp + 4 * b + 4, :].rearrange("p c t -> p (c t)"))
                step.end_loop(EC_ROUNDS)
                step.last = None
            logs_and_exps()
            for t in range(TT):
                for n in range(2):
                    act.wait_ge(*emptied(job("ec", (EC_ROUNDS - 1) * EC_JOBS + EC_SUM + 2 * n + t)))
                root_mean_square(6 + t, t, [(y_sum[:, t, :], mv, D)])

        @block.vector
        def _(dve):
            step = Turn(dve, dve_step)
            v = nc.vector

            def take(k, op, *args, **kw):
                dve.wait_ge(*done(k))
                step(op, *args, signals=emptied(k), **kw)

            def norm_stats(n, t, src=x):
                for half in range(2):
                    step(v.bn_stats, stats[:, t, half, :], src[:, t, wide(half * 512, 512)])
                step(v.bn_aggr, mv[:, t, :], stats[:, t].rearrange("p a b -> p (a b)"), signals=(signal("var_ready"), n + 1))

            def normalize(dst, n, t, gain, shift, signals=None, src=x):
                step(v.scalar_tensor_tensor, dst[:, t, :], src[:, t, :], mv[:, t, 0:1], gain, ALU.subtract, ALU.mult)
                dve.wait_ge(signal("rstd_ready"), n + 1)
                step(v.scalar_tensor_tensor, dst[:, t, :], dst[:, t, :], rstd[:, t, 1:2], shift, ALU.mult, ALU.add, signals=signals)

            def attention(name, n, unit0, masked, keys, out, fills=()):
                due = {fill_span(f, fills, n)[1]: fill for f, fill in enumerate(fills)}
                for i in range(n + LAG_PV):
                    if i < n:
                        u, k, w = unit0 + i, job(f"{name}_qk{i}"), keys(i) * P
                        if i >= ATT_BUF:
                            dve.wait_ge(*done(job(f"{name}_t{i - ATT_BUF}")))
                        dve.wait_ge(*done(k))
                        masked(i, prob[:, u % ATT_BUF, 0:w], bank(k)[:, 0:w], emptied(k))
                        step(v.tensor_reduce, row_max[:, u:u + 1], prob[:, u % ATT_BUF, 0:w], AX, ALU.max, negate=True, signals=(signal("max_ready"), u + 1))
                    if 0 <= (j := i - LAG_PV) < n:
                        u, k = unit0 + j, job(f"{name}_pv{j}")
                        step(v.reciprocal, row_inv[:, u:u + 1], row_sum[:, u:u + 1])
                        take(k, v.tensor_scalar, out(j), bank(k)[:, 0:out(j).shape[-1]], row_inv[:, u:u + 1], None, ALU.mult)
                    if i in due and due[i][0] == "unit":
                        add_row(due[i][1])

            step(v.memset, mod_rows[:], 0.0)
            step(v.memset, table[:], 0.0, signals=(signal("zeros_ready"), 1))
            step(v.memset, cond[:], 0.0)
            dve.wait_ge(signal("pos_in"), 80)
            dve.wait_ge(signal("const_in"), 16)
            step(v.tensor_copy, pos_all, pos_rows[:, 0:S])
            step(v.tensor_copy, pos_quarter, pos_rows[:, S:S + S // 4])
            step(v.tensor_scalar, pos_quarter, pos_quarter, bucket_range[:, 0:1], None, ALU.add, signals=(signal("positions_ready"), 1))

            def in_bucket(it, n):
                dve.wait_ge(signal("distance_abs_ready"), it * BIAS_STEPS + (n + 1))
                step(v.tensor_scalar, one_hot[n], one_hot[n], bucket_range[:, 1:2], None, ALU.is_le, signals=(signal("one_hot_ready"), it * BIAS_STEPS + (n + 1)))

            step.last = None
            with dve.Fori(0, BIAS_ROUNDS) as it:
                for n in range(BIAS_STEPS):
                    in_bucket(it, n)
                step.last = None
            dve.wait_ge(signal("cact_ready"), 1)
            step(v.tensor_copy, cond[:, :, :, 31], cact[:], signals=(signal("cond_ready"), 1))
            dve.wait_ge(signal("x_in"), 16)
            for t in range(TT):
                norm_stats(t, t)
            step(v.memset, u_pad[:, :, 0:3], 0.0, signals=(signal("pad_ready"), 1))
            dve.wait_ge(signal("mod_bias_in"), 64)

            def add_row(u):
                k = job(f"unit{u}")
                take(k, v.tensor_tensor, mod_rows[:], bank(k), mod_rows[:], ALU.add)

            add_row(0)
            add_row(1)
            take(job("vecT"), v.tensor_copy, vecT[:, 0:85], bank(job("vecT"))[:, 0:85])
            for unit in ("mod0", "mod1"):
                for n in range(2):
                    dve.wait_ge(*emptied(job(unit, n)))
            for t in range(TT):
                normalize(h, t, t, mod[:, 1, :], mod[:, 0, :], (signal("h_ready"), t + 1))
            for j in range(4):
                t, half = divmod(j, 2)
                take(job("hT", j), v.tensor_copy, hT[:, 4 * half:4 * half + 4, wide(t * P, P)], bank(job("hT", j)).rearrange("p (c t) -> p c t", c=4))

            for ct in range(16):
                dve.wait_ge(*emptied(job("xbc", ct // 2)))
                if ct >= ATT_BUF:
                    dve.wait_ge(signal("conv_ready"), ct - ATT_BUF + 1)
                acc = prob[:, ct % ATT_BUF, :]
                step(v.tensor_scalar, acc, u_pad[:, ct, 0:S], vecT[:, ct:ct + 1], vecT[:, 64 + ct:65 + ct], ALU.mult, ALU.add)
                for j in range(1, 4):
                    step(v.scalar_tensor_tensor, acc, u_pad[:, ct, j:j + S], vecT[:, 16 * j + ct:16 * j + ct + 1], acc, ALU.mult, ALU.add,
                         signals=(signal("conv_sum_ready"), ct + 1) if j == 3 else None)
                if ct % 4 == 3:
                    add_row(IN_UNITS["xbc"][ct // 4])
            k = job("dtf")
            dve.wait_ge(*done(k))
            both = bank(k)[:, 0:TT * 24].rearrange("p (t c) -> p t c", t=TT)
            step(v.tensor_copy, dtf[:, :, 0:HEADS], both[:, :, 0:HEADS])
            step(v.tensor_scalar, dtf[:, :, HEADS:24], both[:, :, HEADS:24], -1.0, None, ALU.mult, signals=emptied(k))
            step(v.scalar_tensor_tensor, dtf_e[:], dtf[:], -1.0, dtf[:], ALU.mult, ALU.min, signals=(signal("neg_abs_ready"), 1))
            add_row(6)
            add_row(7)
            for j in range(2):
                take(job("v", j), v.tensor_copy, v_tok[:, j, :], bank(job("v", j)))
            add_row(8)
            add_row(9)
            dve.wait_ge(signal("pos_tok_in"), 16)
            step(v.tensor_copy, posf[:], pos_i[:])
            for t in range(TT):
                step(v.tensor_scalar, turn[:, 0, t, :], inv_freq, posf[:, t:t + 1], None, ALU.mult)
            step(v.tensor_scalar, turn[:, 2], turn[:, 0], 1.0 / TWO_PI, MAGIC, ALU.mult, ALU.add)
            step(v.tensor_scalar, turn[:, 2], turn[:, 2], MAGIC, None, ALU.subtract)
            step(v.scalar_tensor_tensor, turn[:, 0], turn[:, 2], -TWO_PI_HI, turn[:, 0], ALU.mult, ALU.add)
            step(v.scalar_tensor_tensor, turn[:, 0], turn[:, 2], -(TWO_PI - TWO_PI_HI), turn[:, 0], ALU.mult, ALU.add)
            step(v.tensor_scalar, turn[:, 1], turn[:, 0], TWO_PI / 4, None, ALU.add)
            step(v.tensor_scalar, turn[:, 2], turn[:, 1], PI, -TWO_PI, ALU.is_gt, ALU.mult)
            step(v.tensor_tensor, turn[:, 1], turn[:, 1], turn[:, 2], ALU.add)
            step(v.tensor_scalar, turn[:, 0:2], turn[:, 0:2], PI, -PI, ALU.min, ALU.max, signals=(signal("angles_ready"), 1))
            dve.wait_ge(signal("softplus_ready"), 1)
            step(v.scalar_tensor_tensor, dtf[:], dtf[:], 0.0, dtf_e[:], ALU.max, ALU.add)
            step(v.tensor_copy, cum_in[:, :, HEADS:24], dtf[:, :, HEADS:24])
            step(v.scalar_tensor_tensor, cum_in[:, :, 0:HEADS], dtf[:, :, 0:HEADS], -1.0, head_v[:, 0:1, :].to_broadcast([P, TT, HEADS]), ALU.mult, ALU.mult,
                 signals=(signal("cum_in_ready"), 1))
            k = job("cumsum")
            dve.wait_ge(*done(k))
            step(v.tensor_copy, a_cs[:], bank(k)[:, 0:64].rearrange("p (t c) -> p t c", t=TT)[:, :, 0:HEADS])
            step(v.tensor_copy, neg_F[:, 0, :], bank(k)[:, 16:24])
            step(v.tensor_copy, neg_F[:, 1, :], bank(k)[:, 64:72])
            step(v.tensor_copy, a_exp[:, 0, :], a_cs[:, 1, :])
            step(v.tensor_tensor, a_exp[:, 1, :], bank(k)[:, 96:112], a_cs[:, 0, :], ALU.subtract, signals=emptied(k))
            for unit in (2, 3, 4):
                for n in range(2):
                    k = job(f"mod{unit}", n)
                    take(k, v.tensor_scalar, mod[:, (2, 0, 1)[unit - 2], wide(n * BANK, BANK)], bank(k), 0.0 if unit == 3 else 1.0, None, ALU.add)
            for j in range(4):
                t, half = divmod(j, 2)
                dve.wait_ge(*emptied(job("xs_tok", j)))
                step(v.tensor_tensor, xdt[:, t, wide(half * BANK, BANK)].rearrange("p (g d) -> p g d", d=HD), xs_tok[:, t, wide(half * BANK, BANK)].rearrange("p (g d) -> p g d", d=HD),
                     dtf[:, t, wide(half * 8, 8)].unsqueeze(2).to_broadcast([P, 8, HD]), ALU.mult)
            dve.wait_ge(signal("a_exp_ready"), 1)
            step(v.tensor_tensor, x_end.rearrange("p (g d) -> p g d", d=HD), xdt[:, 0, :].rearrange("p (g d) -> p g d", d=HD),
                 a_exp[:, 1, :].unsqueeze(2).to_broadcast([P, HEADS, HD]), ALU.mult, signals=(signal("x_end_ready"), 1))

            def segments(k):
                t, g = divmod(k, GROUPS)
                dve.wait_ge(*done(job(f"a_row{k}")))
                if k >= 3:
                    dve.wait_ge(*done(job(f"y_diag{(k - 3) // 2}")))
                for r in range(PER_GROUP):
                    hd = g * PER_GROUP + r
                    last = r == PER_GROUP - 1
                    step(v.scalar_tensor_tensor, decay[k % 3][:, wide(r * P, P)], bank(job(f"a_row{k}"))[:, wide(r * P, P)], a_cs[:, t, hd:hd + 1], seg_mask,
                         ALU.subtract, ALU.add, signals=emptied(job(f"a_row{k}")) if last else None)

            def masked_cb(k):
                t, g = divmod(k, GROUPS)
                dve.wait_ge(signal("decay_exp_ready"), k + 1)
                if k == 0:
                    for j in range(TT):
                        dve.wait_ge(*emptied(job("cb", j)))
                step(v.tensor_tensor, decay[k % 3].rearrange("p (r l) -> p r l", r=PER_GROUP), decay[k % 3].rearrange("p (r l) -> p r l", r=PER_GROUP),
                     cb[:, t, g:g + 1, :].to_broadcast([P, PER_GROUP, P]), ALU.mult, signals=(signal("decay_ready"), k + 1))

            y_off = params[:, 0, :]

            def heads_of(ap):
                return ap.rearrange("p (g d) -> p g d", d=HD)

            def assemble(m):
                t, half = divmod(m, 2)
                cols, k = wide(half * BANK, BANK), job(f"y_diag{m}")
                step(v.tensor_tensor, heads_of(y_tok[:, t, cols]), heads_of(xs_tok[:, t, cols]), head_v[:, 1, wide(half * 8, 8)].unsqueeze(2).to_broadcast([P, 8, HD]), ALU.mult)
                take(k, v.tensor_tensor, y_tok[:, t, cols], bank(k), y_tok[:, t, cols], ALU.add)
                if t:
                    step(v.tensor_tensor, y_tok[:, t, cols], y_tok[:, t, cols], y_off[:, cols], ALU.add)
                if m == 0:
                    for j in range(4):
                        dve.wait_ge(*emptied(job("z", j)))
                step(v.tensor_tensor, y_tok[:, t, cols], y_tok[:, t, cols], silu_z[:, t, cols], ALU.mult, signals=(signal("gated_ready"), t + 1) if half else None)

            segments(0)
            segments(1)
            masked_cb(0)
            segments(2)
            masked_cb(1)
            for half in range(2):
                k = job("y_off", half)
                take(k, v.tensor_tensor, heads_of(y_off[:, wide(half * BANK, BANK)]), heads_of(bank(k)), a_exp[:, 0, wide(half * 8, 8)].unsqueeze(2).to_broadcast([P, 8, HD]), ALU.mult)
            for m in range(2 * TT):
                assemble(m)
                for k in range(3 + 2 * m, min(5 + 2 * m, TT * GROUPS)):
                    segments(k)
                    masked_cb(k - 1)
                if m == 2:
                    masked_cb(TT * GROUPS - 1)
            dve.wait_ge(signal("rms_ready"), 1)
            for t in range(TT):
                step(v.tensor_scalar, y_tok[:, t, :], y_tok[:, t, :], rstd[:, t, 1:2], None, ALU.mult, signals=(signal("y_ssd_ready"), t + 1))

            def fox_mask(i, dst, src, taken):
                hd, t = divmod(i, TT)
                step(v.scalar_tensor_tensor, dst, src, neg_F[:, t, hd:hd + 1], causal[:, (1 - t) * P:2 * P], ALU.subtract, ALU.add, signals=taken)

            attention("fox", FOX_UNITS, 0, fox_mask, lambda i: i % TT + 1, lambda i: o_fox[:, i % TT, wide(i // TT * FOX_D, FOX_D)], fox_fills)
            dve.wait_ge(signal("ssd_w_in"), 16)
            for j in range(4):
                t, half = divmod(j, 2)
                k = job("yT", j)
                take(k, v.tensor_tensor, hT[:, 4 * half:4 * half + 4, wide(t * P, P)], bank(k).rearrange("p (c t) -> p c t", c=4),
                     ssd_w[:, 4 * half:4 * half + 4].unsqueeze(2).to_broadcast([P, 4, P]), ALU.mult)
            for j in range(4):
                n, t = divmod(j, 2)
                cols = wide(n * BANK, BANK)
                if j == 0:
                    dve.wait_ge(signal("gates_ready"), 1)
                k = job("merge", 2 * j)
                take(k, v.tensor_tensor, h[:, t, cols], bank(k), sig_gs[:, t, cols], ALU.mult)
                k = job("merge", 2 * j + 1)
                take(k, v.tensor_tensor, junk[:, 0:BANK], bank(k), sig_ga[:, t, cols], ALU.mult)
                step(v.tensor_tensor, h[:, t, cols], h[:, t, cols], junk[:, 0:BANK], ALU.add, signals=(signal("merged_ready"), t + 1) if n else None)

            for j in range(4):
                n, t = divmod(j, 2)
                cols, k = wide(n * BANK, BANK), job("w_o", j)
                take(k, v.tensor_tensor, junk[:, 0:BANK], bank(k), mod[:, 2, cols], ALU.mult)
                step(v.scalar_tensor_tensor, x[:, t, cols], x[:, t, cols], ALPHA, junk[:, 0:BANK], ALU.mult, ALU.add)
                if n == 0:
                    continue
                if t == 0:
                    dve.wait_ge(signal("params_in"), 32)
                norm_stats(2 + 2 * t, t)
                normalize(x, 2 + 2 * t, t, params[:, 0, :], params[:, 1, :], (signal("x_mid_ready"), 1) if t else None)
                norm_stats(3 + 2 * t, t)
                normalize(h, 3 + 2 * t, t, mod[:, 1, :], mod[:, 0, :], (signal("h2_ready"), t + 1))

            def first_of(dst, vals, top, n):
                step(v.tensor_reduce, top, vals, AX, ALU.max)
                step(v.tensor_tensor, dst, vals, top.unsqueeze(2).to_broadcast([P, TT, n]), ALU.is_equal)
                step(v.tensor_tensor, dst, dst, desc[:, E - n:E].unsqueeze(1).to_broadcast([P, TT, n]), ALU.mult)
                step(v.tensor_reduce, route_top[:], dst, AX, ALU.max)
                step(v.tensor_tensor, dst, dst, route_top[:].unsqueeze(2).to_broadcast([P, TT, n]), ALU.is_equal)

            k = job("router")
            dve.wait_ge(*done(k))
            step(v.tensor_copy, logits[:], bank(k)[:, 0:TT * 20].rearrange("p (t c) -> p t c", t=TT), signals=emptied(k))
            first_of(hot_g[:], logits[:, :, 0:4], top1[:], 4)
            step(v.tensor_tensor, route_g[:], logits[:, :, 0:4], top1[:].unsqueeze(2).to_broadcast([P, TT, 4]), ALU.subtract)
            for t in range(TT):
                step(v.tensor_tensor, in_group[:, t].rearrange("p (g e) -> p g e", g=4), logits[:, t, 4:20].rearrange("p (g e) -> p g e", g=4), hot_g[:, t, :].unsqueeze(2).to_broadcast([P, 4, 4]), ALU.mult)
                step(v.tensor_reduce, e_in[:, t, :], in_group[:, t].rearrange("p (g e) -> p e g", g=4), AX, ALU.add)
            first_of(hot1[:], e_in[:], top1[:], 4)
            step(v.scalar_tensor_tensor, e_in[:], hot1[:], NEG, e_in[:], ALU.mult, ALU.add)
            first_of(hot2[:], e_in[:], top2[:], 4)
            step(v.tensor_tensor, route_2[:], top2[:], top1[:], ALU.subtract, signals=(signal("route_logits_ready"), 1))
            step(v.tensor_tensor, e_in[:], hot1[:], hot2[:], ALU.add)
            for t in range(TT):
                step(v.tensor_tensor, chosen[:, t].rearrange("p (g e) -> p g e", g=4), hot_g[:, t, :].unsqueeze(2).to_broadcast([P, 4, 4]),
                     e_in[:, t, :].unsqueeze(1).to_broadcast([P, 4, 4]), ALU.mult, signals=(signal("chosen_ready"), 1) if t else None)
            dve.wait_ge(signal("route_exp_ready"), 1)
            step(v.tensor_reduce, top1[:], route_g[:], AX, ALU.add)
            step(v.scalar_tensor_tensor, top1[:], route_2[:], 1.0, top1[:], ALU.add, ALU.mult)
            step(v.reciprocal, top1[:], top1[:])
            step(v.tensor_tensor, top2[:], route_2[:], top1[:], ALU.mult)
            step(v.tensor_tensor, hot1[:], hot1[:], top1[:].unsqueeze(2).to_broadcast([P, TT, 4]), ALU.mult)
            step(v.tensor_tensor, hot2[:], hot2[:], top2[:].unsqueeze(2).to_broadcast([P, TT, 4]), ALU.mult)
            step(v.tensor_tensor, hot1[:], hot1[:], hot2[:], ALU.add)
            for t in range(TT):
                step(v.tensor_tensor, gates[:, t].rearrange("p (g e) -> p g e", g=4), hot_g[:, t, :].unsqueeze(2).to_broadcast([P, 4, 4]),
                     hot1[:, t, :].unsqueeze(1).to_broadcast([P, 4, 4]), ALU.mult)
            k = job("rank")
            dve.wait_ge(*done(k))
            step(v.tensor_reduce, top1[:, 0:1], bank(k)[:, TT * E:(TT + 1) * E], AX, ALU.max)
            step(v.tensor_scalar, overflow[:], top1[:, 0:1], float(CAP), None, ALU.is_gt, signals=(signal("overflow_known"), 1))
            step(v.tensor_tensor, rank[:], bank(k)[:, 0:TT * E].rearrange("p (t e) -> p t e", t=TT), chosen[:], ALU.mult, signals=emptied(k))

            for t in range(TT):
                step(v.tensor_scalar, y_sum[:, t, :], x[:, t, :], ALPHA, None, ALU.mult)
            for n in range(2):
                dve.wait_ge(*emptied(job("mod5", n)))

            def picks(step, quad, width, picked):
                for t in range(TT):
                    step(v.tensor_tensor, pick[:, t, 0:4 * width].rearrange("p (e j) -> p e j", e=4), iota1[:, 0:width].unsqueeze(1).to_broadcast([P, 4, width]),
                         rank[:, t, bass.ds(quad * 4, 4)].unsqueeze(2).to_broadcast([P, 4, width]), ALU.is_equal, signals=picked if t else None)

            def pick_gates(step, quad, width, gathered):
                for t in range(TT):
                    step(v.tensor_tensor, pick_gate[:, t, 0:4 * width].rearrange("p (e j) -> p e j", e=4), pick[:, t, 0:4 * width].rearrange("p (e j) -> p e j", e=4),
                         gates[:, t, bass.ds(quad * 4, 4)].unsqueeze(2).to_broadcast([P, 4, width]), ALU.mult, signals=gathered if t else None)

            def first_tokens(step, name, width, picked, gathered):
                picks(step, 0, width, (picked, 1))
                for c in range(KC):
                    take(job(name, c), v.tensor_copy, x_e[:, c, 0:4 * width], bank(job(name, c))[:, 0:4 * width])
                pick_gates(step, 0, width, (gathered, 1))

            def next_tokens(step, R, xe, gw, quad, width, gathered):
                for j in range(4):
                    dve.wait_ge(*R.done(xe + j))
                    step(v.tensor_copy, x_e[:, 2 * j:2 * j + 2, 0:4 * width], R.bank(xe + j)[:, 0:8 * width].rearrange("p (c t) -> p c t", c=2), signals=R.emptied(xe + j))
                for t in range(TT):
                    dve.wait_ge(*R.done(gw + t))
                pick_gates(step, quad, width, (gathered, R.it + 2))

            def moe_products(step, R, quad, gathered):
                for p in range(2):
                    dve.wait_ge(*R.emptied(MOE_GATE[p]))
                    dve.wait_ge(*R.done(MOE_UP[p]))
                    step(v.tensor_tensor, hid[:, p, :], R.bank(MOE_UP[p]), silu_g[:, p, :], ALU.mult, signals=R.emptied(MOE_UP[p]))
                next_tokens(step, R, MOE_XE, MOE_GW, quad, CAP, gathered)
                for p in range(2):
                    for n in range(2):
                        j, cols = MOE_DOWN[p] + n, wide(n * BANK, BANK)
                        dve.wait_ge(*R.done(j))
                        step(v.tensor_tensor, y_e[:, p, cols], R.bank(j), mod[:, 2, cols], ALU.mult, signals=R.emptied(j))
                for p in range(2):
                    for n in range(2):
                        for t in range(TT):
                            j, cols = MOE_SUM[p] + 2 * n + t, wide(n * BANK, BANK)
                            dve.wait_ge(*R.done(j))
                            step(v.tensor_tensor, y_sum[:, t, cols], R.bank(j), y_sum[:, t, cols], ALU.add, signals=R.emptied(j))

            first_tokens(step, "moe_first", CAP, signal("moe_picked"), signal("moe_gathered"))
            dve.wait_ge(signal("mix_gain_in"), 16)
            for n in range(2):
                dve.wait_ge(*emptied(job("mod7", n)))
            step(v.tensor_tensor, mod[:, 1, :], mod[:, 1, :], mix_gain, ALU.mult)
            with dve.Fori(0, MOE_ROUNDS) as it:
                step.begin_loop(it, 2)
                quad = (it + 1) & (QUADS - 1)
                picks(step, quad, CAP, (signal("moe_picked"), it + 2))
                moe_products(step, Rounds(it, job("moe"), MOE_JOBS), quad, signal("moe_gathered"))
                step.end_loop(MOE_ROUNDS)
            moe_over = [emptied(job("moe", (MOE_ROUNDS - 1) * MOE_JOBS + MOE_SUM[0] + j)) for j in range(BANKS)]
            for taken in moe_over:
                dve.wait_ge(*taken)
            with more_tokens(dve):
                more = Turn(dve, sem("more_dve_step"))
                more(v.memset, pass_shift[:], 0.0)
                more(v.memset, pass_shift[:, QUADS - 1:QUADS], float(CAP))
                more(v.tensor_scalar, rank[:], rank[:], float(CAP), None, ALU.subtract)
                picks(more, 0, CAP, (signal("more_picked"), 1))
                for c in range(KC):
                    dve.wait_ge(more_sems["pe_done"], c + 1)
                    more(v.tensor_copy, x_e[:, c, :], bank(c)[:, 0:4 * CAP], signals=(more_sems["evacuated"][c], 1))
                pick_gates(more, 0, CAP, (signal("more_gathered"), 1))
                with dve.Fori(0, MORE_ROUNDS) as it:
                    more.begin_loop(it, 3)
                    quad = (it + 1) & (QUADS - 1)
                    more(v.tensor_tensor, rank[:], rank[:], pass_shift[:, bass.ds(it & (QUADS - 1), 1)].unsqueeze(2).to_broadcast([P, TT, E]), ALU.subtract)
                    picks(more, quad, CAP, (signal("more_picked"), it + 2))
                    moe_products(more, Rounds(it, KC, MOE_JOBS, **more_sems), quad, signal("more_gathered"))
                    more.end_loop(MORE_ROUNDS)
                for j in range(BANKS):
                    dve.wait_ge(more_sems["evacuated"][j], 1 + MORE_ROUNDS * MOE_JOBS // BANKS)

            dve.wait_ge(signal("params_in"), 64)
            for t in range(TT):
                norm_stats(6 + t, t, y_sum)
                normalize(x, 6 + t, t, params[:, 0, :], params[:, 1, :], (signal("x_b1_ready"), t + 1), y_sum)

            def rms_modulated(n, ready):
                for t in range(TT):
                    step(v.tensor_tensor, h[:, t, :], x[:, t, :], mod[:, 1, :], ALU.mult)
                    dve.wait_ge(signal("rms2_ready"), n + t + 1)
                    step(v.scalar_tensor_tensor, h[:, t, :], h[:, t, :], mv[:, t, 0:1], mod[:, 0, :], ALU.mult, ALU.add, signals=(signal(ready), t + 1))

            for n in range(2):
                dve.wait_ge(*emptied(job("mod6", n)))
            rms_modulated(0, "h3_ready")

            def rotate(dst, src, t, heads, taken=None):
                half = ROPE // 2
                n = heads * half
                sin, cos = (turn[:, i, t, :].unsqueeze(1).to_broadcast([P, heads, half]) for i in (2, 3))
                one, two = (rope_tmp[:, i, 0:n].rearrange("p (h d) -> p h d", h=heads) for i in (0, 1))
                s1, s2, d1, d2 = src[:, :, 0:half], src[:, :, half:ROPE], dst[:, :, 0:half], dst[:, :, half:ROPE]
                step(v.tensor_tensor, one, s1, cos, ALU.mult)
                step(v.tensor_tensor, two, s2, sin, ALU.mult)
                step(v.tensor_tensor, d1, one, two, ALU.subtract)
                step(v.tensor_tensor, one, s1, sin, ALU.mult)
                step(v.tensor_tensor, two, s2, cos, ALU.mult, signals=taken)
                return d2, one, two

            for i in range(4):
                dve.wait_ge(*emptied(job("lat", i)))
            dve.wait_ge(signal("sin_ready"), 1)
            for t in range(TT):
                d2, one, two = rotate(k_pe[:, t, 0:ROPE].unsqueeze(1), lat[:, t, LAT - ROPE:LAT].unsqueeze(1), t, 1)
                step(v.tensor_tensor, d2, one, two, ALU.add)
                step(v.tensor_copy, k_pe[:, t, ROPE:2 * ROPE], k_pe[:, t, 0:ROPE])
                dve.wait_ge(signal("rms2_ready"), 3 + t)
                step(v.tensor_scalar, lat[:, t, 0:Q_RANK], lat[:, t, 0:Q_RANK], mv[:, t, 0:1], None, ALU.mult)
                step(v.tensor_scalar, lat[:, t, wide(Q_RANK, KV_RANK)], lat[:, t, wide(Q_RANK, KV_RANK)], mv2[:, t, 0:1], None, ALU.mult,
                     signals=(signal("lat_ready"), 1) if t else None)
            for t in range(TT):
                k = job("latT", 2 * t)
                take(k, v.tensor_tensor, c_qT[:, :, wide(t * P, P)], bank(k)[:, 0:3 * P].rearrange("p (c t) -> p c t", c=3),
                     vecT[:, 80:83].unsqueeze(2).to_broadcast([P, 3, P]), ALU.mult)
                k = job("latT", 2 * t + 1)
                dve.wait_ge(*done(k))
                step(v.tensor_copy, k_peT[:, wide(t * P, P)], bank(k)[:, 2 * P:3 * P])
                step(v.tensor_tensor, c_kvT[:, :, wide(t * P, P)], bank(k)[:, 0:2 * P].rearrange("p (c t) -> p c t", c=2),
                     vecT[:, 83:85].unsqueeze(2).to_broadcast([P, 2, P]), ALU.mult, signals=emptied(k))
            for t in range(TT):
                k = job("q_pe", t)
                dve.wait_ge(*done(k))
                by_head = q_pe[:, t, :].rearrange("p (h d) -> p h d", h=MLA_HEADS)
                d2, one, two = rotate(by_head, bank(k).rearrange("p (h d) -> p h d", h=MLA_HEADS), t, MLA_HEADS, emptied(k))
                dve.wait_ge(dve_step, step.n)
                step(v.tensor_tensor, d2, one, two, ALU.add, signals=(signal("q_pe_ready"), t + 1))

            def mla_scaled(i, dst, src, taken):
                step(v.tensor_scalar, dst, src, (NOPE + ROPE) ** -0.5, None, ALU.mult, signals=taken)

            attention("mla", MLA_UNITS, mla_unit0, mla_scaled, lambda i: TT, lambda i: o_mla[:, i % TT, wide(i // TT * P, P)])

            def by_head(ap):
                return ap.rearrange("p (h d) -> p h d", h=DIL_HEADS)

            def weight(i, t):
                return dil_w[:, i, t:DIL_UNITS:TT].unsqueeze(2).to_broadcast([P, DIL_HEADS, DIL_D])

            def merge_groups(n):
                first, of_first = (row_max[:, stat[0]], row_sum[:, stat[0]]) if n == 1 else (dil_w[:, 2, :], dil_sum[:])
                if n == 2:
                    step(v.tensor_copy, first, dil_top[:])
                step(v.tensor_tensor, dil_top[:], first, row_max[:, stat[n]], ALU.min)
                step(v.tensor_tensor, dil_w[:, 0, :], dil_top[:], first, ALU.subtract)
                step(v.tensor_tensor, dil_w[:, 1, :], dil_top[:], row_max[:, stat[n]], ALU.subtract, signals=(signal("dil_shift_ready"), n))
                dve.wait_ge(signal("dil_exp_ready"), n)
                if n == 1:
                    step(v.tensor_tensor, dil_w[:, 0, :], dil_w[:, 0, :], of_first, ALU.mult)
                    step(v.tensor_tensor, dil_w[:, 1, :], dil_w[:, 1, :], row_sum[:, stat[n]], ALU.mult)
                    step(v.tensor_tensor, dil_sum[:], dil_w[:, 0, :], dil_w[:, 1, :], ALU.add)
                    for t in range(TT):
                        for g in (0, 1):
                            step(v.tensor_tensor, by_head(o_dil[g][:, t, :]), by_head(o_dil[g][:, t, :]), weight(g, t), ALU.mult)
                        step(v.tensor_tensor, o_dil[0][:, t, :], o_dil[0][:, t, :], o_dil[1][:, t, :], ALU.add)
                else:
                    step(v.tensor_tensor, dil_sum[:], dil_sum[:], dil_w[:, 0, :], ALU.mult)
                    step(v.tensor_tensor, dil_w[:, 1, :], dil_w[:, 1, :], row_sum[:, stat[n]], ALU.mult)
                    step(v.tensor_tensor, dil_sum[:], dil_sum[:], dil_w[:, 1, :], ALU.add)
                    step(v.reciprocal, dil_sum[:], dil_sum[:])
                    for i in range(2):
                        step(v.tensor_tensor, dil_w[:, i, :], dil_w[:, i, :], dil_sum[:], ALU.mult)

            stat = [wide(dil_unit0 + g * DIL_UNITS, DIL_UNITS) for g in range(DIL_GROUPS)]
            for g in range(DIL_GROUPS):
                unit0 = dil_unit0 + g * DIL_UNITS

                def dil_biased(i, dst, src, taken):
                    hd, t = divmod(i, TT)
                    n = g * DIL_HEADS + hd
                    if t == 0:
                        dve.wait_ge(signal("bias_masked"), n + 1)
                    step(v.scalar_tensor_tensor, dst, src, DIL_D ** -0.5, bias_tile[:, n % 4, wide(t * S, S)], ALU.mult, ALU.add, signals=taken)

                attention(f"dil{g}_", DIL_UNITS, unit0, dil_biased, lambda i: TT, lambda i: o_dil[g][:, i % TT, wide(i // TT * P, P)])
                if g == 1:
                    merge_groups(1)
            merge_groups(2)
            for t in range(TT):
                for g in (0, 2):
                    step(v.tensor_tensor, by_head(o_dil[g][:, t, :]), by_head(o_dil[g][:, t, :]), weight(g // 2, t), ALU.mult)
                step(v.tensor_tensor, o_dil[0][:, t, :], o_dil[0][:, t, :], o_dil[2][:, t, :], ALU.add)
                dve.wait_ge(signal("gate_b_ready"), t + 1)
                step(v.tensor_tensor, o_dil[0][:, t, :], o_dil[0][:, t, :], sig_b[:, t, :], ALU.mult)
                dve.wait_ge(signal("mla_gated"), t + 1)
                step(v.tensor_tensor, h[:, t, :], o_mla[:, t, :], o_dil[0][:, t, :], ALU.add, signals=(signal("mix_ready"), t + 1))
            dve.wait_ge(signal("params_in"), 96)
            for unit in ("mod8", "mod9", "mod10"):
                for n in range(2):
                    dve.wait_ge(*emptied(job(unit, n)))
            step(v.tensor_tensor, mod[:, 1, :], mod[:, 1, :], params[:, 0, :], ALU.mult)
            for j in range(4):
                n, t = divmod(j, 2)
                cols, k = wide(n * BANK, BANK), job("w_out", j)
                take(k, v.tensor_tensor, junk[:, 0:BANK], bank(k), mod[:, 2, cols], ALU.mult)
                step(v.tensor_tensor, x[:, t, cols], x[:, t, cols], junk[:, 0:BANK], ALU.add, signals=(signal("x2_ready"), t + 1) if n else None)
            rms_modulated(4, "h4_ready")

            k = job("router2")
            dve.wait_ge(*done(k))
            step(v.tensor_copy, gates[:], bank(k)[:, 0:TT * E].rearrange("p (t e) -> p t e", t=TT), signals=emptied(k))
            step(v.tensor_reduce, top1[:], gates[:], AX, ALU.max)
            step(v.tensor_tensor, gates[:], gates[:], top1[:].unsqueeze(2).to_broadcast([P, TT, E]), ALU.subtract, signals=(signal("aff_logits_ready"), 1))
            dve.wait_ge(signal("aff_exp_ready"), 1)
            step(v.tensor_reduce, top1[:], gates[:], AX, ALU.add)
            step(v.reciprocal, top1[:], top1[:])
            step(v.tensor_tensor, gates[:], gates[:], top1[:].unsqueeze(2).to_broadcast([P, TT, E]), ALU.mult, signals=(signal("aff_ready"), 1))
            k = job("affT")
            take(k, v.tensor_copy, affT[:], bank(k)[0:E, 0:S])
            for i in range(CAP2 // 8):
                src, dst = (affT, topped) if i % 2 == 0 else (topped, affT)
                step(v.max, best8[:], src[:])
                step(v.match_replace, dst[:], best8[:], src[:], -1.0)
            step(v.tensor_scalar, affT[:], affT[:], 0.0, None, ALU.is_lt)
            step(v.memset, topped[:], 1.0)
            step(v.tensor_tensor_scan, rank_T[:], topped[:], affT[:], 0.0, ALU.mult, ALU.add)
            step(v.tensor_tensor, rank_T[:], rank_T[:], affT[:], ALU.mult, signals=(signal("rank_T_ready"), 1))
            k = job("rank2")
            take(k, v.tensor_copy, rank[:], bank(k)[:, 0:TT * E].rearrange("p (t e) -> p t e", t=TT))

            for t in range(TT):
                step(v.tensor_copy, y_sum[:, t, :], x[:, t, :])
            for n in range(2):
                dve.wait_ge(*emptied(job("mod11", n)))
            first_tokens(step, "ec_first", CAP2, signal("ec_picked"), signal("ec_gathered"))
            with dve.Fori(0, EC_ROUNDS) as it:
                R = Rounds(it, job("ec"), EC_JOBS)
                step.begin_loop(it, 2)
                quad = (it + 1) & (QUADS - 1)
                picks(step, quad, CAP2, (signal("ec_picked"), it + 2))
                for fp in range(2):
                    for b in range(2):
                        dve.wait_ge(*R.emptied(EC_GATE[fp] + b))
                        dve.wait_ge(*R.done(EC_UP[fp] + b))
                        if fp:
                            dve.wait_ge(*R.done(EC_T[0] + b))
                        step(v.tensor_tensor, hid[:, b, :], R.bank(EC_UP[fp] + b), silu_g[:, b, :], ALU.mult, signals=R.emptied(EC_UP[fp] + b))
                next_tokens(step, R, EC_XE, EC_GW, quad, CAP2, signal("ec_gathered"))
                for n in range(2):
                    j, cols = EC_DOWN + n, wide(n * BANK, BANK)
                    dve.wait_ge(*R.done(j))
                    step(v.tensor_tensor, y_e[:, 0, cols], R.bank(j), mod[:, 2, cols], ALU.mult, signals=R.emptied(j))
                for n in range(2):
                    for t in range(TT):
                        j, cols = EC_SUM + 2 * n + t, wide(n * BANK, BANK)
                        dve.wait_ge(*R.done(j))
                        step(v.tensor_tensor, y_sum[:, t, cols], R.bank(j), y_sum[:, t, cols], ALU.add, signals=R.emptied(j))
                step.end_loop(EC_ROUNDS)
                step.last = None
            for j in range(4):
                dve.wait_ge(evacuated[(job("ec") + EC_SUM + j) % BANKS], (job("ec") + (EC_ROUNDS - 1) * EC_JOBS + EC_SUM + j) // BANKS + 1)
            for t in range(TT):
                dve.wait_ge(signal("rms2_ready"), 7 + t)
                step(v.scalar_tensor_tensor, h[:, t, :], y_sum[:, t, :], mv[:, t, 0:1], params[:, 1, :], ALU.mult, ALU.mult, signals=(signal("out_ready"), t + 1))


def constants():
    import numpy as np

    f = np.float32
    i = np.arange(128)
    ident = np.eye(128, dtype=f)
    tri = (i[:, None] <= i[None, :]).astype(f)
    mask = np.where(i[None, :] > i[:, None], f(-1e30), f(0)).astype(f)
    causal = np.concatenate([np.zeros((128, 128), f), mask], 1)
    seg_mask = np.ascontiguousarray(mask.T)
    ones = np.ones((128, 128), f)
    iota1 = np.broadcast_to(np.arange(1, 65, dtype=f), (128, 64))
    desc = np.broadcast_to(np.arange(16, 0, -1, dtype=f), (128, 16))
    freq = (f(10000.0) ** (-np.arange(0, 64, 2, dtype=f) / f(64))).astype(f)
    inv_freq = np.broadcast_to(freq, (128, 32))
    low = [0, 1, 2, 3, 4, 5, 6, 7] + [int(np.ceil(8 * 128 ** (j / 8) - 1e-9)) for j in range(8)]
    high = [n - 1 for n in low[1:]] + [low[-1] + (1 << 23)]
    table = [(-b, -a) for a, b in zip(low, high)] + [(max(a, 1), b) for a, b in zip(low, high)]
    buckets = np.tile(np.array([((a + b) / 2, (b - a) / 2) for a, b in table], f), (4, 1))
    eps = np.broadcast_to(np.array([1e-5, 1e-6], f), (128, 2))
    col = np.arange(32)
    select = ((i[:, None] // 64 == col // 16) & (i[:, None] % 32 == col % 16)).astype(f)
    return np.ascontiguousarray(np.concatenate([ident, tri, causal, seg_mask, ones, iota1, desc, inv_freq, buckets, eps, select], 1))


def band_masks():
    import numpy as np

    t, s = np.arange(256)[:, None], np.arange(256)[None, :]
    groups = [np.where(((t - s) % d == 0) & (abs(t - s) <= 64 * d), 0.0, -1e30) for d in (1, 4, 16)]
    return np.ascontiguousarray(np.stack(groups).astype(np.float32).reshape(3, 2, 128, 256).transpose(2, 0, 1, 3))


def kernel(**inputs):
    import concourse.bacc as bacc
    import numpy as np
    from concourse import mybir
    from concourse.bass_utils import run_bass_kernel_spmd

    nc = bacc.Bacc("TRN2", target_bir_lowering=False, num_devices=1)
    given = dict(inputs, consts=constants(), bands=band_masks())
    arrays, tensors = {}, {}
    for name, value in given.items():
        value = np.ascontiguousarray(value)
        arrays[f"in_{name}"] = value
        tensors[name] = nc.dram_tensor(f"in_{name}", value.shape, mybir.dt.from_np(value.dtype), kind="ExternalInput").ap()
    out = nc.dram_tensor("out", inputs["x"].shape, mybir.dt.float32, kind="ExternalOutput").ap()
    build_program(nc, tensors, out)
    done = run_bass_kernel_spmd(nc, [arrays], core_ids=[0])
    return done.results[0]["out"]
```
